# Optimizing a Trainium2 kernel written in Bass

```python
import jax, jax.numpy as jnp
from jax import lax
import numpy as np
import math
import jax
import jax.numpy as jnp

D_MODEL = 1024
BATCH = 1
SEQ = 256
DEPTH = 2

D_MIX = D_MODEL
C_CONV = D_MIX // 4
NSA_HEADS = 4
HEAD_DIM = 64
C_NSA = NSA_HEADS * HEAD_DIM
C_SGU = D_MIX // 4
C_POOL = D_MIX // 4
CONV_K = 31
CMP_LEN = 32
CMP_STRIDE = 16
SEL_LEN = 64
SEL_TOPK = 16
WINDOW = 512
Q_BLOCK = 128
SGU_CHUNK = 128
SGU_GROUPS = 4
POOL_WINDOWS = (2, 4, 8, 16)
FFN_DIM = 2816
FFN_CONV_K = 3
ROPE_THETA = 10000.0
RMS_EPS = 1e-6
LN_EPS = 1e-5
NEG_INF = -1e30
FORCE_SCORE = 1e6
N_IN = 2 * C_CONV + C_NSA + 6 * HEAD_DIM + 3 * NSA_HEADS + 2 * C_SGU + C_POOL


def rms_norm(x, g):
    xf = x.astype(jnp.float32)
    y = xf * lax.rsqrt(jnp.mean(xf * xf, axis=-1, keepdims=True) + RMS_EPS)
    return y.astype(x.dtype) * g

def layer_norm(x, g, b):
    xf = x.astype(jnp.float32)
    mu = jnp.mean(xf, axis=-1, keepdims=True)
    var = jnp.mean(jnp.square(xf - mu), axis=-1, keepdims=True)
    return ((xf - mu) * lax.rsqrt(var + LN_EPS)).astype(x.dtype) * g + b

def causal_dwconv(x, w, b):
    k, c = w.shape
    y = lax.conv_general_dilated(x, w[:, None, :].astype(x.dtype), window_strides=(1,),
                                 padding=[(k - 1, 0)], dimension_numbers=('NWC', 'WIO', 'NWC'),
                                 feature_group_count=c)
    return y + b

def rope_tables(seq):
    half = HEAD_DIM // 2
    inv = ROPE_THETA ** (-jnp.arange(half, dtype=jnp.float32) * 2.0 / HEAD_DIM)
    ang = jnp.arange(seq, dtype=jnp.float32)[:, None] * inv[None, :]
    return jnp.cos(ang), jnp.sin(ang)

def apply_rope(x, cos, sin):
    half = HEAD_DIM // 2
    shp = (cos.shape[0],) + (1,) * (x.ndim - 3) + (half,)
    c = cos.reshape(shp).astype(x.dtype)
    s = sin.reshape(shp).astype(x.dtype)
    x1, x2 = x[..., :half], x[..., half:]
    return jnp.concatenate([x1 * c - x2 * s, x2 * c + x1 * s], axis=-1)

def masked_softmax(s, mask):
    p = jax.nn.softmax(jnp.where(mask, s, NEG_INF), axis=-1)
    return jnp.where(mask, p, 0.0)

def conformer_conv(z, w, b, ln_g, ln_b):
    a, gate = jnp.split(z, 2, axis=-1)
    y = causal_dwconv(a * jax.nn.sigmoid(gate), w, b)
    return jax.nn.silu(layer_norm(y, ln_g, ln_b))

def nsa_attention(q, k_cmp, v_cmp, k_slc, v_slc, k_win, v_win, gates,
                  pe_k, pe_v, ck_w1, ck_w2, cv_w1, cv_w2, cos, sin):
    bsz, seq = q.shape[0], q.shape[1]
    scale = HEAD_DIM ** -0.5
    n_cmp = (seq - CMP_LEN) // CMP_STRIDE + 1
    n_sel = seq // SEL_LEN
    top_n = min(SEL_TOPK, n_sel)
    ratio = SEL_LEN // CMP_STRIDE
    n_ov = CMP_LEN // CMP_STRIDE
    front = n_ov - 1
    right = ratio * n_sel + ratio - front - n_cmp

    blk_idx = jnp.arange(n_cmp)[:, None] * CMP_STRIDE + jnp.arange(CMP_LEN)[None, :]

    def compress(t, pe, w1, w2):
        blocks = (t[:, blk_idx] + pe).reshape(bsz, n_cmp, CMP_LEN * HEAD_DIM)
        return jax.nn.gelu(blocks @ w1) @ w2

    kc = compress(k_cmp, pe_k, ck_w1, ck_w2)
    vc = compress(v_cmp, pe_v, cv_w1, cv_w2)
    cmp_end = jnp.arange(n_cmp) * CMP_STRIDE + CMP_LEN - 1

    q_cmp = q * scale
    q_rot = apply_rope(q, cos, sin) * scale
    ks_blocks = apply_rope(k_slc, cos, sin).reshape(bsz, n_sel, SEL_LEN, HEAD_DIM)
    vs_blocks = v_slc.reshape(bsz, n_sel, SEL_LEN, HEAD_DIM)
    kw_pad = jnp.pad(apply_rope(k_win, cos, sin), ((0, 0), (WINDOW, 0), (0, 0)))
    vw_pad = jnp.pad(v_win, ((0, 0), (WINDOW, 0), (0, 0)))
    sel_j = jnp.arange(n_sel)
    gather = jax.vmap(lambda blocks, idx: blocks[idx])

    def query_block(i):
        t0 = i * Q_BLOCK
        pos = t0 + jnp.arange(Q_BLOCK)
        qc = lax.dynamic_slice_in_dim(q_cmp, t0, Q_BLOCK, axis=1)
        qr = lax.dynamic_slice_in_dim(q_rot, t0, Q_BLOCK, axis=1)
        g = lax.dynamic_slice_in_dim(gates, t0, Q_BLOCK, axis=1)

        s = jnp.einsum('bthd,bnd->bhtn', qc, kc, preferred_element_type=jnp.float32)
        p_cmp = masked_softmax(s, cmp_end[None, :] <= pos[:, None])
        o_cmp = jnp.einsum('bhtn,bnd->bthd', p_cmp.astype(vc.dtype), vc)

        pp = jnp.pad(p_cmp.sum(axis=1), ((0, 0), (0, 0), (front, right)))
        imp = jnp.zeros((bsz, Q_BLOCK, n_sel), jnp.float32)
        for m in range(ratio):
            for n in range(n_ov):
                imp = imp + pp[..., m - n + front::ratio][..., :n_sel]
        cur = (pos // SEL_LEN)[:, None]
        forced = (sel_j[None, :] == 0) | (sel_j[None, :] == cur) | (sel_j[None, :] == cur - 1)
        valid = sel_j[None, :] * SEL_LEN <= pos[:, None]
        imp = jnp.where(valid, jnp.where(forced, FORCE_SCORE, imp), NEG_INF)
        top_val, top_idx = lax.top_k(imp, top_n)

        ksel = gather(ks_blocks, top_idx).reshape(bsz, Q_BLOCK, top_n * SEL_LEN, HEAD_DIM)
        vsel = gather(vs_blocks, top_idx).reshape(bsz, Q_BLOCK, top_n * SEL_LEN, HEAD_DIM)
        tok = (top_idx[..., None] * SEL_LEN + jnp.arange(SEL_LEN)).reshape(bsz, Q_BLOCK, top_n * SEL_LEN)
        sel_ok = jnp.repeat(top_val > 0.5 * NEG_INF, SEL_LEN, axis=-1)
        mask_sel = sel_ok & (tok <= pos[None, :, None])
        s = jnp.einsum('bthd,btkd->bhtk', qr, ksel, preferred_element_type=jnp.float32)
        p = masked_softmax(s, mask_sel[:, None])
        o_slc = jnp.einsum('bhtk,btkd->bthd', p.astype(vsel.dtype), vsel)

        kw = lax.dynamic_slice_in_dim(kw_pad, t0, Q_BLOCK + WINDOW, axis=1)
        vw = lax.dynamic_slice_in_dim(vw_pad, t0, Q_BLOCK + WINDOW, axis=1)
        kpos = t0 - WINDOW + jnp.arange(Q_BLOCK + WINDOW)
        mask_win = ((kpos[None, :] >= 0) & (kpos[None, :] <= pos[:, None])
                    & (kpos[None, :] > pos[:, None] - WINDOW))
        s = jnp.einsum('bthd,bkd->bhtk', qr, kw, preferred_element_type=jnp.float32)
        p = masked_softmax(s, mask_win)
        o_win = jnp.einsum('bhtk,bkd->bthd', p.astype(vw.dtype), vw)

        return g[..., 0:1] * o_cmp + g[..., 1:2] * o_slc + g[..., 2:3] * o_win

    out = lax.map(query_block, jnp.arange(seq // Q_BLOCK))
    return out.transpose(1, 0, 2, 3, 4).reshape(bsz, seq, C_NSA)

def spatial_gating(z, ln_g, ln_b, w_s, b_s):
    z = jax.nn.gelu(z)
    u, v = jnp.split(z, 2, axis=-1)
    v = layer_norm(v, ln_g, ln_b)
    bsz, seq, c = v.shape
    vr = v.reshape(bsz, seq // SGU_CHUNK, SGU_CHUNK, SGU_GROUPS, c // SGU_GROUPS)
    causal = jnp.tril(jnp.ones((SGU_CHUNK, SGU_CHUNK), dtype=bool))
    ws = jnp.where(causal, w_s, 0.0).astype(v.dtype)
    f = jnp.einsum('gts,bcsgd->bctgd', ws, vr) + b_s.T[:, :, None]
    return u * f.reshape(bsz, seq, c)

def multiscale_pool(z, w_p, scale):
    bsz, seq, c = z.shape
    cg = c // len(POOL_WINDOWS)
    zf = z.astype(jnp.float32)
    cs = jnp.pad(jnp.cumsum(zf, axis=1), ((0, 0), (1, 0), (0, 0)))
    t = jnp.arange(seq)
    outs = []
    for gi, w in enumerate(POOL_WINDOWS):
        c_g = cs[..., gi * cg:(gi + 1) * cg]
        lag = jnp.pad(c_g[:, :seq + 1 - w], ((0, 0), (w - 1, 0), (0, 0)))
        cnt = jnp.minimum(t + 1, w).astype(jnp.float32)[:, None]
        outs.append((c_g[:, 1:] - lag) / cnt - zf[..., gi * cg:(gi + 1) * cg])
    pooled = jnp.stack(outs, axis=2).astype(z.dtype)
    y = jnp.einsum('bsgc,gcd->bsgd', pooled, w_p).reshape(bsz, seq, c)
    return y * scale

def conv_ffn(h, w_up, cw, cb, w_down):
    gu = causal_dwconv(h @ w_up, cw, cb)
    g, u = jnp.split(gu, 2, axis=-1)
    return (jax.nn.gelu(g, approximate=True) * u) @ w_down

def first_inputs(seed: int = 0) -> dict:
    key = jax.random.key(seed)
    ks = jax.random.split(key, 32)
    L = DEPTH
    hd = HEAD_DIM

    def nrm(k, shape, s):
        return jax.random.normal(k, shape, jnp.float32) * s

    def gain(k, shape):
        return 1.0 + nrm(k, shape, 0.05)

    return {
        'x': nrm(ks[0], (BATCH, SEQ, D_MODEL), 1.0),
        'norm_mix_pre': gain(ks[1], (L, D_MODEL)),
        'norm_mix_post': gain(ks[2], (L, D_MODEL)),
        'norm_ffn_pre': gain(ks[3], (L, D_MODEL)),
        'norm_ffn_post': gain(ks[4], (L, D_MODEL)),
        'w_in': nrm(ks[5], (L, D_MODEL, N_IN), D_MODEL ** -0.5),
        'w_out': nrm(ks[6], (L, D_MIX, D_MODEL), D_MIX ** -0.5),
        'conv_dw_w': nrm(ks[7], (L, CONV_K, C_CONV), CONV_K ** -0.5),
        'conv_dw_b': nrm(ks[8], (L, C_CONV), 0.02),
        'conv_ln_g': gain(ks[9], (L, C_CONV)),
        'conv_ln_b': nrm(ks[10], (L, C_CONV), 0.02),
        'nsa_pe_k': nrm(ks[11], (L, CMP_LEN, hd), 0.1),
        'nsa_pe_v': nrm(ks[12], (L, CMP_LEN, hd), 0.1),
        'nsa_ck_w1': nrm(ks[13], (L, CMP_LEN * hd, hd), (CMP_LEN * hd) ** -0.5),
        'nsa_ck_w2': nrm(ks[14], (L, hd, hd), hd ** -0.5),
        'nsa_cv_w1': nrm(ks[15], (L, CMP_LEN * hd, hd), (CMP_LEN * hd) ** -0.5),
        'nsa_cv_w2': nrm(ks[16], (L, hd, hd), hd ** -0.5),
        'sgu_ln_g': gain(ks[17], (L, C_SGU)),
        'sgu_ln_b': nrm(ks[18], (L, C_SGU), 0.02),
        'sgu_w': nrm(ks[19], (L, SGU_GROUPS, SGU_CHUNK, SGU_CHUNK), SGU_CHUNK ** -0.5),
        'sgu_b': 1.0 + nrm(ks[20], (L, SGU_GROUPS, SGU_CHUNK), 0.1),
        'pool_w': nrm(ks[21], (L, len(POOL_WINDOWS), C_POOL // 4, C_POOL // 4), (C_POOL // 4) ** -0.5),
        'pool_scale': gain(ks[22], (L, C_POOL)),
        'ffn_up': nrm(ks[23], (L, D_MODEL, 2 * FFN_DIM), D_MODEL ** -0.5),
        'ffn_conv_w': nrm(ks[24], (L, FFN_CONV_K, 2 * FFN_DIM), FFN_CONV_K ** -0.5),
        'ffn_conv_b': nrm(ks[25], (L, 2 * FFN_DIM), 0.02),
        'ffn_down': nrm(ks[26], (L, FFN_DIM, D_MODEL), FFN_DIM ** -0.5),
    }

def first_block(x, norm_mix_pre, norm_mix_post, norm_ffn_pre, norm_ffn_post, w_in, w_out,
              conv_dw_w, conv_dw_b, conv_ln_g, conv_ln_b,
              nsa_pe_k, nsa_pe_v, nsa_ck_w1, nsa_ck_w2, nsa_cv_w1, nsa_cv_w2,
              sgu_ln_g, sgu_ln_b, sgu_w, sgu_b, pool_w, pool_scale,
              ffn_up, ffn_conv_w, ffn_conv_b, ffn_down):
    bsz, seq, _ = x.shape
    cos, sin = rope_tables(seq)
    sizes = (2 * C_CONV, C_NSA, 6 * HEAD_DIM, 3 * NSA_HEADS, 2 * C_SGU, C_POOL)
    offsets = [int(o) for o in np.cumsum(sizes)[:-1]]
    for l in range(DEPTH):
        h = rms_norm(x, norm_mix_pre[l])
        z = h @ w_in[l]
        za, zq, zkv, zg, zc, zd = jnp.split(z, offsets, axis=-1)
        y_conv = conformer_conv(za, conv_dw_w[l], conv_dw_b[l], conv_ln_g[l], conv_ln_b[l])
        q = zq.reshape(bsz, seq, NSA_HEADS, HEAD_DIM)
        kv = zkv.reshape(bsz, seq, 6, HEAD_DIM)
        gates = jax.nn.sigmoid(zg).reshape(bsz, seq, NSA_HEADS, 3)
        y_nsa = nsa_attention(q, kv[:, :, 0], kv[:, :, 1], kv[:, :, 2], kv[:, :, 3], kv[:, :, 4], kv[:, :, 5],
                              gates, nsa_pe_k[l], nsa_pe_v[l], nsa_ck_w1[l], nsa_ck_w2[l],
                              nsa_cv_w1[l], nsa_cv_w2[l], cos, sin)
        y_sgu = spatial_gating(zc, sgu_ln_g[l], sgu_ln_b[l], sgu_w[l], sgu_b[l])
        y_pool = multiscale_pool(zd, pool_w[l], pool_scale[l])
        y = jnp.concatenate([y_conv, y_nsa, y_sgu, y_pool], axis=-1) @ w_out[l]
        x = x + rms_norm(y, norm_mix_post[l])
        h = rms_norm(x, norm_ffn_pre[l])
        y = conv_ffn(h, ffn_up[l], ffn_conv_w[l], ffn_conv_b[l], ffn_down[l])
        x = x + rms_norm(y, norm_ffn_post[l])
    return x


DEPTH_2 = 1

GRID_W = 64
CTX_LEN = 256
MIX_WIDTH = D_MODEL
FOURIER_HEAD_DIM = 64
FOURIER_WIDTH = MIX_WIDTH // 4
FOURIER_HEADS = FOURIER_WIDTH // FOURIER_HEAD_DIM
SSD_WIDTH = MIX_WIDTH - FOURIER_WIDTH
SSD_HEAD_DIM = 64
SSD_HEADS = SSD_WIDTH // SSD_HEAD_DIM
SSD_GROUPS = 4
SSD_STATE = 128
GROUP_STATE = SSD_GROUPS * SSD_STATE
CONV_WIDTH = 3
CHUNK = 128
D_FF = 2816
N_MOD = 9
MACARON_WEIGHT = 0.5
EPS = 1e-6
CONV_DIM = GROUP_STATE + SSD_WIDTH + GROUP_STATE
PROJ_WIDTH = FOURIER_WIDTH + SSD_WIDTH + CONV_DIM + 2 * SSD_HEADS


def rms_norm_2(x, g):
    x32 = x.astype(jnp.float32)
    y = x32 * lax.rsqrt(jnp.mean(x32 * x32, axis=-1, keepdims=True) + EPS)
    return (y * g.astype(jnp.float32)).astype(x.dtype)

def modulate(h, shift, scale):
    return h * (1 + scale[:, None, :]) + shift[:, None, :]

def macaron_ffn(x, mod3, norm_pre, norm_post, w_gate, w_up, w_down):
    h = modulate(rms_norm_2(x, norm_pre), mod3[:, 0], mod3[:, 1])
    y = (jax.nn.silu(h @ w_gate) * (h @ w_up)) @ w_down
    return x + MACARON_WEIGHT * mod3[:, 2][:, None, :] * rms_norm_2(y, norm_post)

def centred_dwconv_silu(u, w, b):
    out = lax.conv_general_dilated(u, w[:, None, :], (1,), 'SAME',
                                   dimension_numbers=('NWC', 'WIO', 'NWC'),
                                   feature_group_count=u.shape[-1])
    return jax.nn.silu(out + b)

def softplus_dt(dt_raw, dt_bias):
    b, L = dt_raw.shape[:2]
    return jax.nn.softplus(dt_raw.astype(jnp.float32).reshape(b, L, 2, SSD_HEADS)
                           + dt_bias.astype(jnp.float32))

def flip(t):
    return jnp.flip(t, axis=1)

def fourier_mix(u, fourier_w):
    b, L, _ = u.shape
    uh = u.reshape(b, L, FOURIER_HEADS, FOURIER_HEAD_DIM).astype(jnp.float32)
    f = jnp.fft.fft2(uh, axes=(1, 3), norm='ortho').real.astype(u.dtype)
    return jnp.einsum('blhd,hde->blhe', f, fourier_w).reshape(b, L, FOURIER_WIDTH)

def ssd_chunked(xs, dt, a, bm, cm, h0):
    b, L = xs.shape[:2]
    nc = L // CHUNK
    R = SSD_HEADS // SSD_GROUPS
    xdt = (xs * dt[..., None]).reshape(b, nc, CHUNK, SSD_GROUPS, R, SSD_HEAD_DIM)
    a_cs = jnp.cumsum(jnp.transpose((dt * a).reshape(b, nc, CHUNK, SSD_GROUPS, R), (0, 1, 3, 4, 2)), axis=-1)
    bc = bm.reshape(b, nc, CHUNK, SSD_GROUPS, SSD_STATE)
    cc = cm.reshape(b, nc, CHUNK, SSD_GROUPS, SSD_STATE)
    lower = jnp.tril(jnp.ones((CHUNK, CHUNK), dtype=bool))
    seg = jnp.exp(jnp.where(lower, a_cs[..., :, None] - a_cs[..., None, :], -jnp.inf))
    cb = jnp.einsum('bclgn,bcsgn->bcgls', cc, bc)
    y_diag = jnp.einsum('bcgls,bcgrls,bcsgrp->bclgrp', cb, seg, xdt)
    states = jnp.einsum('bcsgn,bcgrs,bcsgrp->bcgrpn', bc, jnp.exp(a_cs[..., -1:] - a_cs), xdt)

    def step(h, inp):
        s, d = inp
        return h * d[..., None, None] + s, h

    h_last, h_prev = lax.scan(step, h0.reshape(b, SSD_GROUPS, R, SSD_HEAD_DIM, SSD_STATE),
                              (jnp.moveaxis(states, 1, 0), jnp.moveaxis(jnp.exp(a_cs[..., -1]), 1, 0)))
    y_off = jnp.einsum('bclgn,cbgrpn,bcgrl->bclgrp', cc, h_prev, jnp.exp(a_cs))
    y = (y_diag + y_off).reshape(b, L, SSD_HEADS, SSD_HEAD_DIM)
    return y, h_last.reshape(b, SSD_HEADS, SSD_HEAD_DIM, SSD_STATE)

def ssd_final_state(xs, dt, a, bm):
    b, L = xs.shape[:2]
    R = SSD_HEADS // SSD_GROUPS
    cs = jnp.cumsum(dt * a, axis=1)
    xdt = (xs * (dt * jnp.exp(cs[:, -1:] - cs))[..., None]).reshape(b, L, SSD_GROUPS, R, SSD_HEAD_DIM)
    return jnp.einsum('blgn,blgrp->bgrpn', bm, xdt).reshape(b, SSD_HEADS, SSD_HEAD_DIM, SSD_STATE)

def mix_sublayer(x, mod3, h0_f, h0_b, norm_pre, norm_post, w_in, fourier_w, conv_w, conv_b,
                 dt_bias, a_log, d_skip, ssd_norm, w_out):
    b, L, _ = x.shape
    h = modulate(rms_norm_2(x, norm_pre), mod3[:, 0], mod3[:, 1])
    u_f, z, xbc, dt_raw = jnp.split(h @ w_in, [FOURIER_WIDTH, FOURIER_WIDTH + SSD_WIDTH,
                                               FOURIER_WIDTH + SSD_WIDTH + CONV_DIM], axis=-1)
    xbc = centred_dwconv_silu(xbc, conv_w, conv_b)
    cm, xs, bm = jnp.split(xbc, [GROUP_STATE, GROUP_STATE + SSD_WIDTH], axis=-1)
    xs = xs.reshape(b, L, SSD_HEADS, SSD_HEAD_DIM)
    bm = bm.reshape(b, L, SSD_GROUPS, SSD_STATE)
    cm = cm.reshape(b, L, SSD_GROUPS, SSD_STATE)
    dt = softplus_dt(dt_raw, dt_bias)
    a = -jnp.exp(a_log.astype(jnp.float32))
    y_f, h_f = ssd_chunked(xs, dt[:, :, 0], a[0], bm, cm, h0_f)
    y_b, h_b = ssd_chunked(flip(xs), flip(dt[:, :, 1]), a[1], flip(bm), flip(cm), h0_b)
    y = y_f + flip(y_b) + d_skip.astype(jnp.float32)[:, None] * xs
    y = y.reshape(b, L, SSD_WIDTH).astype(x.dtype) * jax.nn.silu(z)
    y = rms_norm_2(y.reshape(b, L, SSD_GROUPS, SSD_WIDTH // SSD_GROUPS),
                 ssd_norm.reshape(SSD_GROUPS, SSD_WIDTH // SSD_GROUPS)).reshape(b, L, SSD_WIDTH)
    out = jnp.concatenate([fourier_mix(u_f, fourier_w), y], axis=-1) @ w_out
    return x + mod3[:, 2][:, None, :] * rms_norm_2(out, norm_post), h_f, h_b

def context_states(ctx, mod3, norm_pre, w_in, conv_w, conv_b, dt_bias, a_log):
    b, L, _ = ctx.shape
    h = modulate(rms_norm_2(ctx, norm_pre), mod3[:, 0], mod3[:, 1])
    xb, dt_raw = jnp.split(h @ w_in[:, FOURIER_WIDTH + SSD_WIDTH + GROUP_STATE:],
                           [SSD_WIDTH + GROUP_STATE], axis=-1)
    xb = centred_dwconv_silu(xb, conv_w[:, GROUP_STATE:], conv_b[GROUP_STATE:])
    xs, bm = jnp.split(xb, [SSD_WIDTH], axis=-1)
    xs = xs.reshape(b, L, SSD_HEADS, SSD_HEAD_DIM)
    bm = bm.reshape(b, L, SSD_GROUPS, SSD_STATE)
    dt = softplus_dt(dt_raw, dt_bias)
    a = -jnp.exp(a_log.astype(jnp.float32))
    h_f = ssd_final_state(xs, dt[:, :, 0], a[0], bm)
    h_b = ssd_final_state(flip(xs), flip(dt[:, :, 1]), a[1], flip(bm))
    return h_f, h_b

def second_inputs(seed: int = 0) -> dict:
    key = jax.random.key(seed)
    ks = iter(jax.random.split(key, 32))
    f32 = jnp.float32
    L = DEPTH_2

    def normal(shape, scale=1.0):
        return scale * jax.random.normal(next(ks), shape, f32)

    def gain(shape):
        return 1.0 + 0.1 * jax.random.normal(next(ks), shape, f32)

    d = {}
    d['x'] = normal((BATCH, SEQ, D_MODEL))
    d['c'] = normal((BATCH, D_MODEL))
    d['ctx'] = normal((BATCH, CTX_LEN, D_MODEL))
    d['c_ctx'] = normal((D_MODEL,))
    d['ada_w'] = normal((L, D_MODEL, N_MOD * D_MODEL), D_MODEL ** -0.5)
    d['ada_b'] = normal((L, N_MOD * D_MODEL), 0.02)
    d['ffn1_norm_pre'] = gain((L, D_MODEL))
    d['ffn1_norm_post'] = gain((L, D_MODEL))
    d['ffn1_w_gate'] = normal((L, D_MODEL, D_FF), D_MODEL ** -0.5)
    d['ffn1_w_up'] = normal((L, D_MODEL, D_FF), D_MODEL ** -0.5)
    d['ffn1_w_down'] = normal((L, D_FF, D_MODEL), D_FF ** -0.5)
    d['mix_norm_pre'] = gain((L, D_MODEL))
    d['mix_norm_post'] = gain((L, D_MODEL))
    d['w_in'] = normal((L, D_MODEL, PROJ_WIDTH), D_MODEL ** -0.5)
    d['fourier_w'] = normal((L, FOURIER_HEADS, FOURIER_HEAD_DIM, FOURIER_HEAD_DIM), FOURIER_HEAD_DIM ** -0.5)
    d['conv_w'] = normal((L, CONV_WIDTH, CONV_DIM), CONV_WIDTH ** -0.5)
    d['conv_b'] = normal((L, CONV_DIM), 0.02)
    dt_init = jnp.exp(jax.random.uniform(next(ks), (L, 2, SSD_HEADS), f32, math.log(1e-3), math.log(1e-1)))
    d['dt_bias'] = dt_init + jnp.log(-jnp.expm1(-dt_init))
    d['a_log'] = jnp.log(jax.random.uniform(next(ks), (L, 2, SSD_HEADS), f32, 1.0, 16.0))
    d['d_skip'] = gain((L, SSD_HEADS))
    d['ssd_norm'] = gain((L, SSD_WIDTH))
    d['w_out'] = normal((L, MIX_WIDTH, D_MODEL), MIX_WIDTH ** -0.5)
    d['ffn2_norm_pre'] = gain((L, D_MODEL))
    d['ffn2_norm_post'] = gain((L, D_MODEL))
    d['ffn2_w_gate'] = normal((L, D_MODEL, D_FF), D_MODEL ** -0.5)
    d['ffn2_w_up'] = normal((L, D_MODEL, D_FF), D_MODEL ** -0.5)
    d['ffn2_w_down'] = normal((L, D_FF, D_MODEL), D_FF ** -0.5)
    return d

def second_block(x, c, ctx, c_ctx, ada_w, ada_b, ffn1_norm_pre, ffn1_norm_post, ffn1_w_gate, ffn1_w_up,
              ffn1_w_down, mix_norm_pre, mix_norm_post, w_in, fourier_w, conv_w, conv_b, dt_bias, a_log,
              d_skip, ssd_norm, w_out, ffn2_norm_pre, ffn2_norm_post, ffn2_w_gate, ffn2_w_up, ffn2_w_down):
    b = x.shape[0]
    for layer in range(DEPTH_2):
        mod = (jax.nn.silu(c) @ ada_w[layer] + ada_b[layer]).reshape(b, N_MOD, D_MODEL)
        mod_ctx = (jax.nn.silu(c_ctx) @ ada_w[layer] + ada_b[layer]).reshape(1, N_MOD, D_MODEL)
        ffn1 = (ffn1_norm_pre[layer], ffn1_norm_post[layer], ffn1_w_gate[layer], ffn1_w_up[layer], ffn1_w_down[layer])
        ffn2 = (ffn2_norm_pre[layer], ffn2_norm_post[layer], ffn2_w_gate[layer], ffn2_w_up[layer], ffn2_w_down[layer])
        mix = (mix_norm_pre[layer], mix_norm_post[layer], w_in[layer], fourier_w[layer], conv_w[layer],
               conv_b[layer], dt_bias[layer], a_log[layer], d_skip[layer], ssd_norm[layer], w_out[layer])

        x = macaron_ffn(x, mod[:, 0:3], *ffn1)
        ctx = macaron_ffn(ctx, mod_ctx[:, 0:3], *ffn1)

        if layer + 1 < DEPTH_2:
            zeros = jnp.zeros((b, SSD_HEADS, SSD_HEAD_DIM, SSD_STATE), jnp.float32)
            ctx, h_ctx_f, h_ctx_b = mix_sublayer(ctx, mod_ctx[:, 3:6], zeros, zeros, *mix)
        else:
            h_ctx_f, h_ctx_b = context_states(ctx, mod_ctx[:, 3:6], mix_norm_pre[layer], w_in[layer],
                                              conv_w[layer], conv_b[layer], dt_bias[layer], a_log[layer])

        x, _, _ = mix_sublayer(x, mod[:, 3:6], h_ctx_f, h_ctx_b, *mix)

        x = macaron_ffn(x, mod[:, 6:9], *ffn2)
        if layer + 1 < DEPTH_2:
            ctx = macaron_ffn(ctx, mod_ctx[:, 6:9], *ffn2)
    return x


def setup_inputs(seed=0):
    out = dict(first_inputs(seed))
    for name, value in second_inputs(seed + 1).items():
        if name != "x":
            out[name + "_2"] = value
    return out


def reference(
    x, norm_mix_pre, norm_mix_post, norm_ffn_pre, norm_ffn_post, w_in, w_out, conv_dw_w,
    conv_dw_b, conv_ln_g, conv_ln_b, nsa_pe_k, nsa_pe_v, nsa_ck_w1, nsa_ck_w2, nsa_cv_w1,
    nsa_cv_w2, sgu_ln_g, sgu_ln_b, sgu_w, sgu_b, pool_w, pool_scale, ffn_up, ffn_conv_w,
    ffn_conv_b, ffn_down, c_2, ctx_2, c_ctx_2, ada_w_2, ada_b_2, ffn1_norm_pre_2,
    ffn1_norm_post_2, ffn1_w_gate_2, ffn1_w_up_2, ffn1_w_down_2, mix_norm_pre_2,
    mix_norm_post_2, w_in_2, fourier_w_2, conv_w_2, conv_b_2, dt_bias_2, a_log_2, d_skip_2,
    ssd_norm_2, w_out_2, ffn2_norm_pre_2, ffn2_norm_post_2, ffn2_w_gate_2, ffn2_w_up_2,
    ffn2_w_down_2,
):
    x = first_block(
        x, norm_mix_pre, norm_mix_post, norm_ffn_pre, norm_ffn_post, w_in, w_out, conv_dw_w,
        conv_dw_b, conv_ln_g, conv_ln_b, nsa_pe_k, nsa_pe_v, nsa_ck_w1, nsa_ck_w2, nsa_cv_w1,
        nsa_cv_w2, sgu_ln_g, sgu_ln_b, sgu_w, sgu_b, pool_w, pool_scale, ffn_up, ffn_conv_w,
        ffn_conv_b, ffn_down,
    )
    return second_block(
        x, c_2, ctx_2, c_ctx_2, ada_w_2, ada_b_2, ffn1_norm_pre_2, ffn1_norm_post_2,
        ffn1_w_gate_2, ffn1_w_up_2, ffn1_w_down_2, mix_norm_pre_2, mix_norm_post_2, w_in_2,
        fourier_w_2, conv_w_2, conv_b_2, dt_bias_2, a_log_2, d_skip_2, ssd_norm_2, w_out_2,
        ffn2_norm_pre_2, ffn2_norm_post_2, ffn2_w_gate_2, ffn2_w_up_2, ffn2_w_down_2,
    )


_drawn_inputs = setup_inputs


def setup_inputs(seed=0):
    import zlib

    import numpy as np

    out = dict(_drawn_inputs(seed))
    spreads = {}
    factors = {'conv_ln_b': 5.433,
     'nsa_pe_k': 8.0,
     'sgu_ln_g': 3.207,
     'sgu_ln_b': 7.948,
     'ctx_2': 41.056,
     'ada_b_2': 3.747,
     'ffn1_norm_pre_2': 3.212,
     'ffn1_norm_post_2': 3.855,
     'conv_b_2': 8.0,
     'd_skip_2': 184.833,
     'ffn2_norm_pre_2': 3.46,
     'ffn2_norm_post_2': 4.361,
     'nsa_pe_v': 2.799,
     'c_ctx_2': 5.181,
     'ssd_norm_2': 2.809}
    for name, (base, spread) in spreads.items():
        noise = np.random.default_rng([zlib.crc32(name.encode()), seed]).standard_normal(out[name].shape)
        drawn = base * np.exp(spread * noise) if base else spread * noise
        out[name] = jnp.asarray(drawn.astype(out[name].dtype))
    for name, factor in factors.items():
        out[name] = (out[name] * factor).astype(out[name].dtype)
    return out
```

```python
from contextlib import ExitStack

import numpy as np

import concourse.bass as bass
from concourse import mybir
from concourse.alu_op_type import AluOpType as ALU

ACT = mybir.ActivationFunctionType
F32 = mybir.dt.float32
F32R = mybir.dt.float32r
AX_X = mybir.AxisListType.X

P = 128
T = 256
D = 1024
KD = D // P
FF = 2816
FB = FF // P
LAYERS = 2
RING = 3
CHUNK = 2048
DVE_PART = 1280
PAD = 30
N_CMP = 15
HEADS1 = 4
W1_COLS = 1932
GATE_COL = 1152
SGU_COL = 1164
POOL_COL = 1676
MIX1_CHUNKS = 8
OUT_CHUNKS = 4
UP_CHUNKS = FB
DOWN_CHUNKS = FB // 2
LAYER_CHUNKS = MIX1_CHUNKS + OUT_CHUNKS + UP_CHUNKS + DOWN_CHUNKS
OUT1_ORDER = (2, 3, 1, 0)

ADA_BLOCKS = 72
ADA_LAYER = ADA_BLOCKS // LAYERS
SSD_HEADS, GROUPS, GW = 12, 4, 192
CONV_BLOCKS = 14
MIX2_CHUNKS = 12
CTX_PROJ_CHUNKS = 6
MIX2_COLS = 2840

V_NORM = 0
V_SSDN, V_ADAB, V_ROWS = 48, 54, 126
V_CW, V_CB, V_ROWS2 = 0, 42, 56

R_MIX_PRE, R_MIX_POST, R_FFN_PRE, R_FFN_POST = 0, 8, 16, 24
R_DW, R_DWB, R_CLG, R_CLB, R_PSC, R_SGB, R_ROWS = 32, 94, 96, 98, 100, 102, 106


def tables():
    i = np.arange(P)
    blk = lambda m: np.kron(np.eye(2), m)
    cols = {}
    cols["ident"] = np.eye(P)
    cols["ones"] = np.ones((P, P))
    row, col = i[:, None], i[None, :]
    cols["col_ge"] = col >= row
    cols["col_le"] = col <= row
    cols["col_lt"] = col < row
    cols["col_gt"] = col > row
    cols["bar_ge"] = np.where(col >= row, 0.0, -1e30)
    cols["bar_le"] = np.where(col <= row, 0.0, -1e30)
    shared, cols = cols, {}
    half = 32
    r = np.zeros((64, 64))
    r[np.arange(half) + half, np.arange(half)] = -1.0
    r[np.arange(half), np.arange(half) + half] = 1.0
    cols["rope_turn"] = blk(r)
    twice = np.zeros((P, P))
    twice[:64] = np.concatenate([np.eye(64), np.eye(64)], axis=1)
    cols["twice"] = twice
    turned = np.zeros((P, P))
    turned[:64] = np.concatenate([r, r], axis=1)
    cols["twice_turn"] = turned
    inv = (np.float32(10000.0) ** (-np.arange(half, dtype=np.float32) * np.float32(2.0) / np.float32(64)))
    ang = (np.arange(T, dtype=np.float32)[:, None] * inv[None, :].astype(np.float32)).astype(np.float32)
    cols["cos"] = np.tile(np.cos(ang).T, (4, 1))
    cols["sin"] = np.tile(np.sin(ang).T, (4, 1))
    ends = np.arange(16) * 16 + 31
    seen = np.stack([ends[None, :] <= (b * P + i)[:, None] for b in range(2)], axis=1)
    cols["cmp_bar"] = np.where(seen, 0.0, -1e30).reshape(P, 32)
    cols["cmp_seen"] = seen.reshape(P, 32)
    w = np.array([[2, 4], [8, 16]])
    n = np.zeros((P, 2, T))
    for b in range(2):
        for h in range(2):
            n[64 * h:64 * h + 64, b] = 1.0 / np.minimum(np.arange(T) + 1, w[b, h])
    cols["inv_count"] = n.reshape(P, 2 * T)
    shared["eps6"] = np.full((P, 1), 1e-6)
    shared["eps5"] = np.full((P, 1), 1e-5)
    cols2 = {}
    cols2["bars"] = np.concatenate([np.where(col >= row, 0.0, -1e30), np.zeros((P, P)), np.where(col <= row, 0.0, -1e30)], axis=1)
    d = np.arange(64)
    angle = 2 * np.pi * ((d[:, None] * d[None, :]) % 64) / 64
    cols2["dft_head"] = np.concatenate([blk(np.cos(angle)) / 128, blk(-np.sin(angle)) / 128], axis=1)
    t = np.arange(T)
    angle = (2 * np.pi * ((t[:, None] * t[None, :]) % T) / T).reshape(2, P, T).transpose(1, 0, 2)
    cols2["dft_cos"] = np.cos(angle)
    cols2["dft_sin"] = np.sin(angle)
    pick = np.zeros((P, 12, P))
    pair = np.zeros((P, 6, P))
    for h in range(12):
        pick[h, h] = 1.0
        pair[h, h // 2, 64 * (h % 2):64 * (h % 2) + 64] = 1.0
    cols2["pick_head"] = pick
    cols2["pick_pair"] = pair
    feature = np.arange(6 * P) // 192
    member = (feature[:, None] == np.arange(4)[None, :]).reshape(6, P, 4)
    cols2["member"] = member.transpose(1, 0, 2)
    spread = np.zeros((P, 6, P))
    spread[0:4] = member.transpose(2, 0, 1)
    cols2["spread"] = spread
    def packed(cols):
        at, parts, n = {}, [], 0
        for name, a in cols.items():
            a = np.asarray(a, np.float32).reshape(P, -1)
            at[name] = (n, a.shape[1])
            parts.append(a)
            n += a.shape[1]
        return at, np.ascontiguousarray(np.concatenate(parts, axis=1))

    return packed(shared), packed(cols), packed(cols2)


class Event:

    def __init__(self, sem, per=1):
        self.sem, self.per = sem, per

    def after(self, call, steps=None):
        return call * self.per + (self.per if steps is None else steps)


class Place:

    def __init__(self, fixed, turns=0):
        self.fixed, self.turns = fixed, turns

    def at(self, steps, turns=0):
        return Place(self.fixed + steps, self.turns + turns)

    @property
    def slot(self):
        return self.fixed % RING

    @property
    def reused(self):
        return self.fixed >= RING or not isinstance(self.turns, int) or self.turns > 0

    def count(self, steps=0):
        return self.turns * RING + (self.fixed + steps)

    def landed(self):
        return self.turns * 32 + 32 * (self.fixed // RING + 1)


class Steps:

    def __init__(self, eng, sem):
        self.eng, self.sem, self.base, self.n = eng, sem, 0, 0

    def __call__(self, ins):
        self.n += 1
        ins.then_inc(self.sem, 1)
        self.eng.wait_ge(self.sem, self.base + self.n)

    def enter(self, i, first, per):
        self.saved = (self.base, self.n, first, per)
        self.base, self.n = self.base + self.n + (i - first) * per, 0

    def leave(self, last):
        base, n, first, per = self.saved
        assert self.n == per, (self.n, per)
        self.base, self.n = base, n + (last - first) * per


def build(nc, names, ins, out, at, at1, at2):
    a = dict(zip(names, ins))
    ctx = ExitStack()
    with ctx:
        def sb(name, shape, dt=F32):
            return ctx.enter_context(nc.sbuf_tensor(name, shape, dt))

        def sem(name):
            return ctx.enter_context(nc.semaphore(name))

        def event(name, per=1):
            return Event(sem(name), per)

        tab = sb("tab", [P, a["tables"].shape[1]])
        K = {k: tab[:, o:o + w] for k, (o, w) in at.items()}
        raw = [sb(f"raw{i}", [P, CHUNK]) for i in range(RING)]
        whi = [sb(f"whi{i}", [P, CHUNK], F32R) for i in range(RING)]
        wlo = [sb(f"wlo{i}", [P, CHUNK], F32R) for i in range(RING)]
        xT = sb("xT", [P, KD, T])
        hhi = sb("hhi", [P, KD, T], F32R)
        hlo = sb("hlo", [P, KD, T], F32R)
        work = sb("work", [P, KD, T])
        rstd = sb("rstd", [P, T])
        root = sb("root", [P, T])

        ada = [sb(f"ada{i}", [P, KD, P]) for i in range(2)]
        crow = sb("crow", [16, P])
        vcol = sb("vcol", [P, R_ROWS])
        fcol = sb("fcol", [P, 2, 88])
        csil = sb("csil", [P, 2, KD])
        mod = sb("mod", [P, ADA_BLOCKS, 2])
        before = nc.sbuf_bytes_remaining
        with ExitStack() as one_ctx:
            def one_(name, shape, dt=F32):
                return one_ctx.enter_context(nc.sbuf_tensor(name, shape, dt))

            vrow = one_("vrow", [R_ROWS, P])
            perow = one_("perow", [32, P])
            pecol = one_("pecol", [P, 32])
            frow = one_("frow", [88, 2, P])
            sgln = one_("sgln", [P, 2, T])
            wsp = one_("wsp", [P, 4, P])
            bsp = one_("bsp", [P, 2, P])
            cw1 = one_("cw1", [P, 32, 64])
            cw2 = one_("cw2", [P, 192])
            pw = one_("pw", [P, 2, P])
            glu = one_("glu", [P, 2, PAD + T])
            zpad = one_("zpad", [P, 2, 16 + T])
            psum2 = one_("psum2", [P, 4, 16 + T])
            gates = one_("gates", [P, 2, 12])
            hid = one_("hid", [P, 16])
            kc = one_("kc", [P, 16])
            vc = one_("vc", [N_CMP, 64])
            mx = one_("mx", [P, 8])
            sm = one_("sm", [P, 8])
            gs = one_("gs", [P, 8])
            bns = one_("bns", [P, 2, 6])
            mv = one_("mv", [P, 2, 2])
            srt = one_("srt", [P, 4])
            tab1 = one_("tab1", [P, a["tables_1"].shape[1]])
            K.update({k: tab1[:, o:o + w] for k, (o, w) in at1.items()})
            size_one = before - nc.sbuf_bytes_remaining
        tab2 = sb("tab2", [P, a["tables_2"].shape[1]])
        K2 = {k: tab2[:, o:o + w] for k, (o, w) in at2.items()}
        cT = sb("cT", [P, KD, T])
        h0 = cT[:].rearrange("p k t -> p (k t)")[:, 0:GROUPS * 2 * GW].rearrange("p (g d c) -> p g d c", g=GROUPS, d=2)
        xrow = sb("xrow", [P, 2, P])
        xcol = sb("xcol", [P, 2, P])
        gain2 = sb("gain2", [P, 9, KD])
        drow = sb("drow", [P, 3, 24])
        small = sb("small", [P, 8, 2, 24])
        skip_all = sb("skip_all", [P, SSD_HEADS])
        dsk = sb("dsk", [P, 6])
        fw = sb("fw", [P, 2, P])
        short = size_one - (before - nc.sbuf_bytes_remaining)
        if short > 0:
            sb("rest_of_region", [P, short // 4 + 8])
        with ExitStack() as turn_ctx:
            def tmp(name, shape, dt=F32):
                return turn_ctx.enter_context(nc.sbuf_tensor(name, shape, dt))

            wspT = tmp("wspT", [P, 4, P])
            aT = tmp("aT", [P, 2, T])
            sig = tmp("sig", [P, 2, T])
            qT = tmp("qT", [P, 2, T])
            qrot = tmp("qrot", [P, 2, T])
            krot = tmp("krot", [P, 2, T])
            rt = tmp("rt", [P, 2, T])
            kvT = tmp("kvT", [P, 4, T])
            uT = tmp("uT", [P, 2, T])
            vT = tmp("vT", [P, 2, T])
            pooled = tmp("pooled", [P, 2, T])
            vtok = tmp("vtok", [P, 4, 64])
            cbuf = tmp("cbuf", [P, 32, N_CMP])
            sc = tmp("sc", [P, 4, T])
            prob = tmp("prob", [P, 4, T])
            scc = tmp("scc", [P, 8, 16])
            probc = tmp("probc", [P, 8, 16])
            pT = tmp("pT", [P, 6, 4, P])
            outt = pT[:].rearrange("p b h k -> p (b h k)")[:, 0:2 * D].rearrange("p (t d) -> p t d", t=2)
            pcT = tmp("pcT", [16, 8, P])
            vn = tmp("vn", [P, 2, T])
            convy = aT
        with ExitStack() as turn_ctx:
            def tmp(name, shape, dt=F32):
                return turn_ctx.enter_context(nc.sbuf_tensor(name, shape, dt))

            ctx_cv = tmp("ctx_cv", [P, 10, T])
            ctx_dt = tmp("ctx_dt", [P, T])
            btok = tmp("btok", [P, 2, 4 * P])
            xw = tmp("xw", [P, 2, 2, 6 * P])
        with ExitStack() as turn_ctx:
            def tmp(name, shape, dt=F32):
                return turn_ctx.enter_context(nc.sbuf_tensor(name, shape, dt))

            uf = tmp("uf", [P, 2, T])
            zs = tmp("zs", [P, 6, T])
            cv = tmp("cv", [P, CONV_BLOCKS, T])
            dtT = tmp("dtT", [P, T])
            xtok = tmp("xtok", [P, 2, 6 * P])
            cb = tmp("cb", [P, GROUPS, 2, T])
            csr = tmp("csr", [SSD_HEADS, 2, T])
            ex = tmp("ex", [P, 2, 3 * T])
            pcs = ex[:].rearrange("p a b -> p (a b)")[:, 0:4 * T].rearrange("p (t b c) -> p t b c", t=2, b=2)
            mt = tmp("mt", [P, 2, 2, T])
            ep = tmp("ep", [P, 2, T])
            yo = tmp("yo", [P, 2, T])
            grt = tmp("grt", [4, T])
            grs = tmp("grs", [4, T])
        ahi = sb("ahi", [P, FB, T], F32R)
        alo = sb("alo", [P, FB, T], F32R)
        taps = sb("taps", [P, RING, 2, T])
        gel = sb("gel", [P, RING, T])
        prod = gel

        lin = ctx.enter_context(nc.psum_tensor("lin", [P, RING, 512], F32))
        acc = ctx.enter_context(nc.psum_tensor("acc", [P, 4, 512], F32))
        misc = ctx.enter_context(nc.psum_tensor("misc", [P, 512], F32))

        s_raw = [sem(f"raw_landed{i}") for i in range(RING)]
        s_hi = sem("high_parts_ready")
        s_lo = sem("low_parts_ready_vector")
        s_lop = sem("low_parts_ready_gpsimd")
        s_used = sem("chunk_used")
        s_tab = sem("tables_landed")
        s_x = sem("x_landed")
        s_par = sem("mixer_vectors_landed")
        s_parw = sem("mixer_weights_landed")
        s_fpar = sem("ffn_vectors_landed")
        s_zero = sem("zeros_written")
        s_st = {e: sem(f"{e}_own_steps") for e in ("pe", "act", "dve", "pool")}
        s_fin = sem("output_turned")
        s_outr = sem("output_ready")
        s_out = sem("output_landed")

        e_xt = event("input_turned", 4)
        e_xc = event("input_copied", 4)
        e_vt = event("vectors_turned", 1)
        e_vc = event("vectors_copied", 1)
        e_sq = event("squares_ready", KD)
        e_ss = event("sum_of_squares_ready", 1)
        e_rt = event("root_ready", 1)
        e_nv = event("normed_ready", KD)
        e_nh = event("norm_high_ready", KD)
        e_h = event("h_ready", KD)
        e_psq = event("post_squares_ready", 4)
        e_pss = event("post_sum_ready", 1)
        e_prt = event("post_root_ready", 1)
        e_pt = event("post_scaled_ready", KD)
        e_x = event("residual_updated", KD)
        e_c0 = event("first_tap_ready", FB)
        e_cv = event("taps_ready", FB)
        e_gl = event("gelu_ready", FB)
        e_pr = event("product_ready", FB)
        e_ah = event("act_high_ready", FB)
        e_al = event("act_ready", FB)
        e_sg = event("gate_silu_ready", FB)
        s_crow = sem("conditions_landed")
        e_ct = sem("conditions_turned")
        e_cs = sem("conditions_ready")
        s_ada = [sem(f"modulation_landed{i}") for i in range(2)]
        e_ad = event("modulation_block_used", ADA_LAYER)
        e_am = event("modulation_copied", 1)
        s_p2 = sem("second_parameters_landed")
        s_ctx = sem("ctx_landed")
        p_ea = sem("projection_read_scalar")
        p_ed = sem("projection_read_vector")
        p_c0 = sem("middle_tap_ready")
        p_si = sem("convolved_ready")
        (t_vt, t_vc, t_gn, d_tr, d_x, d_e, d_a, d_dt, d_cs, d_cc, c_w, c_xt, c_bt, c_bc, c_xw, c_h, c_hc, f_p, f_pc, f_f,
         f_fc, f_y, f_yc, x_cb, x_cbc, x_xt, x_xc, x_csr, x_csc, x_cs, x_d, x_e, x_m, x_mm, x_y, x_yo, x_ps, x_ep, x_t, x_yp,
         x_sq, x_gs, x_gr, x_gi, x_sp, x_cat, x_ch, x_cl) = (event(name) for name in (
             "second_vectors_turned", "second_vectors_copied", "gains_ready", "steps_turned", "steps_biased",
             "steps_exponential", "decay_rates_ready", "steps_ready", "decays_summed", "decays_copied",
             "state_weights_ready", "x_turned", "b_turned", "b_copied", "weighted_x_ready", "states_ready", "states_copied",
             "fourier_heads", "fourier_heads_copied", "fourier_tokens", "fourier_tokens_copied", "fourier_out",
             "fourier_out_copied", "bc_ready", "bc_copied", "x_rows_turned", "x_rows_copied", "decays_by_head",
             "decays_by_head_copied", "decays_spread", "decay_differences_ready", "decay_factors_ready",
             "matrix_factors_ready", "mixing_matrix_ready", "head_output_ready", "state_output_ready",
             "pair_decays_spread", "pair_decays_ready", "state_terms_ready", "pair_gated", "pair_squares_ready",
             "group_sums_ready", "group_roots_ready", "group_factors_ready", "group_factors_spread", "pair_normed",
             "second_branch_high", "second_branch_ready"))
        m_ev = event("projection_copied", MIX1_CHUNKS)
        m_rope = event("turned_keys_queries_ready", 1)
        m_tr = event("values_gates_turned", 1)
        m_qk = event("rotary_ready", 1)
        m_vt = event("values_gates_copied", 1)
        m_cb = event("compression_input_ready", 1)
        m_hid = event("compression_hidden", 1)
        m_hg = event("compression_gelu", 1)
        m_kc = event("compressed_ready", 1)
        m_kcc = event("compressed_copied", 1)
        m_glu = event("glu_ready", 1)
        m_sc = event("scores_ready", 4)
        m_mx = event("maxima_ready", 4)
        m_ex = event("exponentials_ready", 4)
        m_gs = event("row_factors_ready", 4)
        m_pb = event("probabilities_ready", 4)
        m_pt = event("probabilities_turned", 8)
        m_pc = event("probabilities_copied", 8)
        m_o = event("attention_out", 1)
        m_vx = event("gate_values_turned", 2)
        m_bn = event("gate_variance_ready", 1)
        m_br = event("gate_root_ready", 1)
        m_vn = event("gate_values_centred", 1)
        m_vw = event("gate_values_ready", 1)
        m_ws = event("spatial_weights_ready", 1)
        m_f = event("spatial_out", 1)
        m_pl = event("pooled_ready", 1)
        m_pm = event("pool_out", 1)
        m_cy = event("conv_ready", 1)
        m_cs = event("conv_sum_ready", 2)
        m_cc = event("conv_centred", 1)
        m_cq = event("conv_squares", 1)
        m_cr = event("conv_root", 1)
        m_cn = event("conv_normed", 1)
        m_csg = event("gating_output_ready", 1)
        m_cns = event("attention_output_ready", 1)
        m_cah = event("branch_high_ready", 4)
        m_cal = event("branch_ready", 4)

        block = ctx.enter_context(nc.Block())

        def mm(out_, lhsT, rhs, start=True, stop=True, **kw):
            return nc.tensor.matmul(out_, lhsT, rhs, start=start, stop=stop, **kw)

        def mm3(out_, w, xh, xl, first, last):
            wh, wl = w
            mm(out_, wh, xh, start=first, stop=False, skip_group_check=True)
            mm(out_, wh, xl, start=False, stop=False, skip_group_check=True)
            return mm(out_, wl, xh, start=False, stop=last, skip_group_check=True)

        def ring(place):
            return whi[place.slot], wlo[place.slot]

        def load(sp, n, pieces):
            if n.reused:
                sp.wait_ge(s_lo, n.count(1 - RING))
                sp.wait_ge(s_lop, n.count(1 - RING))
            assert len(pieces) == 2
            for dst, src in pieces:
                sp.dma_start(dst, src).then_inc(s_raw[n.slot], 16)

        def split_high(act, n, width=CHUNK):
            act.wait_ge(s_raw[n.slot], n.landed())
            if n.reused:
                act.wait_ge(s_used, n.count(1 - RING))
            nc.scalar.activation(whi[n.slot][:, 0:width], raw[n.slot][:, 0:width], ACT.Copy).then_inc(s_hi, 1)

        def split_low(eng, n, width=CHUNK):
            eng.wait_ge(s_hi, n.count(1))
            part = DVE_PART * width // CHUNK
            lo, hi, done = (0, part, s_lo) if eng is dve_ else (part, width, s_lop)
            eng.tensor_tensor(wlo[n.slot][:, lo:hi], raw[n.slot][:, lo:hi],
                              whi[n.slot][:, lo:hi].bitcast(F32), ALU.subtract).then_inc(done, 1)

        dve_ = nc.vector

        def by_threes(eng, n_steps, body, steps=None, per=0):
            full = n_steps // RING
            for j in range(RING):
                body(j, 0)
            with eng.Fori(1, full) as turn:
                if steps:
                    steps.enter(turn, 1, per)
                for j in range(RING):
                    body(j, turn)
                if steps:
                    steps.leave(full)
            for j in range(n_steps - RING * full):
                body(j, full)

        def base(layer):
            return Place(STREAM0, 0).at(0, layer * (LAYER_CHUNKS // RING))

        STREAM0 = 0
        TOTAL = STREAM0 + LAYERS * LAYER_CHUNKS

        def load_cols(sp, n, w, c0, width):
            dst = raw[n.slot][:, 0:KD * width].rearrange("p (k c) -> p k c", k=KD)
            src = w.rearrange("(k p) c -> p k c", p=P)
            h = KD // 2
            load(sp, n, [(dst[:, 0:h], src[:, 0:h, c0:c0 + width]), (dst[:, h:KD], src[:, h:KD, c0:c0 + width])])

        def load_rows(sp, n, w, r0):
            load(sp, n, [(raw[n.slot][:, D * j:D * j + D], w[bass.ds(r0 + j * P, P), :]) for j in range(2)])

        def load_ffn(sp, n0, w_gate, w_up, w_down):
            def up(j, turn):
                n = n0.at(j, turn)
                dst = raw[n.slot][:].rearrange("p (s k c) -> p s k c", s=2, k=KD)
                load(sp, n, [(dst[:, s], w.rearrange("(k p) c -> p k c", p=P)[:, :, bass.ds(turn * (RING * P) + j * P, P)])
                             for s, w in enumerate((w_gate, w_up))])
            by_threes(sp, UP_CHUNKS, up)
            by_threes(sp, DOWN_CHUNKS, lambda j, turn: load_rows(
                sp, n0.at(UP_CHUNKS + j, turn), w_down, turn * (2 * RING * P) + 2 * j * P))

        def one(ap, layer):
            return ap[bass.ds(layer, 1)].squeeze(0)

        def load_mixer_params(sp, layer):
            rows = lambda n: one(a[n], layer).rearrange("(r p) -> r p", p=P)
            for r0, name, k in ((R_MIX_PRE, "norm_mix_pre", 8), (R_MIX_POST, "norm_mix_post", 8),
                                (R_FFN_PRE, "norm_ffn_pre", 8), (R_FFN_POST, "norm_ffn_post", 8),
                                (R_DWB, "conv_dw_b", 2), (R_CLG, "conv_ln_g", 2), (R_CLB, "conv_ln_b", 2),
                                (R_PSC, "pool_scale", 2)):
                sp.dma_start(vrow[r0:r0 + k, :], rows(name)).then_inc(s_par, 16)
            sp.dma_start(vrow[R_DW:R_DW + 62, :], one(a["conv_dw_w"], layer).rearrange("k (b p) -> (k b) p", p=P)).then_inc(s_par, 16)
            sp.dma_start(vrow[R_SGB:R_SGB + 4, :], one(a["sgu_b"], layer)).then_inc(s_par, 16)
            sp.dma_start(perow[:, 0:64], one(a["nsa_pe_k"], layer)).then_inc(s_par, 16)
            sp.dma_start(perow[:, 64:128], one(a["nsa_pe_v"], layer)).then_inc(s_par, 16)
            for j, name in enumerate(("sgu_ln_g", "sgu_ln_b")):
                sp.dma_start(sgln[:, j, :], a[name][bass.ds(layer, 1), :].broadcast_to([P, T])).then_inc(s_parw, 16)
            sp.dma_start(wsp[:], one(a["sgu_w"], layer).rearrange("g t s -> t g s")).then_inc(s_parw, 16)
            for g in range(4):
                sp.dma_start(bsp[64 * (g % 2):64 * (g % 2) + 64, g // 2, :],
                             one(a["sgu_b"], layer)[g:g + 1, :].broadcast_to([64, P])).then_inc(s_parw, 16)
            for h, name in enumerate(("nsa_ck_w1", "nsa_cv_w1")):
                sp.dma_start(cw1[64 * h:64 * h + 64, :, :],
                             one(a[name], layer).rearrange("(l d) e -> d l e", d=64)).then_inc(s_parw, 16)
            sp.dma_start(cw2[0:64, 0:64], one(a["nsa_ck_w2"], layer)).then_inc(s_parw, 16)
            sp.dma_start(cw2[0:64, 64:128], one(a["nsa_ck_w2"], layer)).then_inc(s_parw, 16)
            sp.dma_start(cw2[64:128, 128:192], one(a["nsa_cv_w2"], layer)).then_inc(s_parw, 16)
            for g in range(4):
                h = 64 * (g % 2)
                sp.dma_start(pw[h:h + 64, g // 2, h:h + 64],
                             a["pool_w"][bass.ds(layer, 1), g].squeeze(0)).then_inc(s_parw, 16)
        N_PAR, N_PARW = 12 * 16, 16 * 16

        def load_ffn_params(sp, layer):
            rows = one(a["ffn_conv_w"], layer).rearrange("k (b p) -> k b p", p=P)
            sp.dma_start(frow[0:44, 0, :], rows[0]).then_inc(s_fpar, 16)
            sp.dma_start(frow[44:88, 0, :], rows[1]).then_inc(s_fpar, 16)
            sp.dma_start(frow[0:44, 1, :], rows[2]).then_inc(s_fpar, 16)
            sp.dma_start(frow[44:88, 1, :], one(a["ffn_conv_b"], layer).rearrange("(b p) -> b p", p=P)).then_inc(s_fpar, 16)
        N_FPAR = 4 * 16

        def pre_pe(pe, c):
            for k in range(KD):
                pe.wait_ge(e_sq.sem, e_sq.after(c, k + 1))
                i = mm(misc[:, 0:T], K["ones"], work[:, k, :], start=(k == 0), stop=(k == KD - 1))
            i.then_inc(e_ss.sem, 1)

        def pre_act(act, c, x, x_ready, shift=None):
            for k in range(KD):
                x_ready(act, k)
                nc.scalar.activation(work[:, k, :], x[:, k, :], ACT.Square).then_inc(e_sq.sem, 1)
            act.wait_ge(e_ss.sem, e_ss.after(c))
            nc.scalar.activation(root[:], misc[:, 0:T], ACT.Sqrt, bias=K["eps6"], scale=1.0 / D).then_inc(e_rt.sem, 1)
            for k in range(KD):
                act.wait_ge(e_nv.sem, e_nv.after(c, k + 1))
                if shift:
                    i = nc.scalar.activation(hhi[:, k, :], work[:, k, :], ACT.Identity, bias=shift(k))
                else:
                    i = nc.scalar.activation(hhi[:, k, :], work[:, k, :], ACT.Copy)
                i.then_inc(e_nh.sem, 1)

        def pre_dve(dve, st, c, x, gain, shift=None):
            dve.wait_ge(e_rt.sem, e_rt.after(c))
            st(dve.reciprocal(rstd[:], root[:]))
            for k in range(KD):
                dve.scalar_tensor_tensor(out=work[:, k, :], in0=x[:, k, :], scalar=gain(k), in1=rstd[:],
                                         op0=ALU.mult, op1=ALU.mult).then_inc(e_nv.sem, 1)
            for k in range(KD):
                dve.wait_ge(e_nh.sem, e_nh.after(c, k + 1))
                if shift:
                    i = dve.scalar_tensor_tensor(out=hlo[:, k, :], in0=work[:, k, :], scalar=shift(k),
                                                 in1=hhi[:, k, :].bitcast(F32), op0=ALU.add, op1=ALU.subtract)
                else:
                    i = dve.tensor_tensor(hlo[:, k, :], work[:, k, :], hhi[:, k, :].bitcast(F32), ALU.subtract)
                i.then_inc(e_h.sem, 1)

        def post_pe(pe, c):
            for b in range(4):
                pe.wait_ge(e_psq.sem, e_psq.after(c, b + 1))
                for k in (2 * b, 2 * b + 1):
                    i = mm(misc[:, 0:T], K["ones"], work[:, k, :], start=(k == 0), stop=(k == KD - 1))
            i.then_inc(e_pss.sem, 1)

        def post_act(act, c, used):
            act.wait_ge(s_used, used)
            for b in range(4):
                nc.scalar.activation(work[:, 2 * b:2 * b + 2, :], acc[:, b, :].rearrange("p (k t) -> p k t", k=2),
                                     ACT.Square).then_inc(e_psq.sem, 1)
            act.wait_ge(e_pss.sem, e_pss.after(c))
            nc.scalar.activation(root[:], misc[:, 0:T], ACT.Sqrt, bias=K["eps6"], scale=1.0 / D).then_inc(e_prt.sem, 1)

        def post_dve(dve, st, c, gain):
            dve.wait_ge(e_prt.sem, e_prt.after(c))
            st(dve.reciprocal(rstd[:], root[:]))
            for k in range(KD):
                dve.scalar_tensor_tensor(out=work[:, k, :], in0=acc[:, k // 2, (k % 2) * T:(k % 2) * T + T],
                                         scalar=gain(k), in1=rstd[:], op0=ALU.mult,
                                         op1=ALU.mult).then_inc(e_pt.sem, 1)

        def post_pool(pool, c, x):
            for k in range(KD):
                pool.wait_ge(e_pt.sem, e_pt.after(c, k + 1))
                pool.tensor_tensor(x[:, k, :], x[:, k, :], work[:, k, :], ALU.add).then_inc(e_x.sem, 1)

        def after_post(c):
            return lambda eng, k: eng.wait_ge(e_x.sem, e_x.after(c, k + 1))

        def cols_pe(pe, n, out_, blocks, first_k=None, width=256, offs=(0, P)):
            w = [t[:, 0:KD * width].rearrange("p (k c) -> p k c", k=KD) for t in ring(n)]
            pe.wait_ge(s_lo, n.count(1))
            pe.wait_ge(s_lop, n.count(1))
            for b in range(blocks):
                for k in range(KD):
                    if first_k and b == 0:
                        first_k(k)
                    i = mm3(out_[:, b * T:(b + 1) * T], [t[:, k, offs[b]:offs[b] + P] for t in w], hhi[:, k, :],
                            hlo[:, k, :], k == 0, k == KD - 1)
            i.then_inc(s_used, 1)
            return i

        def rows_pe(pe, n, xh, xl, pair, first, last, half_ready):
            w = [t[:].rearrange("p (j m) -> p j m", j=2) for t in ring(n)]
            pe.wait_ge(s_lo, n.count(1))
            pe.wait_ge(s_lop, n.count(1))
            for j in range(2):
                half_ready(j)
                for m in range(KD):
                    i = mm3(acc[:, m // 2, (m % 2) * T:(m % 2) * T + T], [t[:, j, m * P:(m + 1) * P] for t in w],
                            xh(j), xl(j), first and j == 0 and m % 2 == 0, last and j == 1)
            i.then_inc(s_used, 1)
            return i

        def ffn_pe(pe, f, n0):
            def up(j, turn):
                n = n0.at(j, turn)
                static = isinstance(turn, int) and turn == 0
                if not static:
                    pe.wait_ge(e_cv.sem, f * FB + turn * RING + (j + 1 - RING))
                w = [t[:].rearrange("p (s k c) -> p s k c", s=2, k=KD) for t in ring(n)]
                pe.wait_ge(s_lo, n.count(1))
                pe.wait_ge(s_lop, n.count(1))
                for s in range(2):
                    for k in range(KD):
                        if static and j == 0 and s == 0:
                            pe.wait_ge(e_h.sem, e_h.after(PRE_OF(f), k + 1))
                        i = mm3(lin[:, n.slot, s * T:(s + 1) * T], [t[:, s, k, :] for t in w], hhi[:, k, :],
                                hlo[:, k, :], k == 0, k == KD - 1)
                i.then_inc(s_used, 1)
            by_threes(pe, UP_CHUNKS, up)

            def down(j, turn):
                n = n0.at(UP_CHUNKS + j, turn)
                first = isinstance(turn, int) and turn == 0 and j == 0
                last = isinstance(turn, int) and 3 * turn + j == DOWN_CHUNKS - 1
                blk = turn * (2 * RING) + 2 * j
                i = rows_pe(pe, n, lambda h: ahi[:, bass.ds(blk + h, 1), :].squeeze(1),
                            lambda h: alo[:, bass.ds(blk + h, 1), :].squeeze(1), blk, first, last,
                            lambda h: pe.wait_ge(e_al.sem, f * FB + (blk + h) + 1))
            by_threes(pe, DOWN_CHUNKS, down)

        def ffn1_act(act, f, n0, width=lambda k: CHUNK):
            def gelu(i, slot):
                act.wait_ge(e_cv.sem, f * FB + i + 1)
                nc.scalar.activation(gel[:, slot, :], taps[:, slot, 0, :], ACT.Gelu_apprx_tanh).then_inc(e_gl.sem, 1)

            def high(i, slot):
                act.wait_ge(e_pr.sem, f * FB + i + 1)
                nc.scalar.activation(ahi[:, bass.ds(i, 1), :].squeeze(1), prod[:, slot, :], ACT.Copy).then_inc(e_ah.sem, 1)

            def step(j, turn):
                i = turn * RING + j
                static = isinstance(turn, int)
                if not (static and turn == 0 and j < 2):
                    high(i - 2, (j - 2) % RING)
                if not (static and turn == 0 and j < 1):
                    gelu(i - 1, (j - 1) % RING)
                split_high(act, n0.at(j + 2, turn))
                act.wait_ge(s_used, n0.count(j + 1) + turn * RING)
                slot = n0.at(j).slot
                for s in range(2):
                    b = i + s * FB
                    nc.scalar.activation(taps[:, j, s, :], lin[:, slot, s * T:(s + 1) * T], ACT.Identity,
                                         bias=fcol[:, 1, bass.ds(b + 44, 1)], scale=fcol[:, 1, bass.ds(b, 1)])\
                        .then_inc(e_c0.sem, 1) if s else \
                        nc.scalar.activation(taps[:, j, s, :], lin[:, slot, s * T:(s + 1) * T], ACT.Identity,
                                             bias=fcol[:, 1, bass.ds(b + 44, 1)], scale=fcol[:, 1, bass.ds(b, 1)])
            by_threes(act, UP_CHUNKS, step)
            high(FB - 2, (FB - 2) % RING)
            gelu(FB - 1, (FB - 1) % RING)
            high(FB - 1, (FB - 1) % RING)

        def ffn1_dve(dve, st, f, n0):
            def step(j, turn):
                i = turn * RING + j
                split_low(dve, n0.at(j + 2, turn))
                dve.wait_ge(e_c0.sem, f * FB + i + 1)
                slot = n0.at(j).slot
                for tap in (1, 0):
                    d = 2 - tap
                    for s in range(2):
                        ins = dve.scalar_tensor_tensor(
                            out=taps[:, j, s, d:T], in0=lin[:, slot, s * T:(s + 1) * T - d],
                            scalar=fcol[:, 0, bass.ds(i + (s * FB + 44 * tap), 1)], in1=taps[:, j, s, d:T],
                            op0=ALU.mult, op1=ALU.add)
                    if tap:
                        st(ins)
                    else:
                        ins.then_inc(e_cv.sem, 1)
            by_threes(dve, UP_CHUNKS, step, st, RING)

        def ffn1_pool(pool, f, n0):
            def product(i, slot):
                pool.wait_ge(e_gl.sem, f * FB + i + 1)
                pool.tensor_tensor(prod[:, slot, :], gel[:, slot, :], taps[:, slot, 1, :], ALU.mult).then_inc(e_pr.sem, 1)

            def low(i, slot):
                pool.wait_ge(e_ah.sem, f * FB + i + 1)
                pool.tensor_tensor(alo[:, bass.ds(i, 1), :].squeeze(1), prod[:, slot, :],
                                   ahi[:, bass.ds(i, 1), :].squeeze(1).bitcast(F32), ALU.subtract).then_inc(e_al.sem, 1)

            def step(j, turn):
                i = turn * RING + j
                split_low(pool, n0.at(j + 2, turn))
                if not (isinstance(turn, int) and turn == 0 and j < 2):
                    low(i - 2, (j - 2) % RING)
                if not (isinstance(turn, int) and turn == 0 and j < 1):
                    product(i - 1, (j - 1) % RING)
            by_threes(pool, UP_CHUNKS, step)
            low(FB - 2, (FB - 2) % RING)
            product(FB - 1, (FB - 1) % RING)
            low(FB - 1, (FB - 1) % RING)

        def ffn2_act(act, f, n0):
            def high(i, slot):
                act.wait_ge(e_cv.sem, f * FB + i + 1)
                nc.scalar.activation(ahi[:, bass.ds(i, 1), :].squeeze(1), prod[:, slot, :], ACT.Copy).then_inc(e_ah.sem, 1)

            def step(j, turn):
                i = turn * RING + j
                split_high(act, n0.at(j + 2, turn))
                if not (isinstance(turn, int) and turn == 0 and j == 0):
                    high(i - 1, (j - 1) % RING)
                act.wait_ge(s_used, n0.count(j + 1) + turn * RING)
                if not (isinstance(turn, int) and turn == 0):
                    act.wait_ge(e_al.sem, f * FB + i - 2)
                nc.scalar.activation(gel[:, j, :], lin[:, n0.at(j).slot, 0:T], ACT.Silu).then_inc(e_sg.sem, 1)
            by_threes(act, UP_CHUNKS, step)
            high(FB - 1, (FB - 1) % RING)

        def ffn2_dve(dve, f, n0):
            def step(j, turn):
                split_low(dve, n0.at(j + 2, turn))
                dve.wait_ge(e_sg.sem, (f - LAYERS) * FB + turn * RING + (j + 1))
                dve.tensor_tensor(prod[:, j, :], gel[:, j, :], lin[:, n0.at(j).slot, T:2 * T], ALU.mult).then_inc(e_cv.sem, 1)
            by_threes(dve, UP_CHUNKS, step)

        def ffn2_pool(pool, f, n0):
            def low(i, slot):
                pool.wait_ge(e_ah.sem, f * FB + i + 1)
                pool.tensor_tensor(alo[:, bass.ds(i, 1), :].squeeze(1), prod[:, slot, :],
                                   ahi[:, bass.ds(i, 1), :].squeeze(1).bitcast(F32), ALU.subtract).then_inc(e_al.sem, 1)

            def step(j, turn):
                i = turn * RING + j
                split_low(pool, n0.at(j + 2, turn))
                if not (isinstance(turn, int) and turn == 0 and j == 0):
                    low(i - 1, (j - 1) % RING)
            by_threes(pool, UP_CHUNKS, step)
            low(FB - 1, (FB - 1) % RING)

        def down_split(eng, n0, split, after=2):
            by_threes(eng, DOWN_CHUNKS, lambda j, turn: split(eng, n0.at(UP_CHUNKS + j + 2, turn))
                      if not (isinstance(turn, int) and 3 * turn + j + 2 >= DOWN_CHUNKS + after) else None)

        PRE_OF = lambda f: 2 * f + 1 if f < LAYERS else 2 * f

        def turn_in_pe(pe, x):
            for q in range(4):
                for k in (2 * q, 2 * q + 1):
                    for t in range(2):
                        o = (k % 2) * T + t * P
                        i = pe.transpose(acc[:, q, o:o + P], x(t)[:, k * P:(k + 1) * P], K["ident"])
                i.then_inc(e_xt.sem, 1)

        def turn_in_dve(dve, c, xt):
            for q in range(4):
                dve.wait_ge(e_xt.sem, e_xt.after(c, q + 1))
                dve.tensor_copy(xt[:, 2 * q:2 * q + 2, :], acc[:, q, :].rearrange("p (k t) -> p k t", k=2)).then_inc(e_xc.sem, 1)

        def cat_pe(pe, L, n, pos, first, last):
            pair = OUT1_ORDER[pos]
            pe.wait_ge(m_cal.sem, m_cal.after(L, pos + 1))
            rows_pe(pe, n, lambda h: hhi[:, 2 * pair + h, :], lambda h: hlo[:, 2 * pair + h, :], None, first, last,
                    lambda h: None)

        def heads(h):
            return slice(64 * (h % 2), 64 * (h % 2) + 64), h // 2

        ROUNDS = ((0, 0, "acc", 0), (1, 0, "acc", 1), (0, 1, "acc", 2), (1, 1, "lin", 0))

        def round_scores(r):
            branch, tb, where, b = ROUNDS[r]
            keys = (tb + 1) * P
            t = acc if where == "acc" else lin
            if tb == 0:
                return t[:, b, :].rearrange("p (h k) -> p h k", h=4)
            return t[:, b:b + 2, :].rearrange("p b (h k) -> p (b h) k", h=2)

        def mixer1_pe(pe, st, L, n0):
            if L:
                pe.wait_ge(e_prt.sem, e_prt.after(2 * L - 1))
            pe.wait_ge(s_par, L * N_PAR + N_PAR)
            pe.wait_ge(s_fpar, L * N_FPAR + N_FPAR)
            pe.transpose(misc[:, 0:R_ROWS], vrow[:], K["ident"][0:R_ROWS, 0:R_ROWS])
            pe.transpose(misc[:, 128:160], perow[:], K["ident"][0:32, 0:32])
            for j in range(2):
                i = pe.transpose(misc[:, 256 + 88 * j:256 + 88 * j + 88], frow[:, j, :], K["ident"][0:88, 0:88])
            i.then_inc(e_vt.sem, 1)
            pe.wait_ge(e_vc.sem, e_vc.after(L))
            pre_pe(pe, 2 * L)
            for j in range(MIX1_CHUNKS):
                if j >= RING:
                    pe.wait_ge(m_ev.sem, m_ev.after(L, j + 1 - RING))
                n = n0.at(j)
                width, offs = (140, (0, 12)) if j == 4 else (256, (0, P))
                cols_pe(pe, n, lin[:, n.slot, :], 2,
                        (lambda k: pe.wait_ge(e_h.sem, e_h.after(2 * L, k + 1))) if j == 0 else None, width, offs)
            pe.wait_ge(m_ev.sem, m_ev.after(L, 5))
            for j in range(2):
                mm(acc[:, 0, j * T:(j + 1) * T], K["rope_turn"], qT[:, j, :])
            for b in range(2):
                mm(acc[:, 1, b * T:(b + 1) * T], K["twice"][0:64, :], kvT[0:64, 1 + b, :])
                i = mm(acc[:, 2, b * T:(b + 1) * T], K["twice_turn"][0:64, :], kvT[0:64, 1 + b, :])
            i.then_inc(m_rope.sem, 1)
            for b in range(3):
                if b == 2:
                    pe.wait_ge(m_ev.sem, m_ev.after(L, 7))
                for t in range(2):
                    o = (2 * b + t) * P
                    dst = acc[:, 3, o:o + P] if b < 2 else lin[:, 0, t * P:(t + 1) * P]
                    i = pe.transpose(dst, kvT[:, 1 + b, t * P:(t + 1) * P], K["ident"])
            i.then_inc(m_tr.sem, 1)
            pe.wait_ge(m_ev.sem, m_ev.after(L, 8))
            for t in range(2):
                for b in range(2):
                    i = pe.transpose(lin[:, 2, t * T + b * P:t * T + (b + 1) * P], vT[:, b, t * P:(t + 1) * P], K["ident"])
            i.then_inc(m_vx.sem, 1)
            ada_pe(pe, L, 0, 8)
            def scores(r):
                branch, tb, _, _ = ROUNDS[r]
                s = round_scores(r)
                for h in (0, 2, 1, 3):
                    ps, hp = heads(h)
                    i = mm(s[:, h, :], qrot[ps, hp, tb * P:(tb + 1) * P], krot[ps, branch, 0:(tb + 1) * P])
                    if h == 2:
                        st(i)
                i.then_inc(m_sc.sem, 1)
            pe.wait_ge(m_qk.sem, m_qk.after(L))
            pe.wait_ge(m_cb.sem, m_cb.after(L))
            pe.wait_ge(s_parw, L * N_PARW + N_PARW)
            pe.wait_ge(m_vt.sem, m_vt.after(L))
            for h in range(2):
                for l in range(32):
                    q = slice(64 * h, 64 * h + 64)
                    i = mm(lin[q, 1, 0:N_CMP], cw1[q, l, :], cbuf[q, l, :], start=(l == 0), stop=(l == 31))
            i.then_inc(m_hid.sem, 1)
            scores(0)
            scores(1)
            pe.wait_ge(m_hg.sem, m_hg.after(L))
            st(mm(lin[:, 1, 16:16 + N_CMP], cw2[0:64, 0:P], hid[0:64, 0:N_CMP]))
            mm(lin[0:N_CMP, 1, 32:96], hid[64:128, 0:N_CMP], cw2[64:128, 128:192]).then_inc(m_kc.sem, 1)
            scores(2)
            pe.wait_ge(m_kcc.sem, m_kcc.after(L))
            scores(3)
            pe.wait_ge(m_vn.sem, m_vn.after(L))
            for odd in range(2):
                for t in range(2):
                    for h in (odd, 2 + odd):
                        ps, hp = heads(h)
                        o = (t * 4 + h) * 16
                        i = mm(lin[:, 2, o:o + N_CMP], qT[ps, hp, t * P:(t + 1) * P], kc[ps, 0:N_CMP])
                if not odd:
                    st(i)
            i.then_inc(m_cmp.sem, 1)
            ada_pe(pe, L, 8, 8)
            blk = 0
            for r in range(4):
                branch, tb, _, _ = ROUNDS[r]
                if r:
                    ada_pe(pe, L, 12 + 4 * r, 4)
                pe.wait_ge(m_pb.sem, m_pb.after(L, r + 1))
                for kb in range(tb + 1):
                    if blk >= 2:
                        pe.wait_ge(m_pc.sem, m_pc.after(L, blk - 1))
                    for h in range(HEADS1):
                        i = pe.transpose(acc[:, blk % 2, h * P:(h + 1) * P], prob[:, h, kb * P:(kb + 1) * P], K["ident"])
                    i.then_inc(m_pt.sem, 1)
                    blk += 1
            pe.wait_ge(m_pcr.sem, m_pcr.after(L))
            for t in range(2):
                pe.wait_ge(m_pc.sem, m_pc.after(L, 5 + t))
                for h in range(HEADS1):
                    i = pe.transpose(acc[0:N_CMP, t, h * P:(h + 1) * P], probc[:, t * 4 + h, 0:N_CMP], K["ident"])
                i.then_inc(m_pt.sem, 1)
            pe.wait_ge(m_pc.sem, m_pc.after(L, 8))
            for t in range(2):
                for h in range(HEADS1):
                    ps, hp = heads(h)
                    dst = acc[ps, 2, hp * T + t * P:hp * T + (t + 1) * P]
                    mm(dst, vc[:], pcT[0:N_CMP, t * 4 + h, :], start=True, stop=False)
                    for branch in range(2):
                        for kb in range(t + 1):
                            b = BLK[(branch, kb, t)]
                            i = mm(dst, vtok[:, 2 * branch + kb, :], pT[:, b, h, :], start=False,
                                   stop=(branch == 1 and kb == t))
            i.then_inc(m_o.sem, 1)
            pe.wait_ge(m_cmx.sem, m_cmx.after(L))
            for g in range(4):
                i = pe.transpose(lin[:, 2, g * P:(g + 1) * P], wsp[:, g, :], K["ident"])
            i.then_inc(m_vx.sem, 1)
            pe.wait_ge(m_ws.sem, m_ws.after(L))
            pe.wait_ge(m_vw.sem, m_vw.after(L))
            for g in range(4):
                for t in range(2):
                    i = mm(acc[64 * (g % 2):64 * (g % 2) + 64, 3, (g // 2) * T + t * P:(g // 2) * T + (t + 1) * P],
                           vn[:, t, 64 * g:64 * g + 64], wspT[:, g, :])
            i.then_inc(m_f.sem, 1)
            ada_pe(pe, L, 28, 8)
            pe.wait_ge(m_pl.sem, m_pl.after(L))
            for b in range(2):
                i = mm(lin[:, 0, b * T:(b + 1) * T], pw[:, b, :], pooled[:, b, :])
            i.then_inc(m_pm.sem, 1)
            pe.wait_ge(m_csg.sem, m_csg.after(L))
            pe.wait_ge(m_cns.sem, m_cns.after(L))
            for p in range(3):
                cat_pe(pe, L, n0.at(MIX1_CHUNKS + p), p, p == 0, False)
            pe.wait_ge(m_cy.sem, m_cy.after(L))
            for b in range(2):
                i = mm(lin[:, 1, 0:T], K["ones"], convy[:, b, :], start=(b == 0), stop=(b == 1))
            i.then_inc(m_cs.sem, 1)
            pe.wait_ge(m_cq.sem, m_cq.after(L))
            for b in range(2):
                i = mm(lin[:, 1, T:2 * T], K["ones"], sig[:, b, :], start=(b == 0), stop=(b == 1))
            i.then_inc(m_cs.sem, 1)
            cat_pe(pe, L, n0.at(MIX1_CHUNKS + 3), 3, False, True)

        BLK = {(0, 0, 0): 0, (1, 0, 0): 1, (0, 0, 1): 2, (0, 1, 1): 3, (1, 0, 1): 4, (1, 1, 1): 5}
        m_cmp = event("compressed_scores", 1)
        m_cmx = event("compressed_maxima", 1)
        m_cex = event("compressed_exponentials", 1)
        m_pcr = event("compressed_probabilities", 1)

        def mixer1_act(act, st, L, n0):
            for j in range(MIX1_CHUNKS):
                split_high(act, n0.at(j + 2), 1120 if j + 2 == 4 else CHUNK)
                act.wait_ge(s_used, n0.count(j + 1))
                src = lin[:, n0.at(j).slot, :].rearrange("p (b t) -> p b t", b=2)
                dst, fn = ((aT[:], ACT.Copy), (sig[:], ACT.Sigmoid), (qT[:], ACT.Copy), (kvT[:, 0:2, :], ACT.Copy),
                           (kvT[:, 2:4, :], ACT.Copy), (uT[:], ACT.Gelu_apprx_tanh), (vT[:], ACT.Gelu_apprx_tanh),
                           (zpad[:, :, 16:16 + T], ACT.Copy))[j]
                nc.scalar.activation(dst, src, fn).then_inc(m_ev.sem, 1)
            split_high(act, n0.at(MIX1_CHUNKS + 2))
            act.wait_ge(m_tr.sem, m_tr.after(L))
            nc.scalar.activation(vtok[:], acc[:, 3, :].rearrange("p (b c) -> p b c", b=4)[:, :, 64:128], ACT.Copy)
            nc.scalar.activation(gates[:], lin[:, 0, 0:2 * P].rearrange("p (t c) -> p t c", t=2)[:, :, 116:128],
                                 ACT.Sigmoid).then_inc(m_vt.sem, 1)
            act.wait_ge(m_hid.sem, m_hid.after(L))
            nc.scalar.activation(hid[:, 0:N_CMP], lin[:, 1, 0:N_CMP], ACT.Gelu_apprx_tanh).then_inc(m_hg.sem, 1)
            act.wait_ge(m_kc.sem, m_kc.after(L))
            nc.scalar.activation(kc[:, 0:N_CMP], lin[:, 1, 16:16 + N_CMP], ACT.Copy)
            nc.scalar.activation(vc[:], lin[0:N_CMP, 1, 32:96], ACT.Copy).then_inc(m_kcc.sem, 1)
            act.wait_ge(m_bn.sem, m_bn.after(L))
            nc.scalar.activation(srt[:, 0:2], mv[:, :, 1], ACT.Sqrt, bias=K["eps5"]).then_inc(m_br.sem, 1)

            blk = 0
            def copies(count):
                nonlocal blk
                for _ in range(count):
                    act.wait_ge(m_pt.sem, m_pt.after(L, blk + 1))
                    nc.scalar.activation(pT[:, blk, :, :], acc[:, blk % 2, :].rearrange("p (h k) -> p h k", h=4),
                                         ACT.Copy).then_inc(m_pc.sem, 1)
                    blk += 1
            for r in range(4):
                tb = ROUNDS[r][1]
                keys = (tb + 1) * P
                act.wait_ge(m_mx.sem, m_mx.after(L, r + 1))
                if r:
                    act.wait_ge(m_pb.sem, m_pb.after(L, r))
                for h in range(HEADS1):
                    i = nc.scalar.activation(prob[:, h, 0:keys], sc[:, h, 0:keys], ACT.Exp, bias=mx[:, h:h + 1],
                                             accum_out=sm[:, h:h + 1])
                i.then_inc(m_ex.sem, 1)
                copies(tb + 1)
            act.wait_ge(m_cmx.sem, m_cmx.after(L))
            nc.scalar.activation(probc[:, :, 0:N_CMP], scc[:, :, 0:N_CMP], ACT.Exp).then_inc(m_cex.sem, 1)
            for t in range(2):
                act.wait_ge(m_pt.sem, m_pt.after(L, 7 + t))
                nc.scalar.activation(pcT[0:N_CMP, 4 * t:4 * t + 4, :], acc[0:N_CMP, t, :].rearrange("p (h k) -> p h k", h=4),
                                     ACT.Copy).then_inc(m_pc.sem, 1)
            act.wait_ge(m_pm.sem, m_pm.after(L))
            for b in range(2):
                i = nc.scalar.activation(work[:, 6 + b, :], lin[:, 0, b * T:(b + 1) * T], ACT.Copy,
                                         scale=vcol[:, R_PSC + b:R_PSC + b + 1])
            i.then_inc(m_cpool.sem, 1)
            for pos in range(3):
                done = (m_csg, m_cpool, m_cns)[pos]
                act.wait_ge(done.sem, done.after(L))
                p = OUT1_ORDER[pos]
                nc.scalar.activation(hhi[:, 2 * p:2 * p + 2, :], work[:, 2 * p:2 * p + 2, :], ACT.Copy).then_inc(m_cah.sem, 1)
            split_high(act, n0.at(MIX1_CHUNKS + 3))
            act.wait_ge(m_cc.sem, m_cc.after(L))
            nc.scalar.activation(sig[:], convy[:], ACT.Square).then_inc(m_cq.sem, 1)
            act.wait_ge(m_cs.sem, m_cs.after(L, 2))
            nc.scalar.activation(root[:], lin[:, 1, T:2 * T], ACT.Sqrt, bias=K["eps5"], scale=1.0 / T).then_inc(m_cr.sem, 1)
            act.wait_ge(m_cn.sem, m_cn.after(L))
            for b in range(2):
                i = nc.scalar.activation(work[:, b, :], convy[:, b, :], ACT.Silu, bias=vcol[:, R_CLB + b:R_CLB + b + 1],
                                         scale=vcol[:, R_CLG + b:R_CLG + b + 1])
            st(i)
            nc.scalar.activation(hhi[:, 0:2, :], work[:, 0:2, :], ACT.Copy).then_inc(m_cah.sem, 1)
            for j in (4, 5):
                split_high(act, n0.at(MIX1_CHUNKS + j))

        m_cpool = event("pool_scaled", 1)

        def mixer1_dve(dve, st, L, n0):
            def low(j):
                split_low(dve, n0.at(j), 1120 if j == 4 else CHUNK)
            low(2)
            low(3)
            dve.wait_ge(m_ev.sem, m_ev.after(L, 2))
            dve.tensor_tensor(glu[:, :, PAD:PAD + T], aT[:], sig[:], ALU.mult).then_inc(m_glu.sem, 1)
            dve.wait_ge(m_glu.sem, m_glu.after(L))
            def conv(t0, t1):
                for k in range(t0, t1):
                    for b in range(2):
                        w = vcol[:, R_DW + 2 * k + b:R_DW + 2 * k + b + 1]
                        if k == 0:
                            i = dve.tensor_scalar(convy[:, b, :], glu[:, b, 0:T], w, vcol[:, R_DWB + b:R_DWB + b + 1],
                                                  ALU.mult, ALU.add)
                        else:
                            i = dve.scalar_tensor_tensor(out=convy[:, b, :], in0=glu[:, b, k:k + T], scalar=w,
                                                         in1=convy[:, b, :], op0=ALU.mult, op1=ALU.add)
                    st(i)
            low(4)
            conv(0, 5)
            low(5)
            conv(5, 9)
            low(6)
            dve.wait_ge(m_ev.sem, m_ev.after(L, 4))
            src = kvT[:, 0, :].rearrange("p (n l) -> p l n", l=16)
            for half in range(2):
                i = dve.tensor_tensor(cbuf[:, 16 * half:16 * half + 16, :], src[:, :, half:half + N_CMP],
                                      pecol[:, 16 * half:16 * half + 16].unsqueeze(2).broadcast_to([P, 16, N_CMP]), ALU.add)
            i.then_inc(m_cb.sem, 1)
            conv(9, 12)
            low(7)
            low(8)
            low(9)
            dve.wait_ge(m_rope.sem, m_rope.after(L))
            cos = K["cos"].unsqueeze(1).broadcast_to([P, 2, T])
            sin = K["sin"].unsqueeze(1).broadcast_to([P, 2, T])
            bank = lambda b: acc[:, b, :].rearrange("p (j t) -> p j t", j=2)
            dve.scalar_tensor_tensor(out=qrot[:], in0=qT[:], scalar=0.125, in1=cos, op0=ALU.mult, op1=ALU.mult)
            st(dve.scalar_tensor_tensor(out=rt[:], in0=bank(0), scalar=0.125, in1=sin, op0=ALU.mult, op1=ALU.mult))
            dve.tensor_tensor(krot[:], bank(1), cos, ALU.mult)
            st(dve.tensor_tensor(qrot[:], qrot[:], rt[:], ALU.add))
            st(dve.tensor_tensor(rt[:], bank(2), sin, ALU.mult))
            dve.tensor_tensor(krot[:], krot[:], rt[:], ALU.add).then_inc(m_qk.sem, 1)
            dve.wait_ge(m_vx.sem, m_vx.after(L, 1))
            for t in range(2):
                i = dve.bn_stats(bns[:, t, :], lin[:, 2, t * T:(t + 1) * T])
            st(i)
            for t in range(2):
                i = dve.bn_aggr(mv[:, t, :], bns[:, t, :])
            i.then_inc(m_bn.sem, 1)
            low(10)
            for r in range(4):
                branch, tb, _, _ = ROUNDS[r]
                keys = (tb + 1) * P
                dve.wait_ge(m_sc.sem, m_sc.after(L, r + 1))
                if r:
                    dve.wait_ge(m_pb.sem, m_pb.after(L, r))
                s = round_scores(r)
                bar = K["bar_le"].unsqueeze(1).broadcast_to([P, 4, P])
                if tb:
                    dve.tensor_copy(sc[:, :, 0:P], s[:, :, 0:P])
                st(dve.tensor_tensor(sc[:, :, tb * P:keys], s[:, :, tb * P:keys], bar, ALU.add))
                st(dve.tensor_reduce(mx[:, 4:8], sc[:, :, 0:keys], AX_X, ALU.max))
                dve.tensor_scalar(mx[:, 0:4], mx[:, 4:8], -1.0, None, ALU.mult).then_inc(m_mx.sem, 1)
                if r == 0:
                    dve.wait_ge(m_br.sem, m_br.after(L))
                    st(dve.reciprocal(srt[:, 2:4], srt[:, 0:2]))
                    for t in range(2):
                        i = dve.tensor_scalar(vn[:, t, :], lin[:, 2, t * T:(t + 1) * T], mv[:, t, 0:1], srt[:, 2 + t:3 + t],
                                              ALU.subtract, ALU.mult)
                    i.then_inc(m_vn.sem, 1)
                dve.wait_ge(m_ex.sem, m_ex.after(L, r + 1))
                st(dve.reciprocal(gs[:, 0:4], sm[:, 0:4]))
                g = gates[:, tb, :].rearrange("p (h b) -> p h b", b=3)[:, :, 1 + branch]
                st(dve.tensor_tensor(gs[:, 4:8], gs[:, 0:4], g, ALU.mult))
                dve.tensor_tensor(prob[:, :, 0:keys], prob[:, :, 0:keys],
                                  gs[:, 4:8].unsqueeze(2).broadcast_to([P, 4, keys]), ALU.mult).then_inc(m_pb.sem, 1)
                conv(12 + 2 * r, 14 + 2 * r)
            dve.wait_ge(m_cmp.sem, m_cmp.after(L))
            c8 = lin[:, 2, 0:P].rearrange("p (r k) -> p r k", r=8)[:, :, 0:N_CMP]
            bar = K["cmp_bar"].rearrange("p (t k) -> p t k", t=2)[:, :, 0:N_CMP]
            for t in range(2):
                i = dve.scalar_tensor_tensor(out=scc[:, 4 * t:4 * t + 4, 0:N_CMP], in0=c8[:, 4 * t:4 * t + 4, :], scalar=0.125,
                                             in1=bar[:, t:t + 1, :].broadcast_to([P, 4, N_CMP]), op0=ALU.mult, op1=ALU.add)
            st(i)
            st(dve.tensor_reduce(mx[:], scc[:, :, 0:N_CMP], AX_X, ALU.max))
            dve.tensor_tensor(scc[:, :, 0:N_CMP], scc[:, :, 0:N_CMP], mx[:].unsqueeze(2).broadcast_to([P, 8, N_CMP]),
                              ALU.subtract).then_inc(m_cmx.sem, 1)
            dve.wait_ge(m_cex.sem, m_cex.after(L))
            st(dve.tensor_reduce(sm[:], probc[:, :, 0:N_CMP], AX_X, ALU.add))
            st(dve.reciprocal(gs[:], sm[:]))
            g = gates[:].rearrange("p t (h b) -> p (t h) b", b=3)[:, :, 0]
            st(dve.tensor_tensor(gs[:], gs[:], g, ALU.mult))
            st(dve.tensor_tensor(probc[:, :, 0:N_CMP], probc[:, :, 0:N_CMP],
                                 gs[:].unsqueeze(2).broadcast_to([P, 8, N_CMP]), ALU.mult))
            seen = K["cmp_seen"].rearrange("p (t k) -> p t k", t=2)[:, :, 0:N_CMP]
            for t in range(2):
                i = dve.tensor_tensor(probc[:, 4 * t:4 * t + 4, 0:N_CMP], probc[:, 4 * t:4 * t + 4, 0:N_CMP],
                                      seen[:, t:t + 1, :].broadcast_to([P, 4, N_CMP]), ALU.mult)
            i.then_inc(m_pcr.sem, 1)
            dve.wait_ge(m_vx.sem, m_vx.after(L, 2))
            dve.tensor_tensor(wspT[:], lin[:, 2, :].rearrange("p (g t) -> p g t", g=4),
                              K["col_ge"].unsqueeze(1).broadcast_to([P, 4, P]), ALU.mult).then_inc(m_ws.sem, 1)
            dve.wait_ge(m_f.sem, m_f.after(L))
            f = acc[:, 3, :].rearrange("p (b t s) -> p b t s", b=2, t=2)
            for b in range(2):
                i = dve.tensor_tensor(work[:, 4 + b, :].rearrange("p (t s) -> p t s", t=2), f[:, b],
                                      bsp[:, b:b + 1, :].broadcast_to([P, 2, P]), ALU.add)
            st(i)
            dve.tensor_tensor(work[:, 4:6, :], work[:, 4:6, :], uT[:], ALU.mult).then_inc(m_csg.sem, 1)
            dve.wait_ge(m_o.sem, m_o.after(L))
            dve.tensor_copy(work[:, 2:4, :], acc[:, 2, :].rearrange("p (b t) -> p b t", b=2)).then_inc(m_cns.sem, 1)
            for pos in range(3):
                p = OUT1_ORDER[pos]
                dve.wait_ge(m_cah.sem, m_cah.after(L, pos + 1))
                dve.tensor_tensor(hlo[:, 2 * p:2 * p + 2, :], work[:, 2 * p:2 * p + 2, :],
                                  hhi[:, 2 * p:2 * p + 2, :].bitcast(F32), ALU.subtract).then_inc(m_cal.sem, 1)
            conv(20, 31)
            dve.sem_inc(m_cy.sem, 1)
            low(11)
            dve.wait_ge(m_cs.sem, m_cs.after(L, 1))
            dve.scalar_tensor_tensor(out=convy[:], in0=lin[:, 1:2, 0:T].broadcast_to([P, 2, T]), scalar=-1.0 / T,
                                     in1=convy[:], op0=ALU.mult, op1=ALU.add).then_inc(m_cc.sem, 1)
            dve.wait_ge(m_cr.sem, m_cr.after(L))
            st(dve.reciprocal(rstd[:], root[:]))
            dve.tensor_tensor(convy[:], convy[:], rstd[:].unsqueeze(1).broadcast_to([P, 2, T]), ALU.mult).then_inc(m_cn.sem, 1)
            dve.wait_ge(m_cah.sem, m_cah.after(L, 4))
            dve.tensor_tensor(hlo[:, 0:2, :], work[:, 0:2, :], hhi[:, 0:2, :].bitcast(F32), ALU.subtract).then_inc(m_cal.sem, 1)
            low(12)
            low(13)

        def mixer1_pool(pool, st, L, n0):
            for j in range(2, MIX1_CHUNKS + 3):
                split_low(pool, n0.at(j), 1120 if j == 4 else CHUNK)
                if j == MIX1_CHUNKS + 2:
                    break
            pool.wait_ge(m_ev.sem, m_ev.after(L, 8))
            W = 16 + T
            for b in range(2):
                src = zpad[:, b, :]
                for s in range(2 * b + 2):
                    d = 1 << s
                    st(pool.tensor_tensor(psum2[:, s, d:W], src[:, d:W], src[:, 0:W - d], ALU.add))
                    src = psum2[:, s, :]
                for h in range(2):
                    q = slice(64 * h, 64 * h + 64)
                    i = pool.tensor_tensor(pooled[q, b, :], psum2[q, 2 * b + h, 16:W],
                                           K["inv_count"][q, b * T:(b + 1) * T], ALU.mult)
                st(i)
                i = pool.tensor_tensor(pooled[:, b, :], pooled[:, b, :], zpad[:, b, 16:W], ALU.subtract)
            i.then_inc(m_pl.sem, 1)
            pool.wait_ge(m_vn.sem, m_vn.after(L))
            pool.wait_ge(s_parw, L * N_PARW + N_PARW)
            st(pool.tensor_tensor(vn[:], vn[:], sgln[:, 0:1, :].broadcast_to([P, 2, T]), ALU.mult))
            pool.tensor_tensor(vn[:], vn[:], sgln[:, 1:2, :].broadcast_to([P, 2, T]), ALU.add).then_inc(m_vw.sem, 1)
            for j in range(3, 6):
                split_low(pool, n0.at(MIX1_CHUNKS + j))


        def ada_load(sp, t):
            if t >= 2:
                sp.wait_ge(e_ad.sem, t - 1)
            sp.dma_start(ada[t % 2][:], a["ada_w_2"][0].rearrange("(k p) c -> p k c", p=P)[:, :, t * P:(t + 1) * P])\
                .then_inc(s_ada[t % 2], 16)

        def ada_pe(pe, L, first, count):
            for t in range(first, first + count):
                pe.wait_ge(s_ada[t % 2], (L * ADA_LAYER + t) // 2 * 16 + 16)
                for k in range(KD):
                    i = mm(misc[:, T + 2 * t:T + 2 * t + 2], ada[t % 2][:, k, :], csil[:, :, k], start=(k == 0), stop=(k == KD - 1))
                i.then_inc(e_ad.sem, 1)

        N_P2 = 18 * 16

        def load_second_params(sp):
            n = 0

            def go(dst, src):
                nonlocal n
                n += 16
                sp.dma_start(dst, src).then_inc(s_p2, 16)
            rows = lambda name: a[name].rearrange("o (r p) -> (o r) p", p=P)
            go(tab2[:], a["tables_2"])
            for j, name in enumerate(("ffn1_norm_pre_2", "ffn1_norm_post_2", "mix_norm_pre_2", "mix_norm_post_2",
                                      "ffn2_norm_pre_2", "ffn2_norm_post_2")):
                go(xrow[8 * j:8 * j + 8, 0, :], rows(name))
            go(xrow[V_SSDN:V_SSDN + 6, 0, :], rows("ssd_norm_2"))
            go(xrow[V_ADAB:V_ADAB + ADA_BLOCKS, 0, :], rows("ada_b_2"))
            go(xrow[V_CW:V_CW + 3 * CONV_BLOCKS, 1, :], a["conv_w_2"][0].rearrange("k (b p) -> (k b) p", p=P))
            go(xrow[V_CB:V_CB + CONV_BLOCKS, 1, :], rows("conv_b_2"))
            go(drow[:, 0, :], a["dt_bias_2"].rearrange("o d h -> o (d h)").broadcast_to([P, 24]))
            go(drow[:, 1, :], a["a_log_2"].rearrange("o d h -> o (d h)").broadcast_to([P, 24]))
            go(skip_all[:], a["d_skip_2"].broadcast_to([P, SSD_HEADS]))
            for h in range(4):
                q = 64 * (h % 2)
                go(fw[q:q + 64, h // 2, q:q + 64], a["fourier_w_2"][0, h])
            assert n == N_P2

        def second_start_pe(pe):
            pe.wait_ge(s_p2, N_P2)
            pe.wait_ge(e_prt.sem, e_prt.after(2 * LAYERS - 1))
            pe.transpose(misc[:, 0:V_ROWS], xrow[0:V_ROWS, 0, :], K["ident"][0:V_ROWS, 0:V_ROWS])
            pe.transpose(misc[:, P:P + V_ROWS2], xrow[0:V_ROWS2, 1, :], K["ident"][0:V_ROWS2, 0:V_ROWS2]).then_inc(t_vt.sem, 1)

        def second_start_dve(dve, st):
            dve.wait_ge(t_vt.sem, 1)
            dve.tensor_copy(xcol[:, 0, 0:V_ROWS], misc[:, 0:V_ROWS])
            dve.tensor_copy(xcol[:, 1, 0:V_ROWS2], misc[:, P:P + V_ROWS2]).then_inc(t_vc.sem, 1)
            dve.wait_ge(t_vc.sem, 1)
            st(dve.tensor_tensor(mod[:], mod[:], xcol[:, 0, V_ADAB:V_ADAB + ADA_BLOCKS].unsqueeze(2).broadcast_to([P, ADA_BLOCKS, 2]), ALU.add))
            for g, (who, stage) in enumerate(((1, 0), (1, 1), (0, 0), (0, 1), (0, 2))):
                dve.scalar_tensor_tensor(out=gain2[:, g, :], in0=mod[:, (3 * stage + 1) * KD:(3 * stage + 2) * KD, who], scalar=1.0,
                                         in1=xcol[:, 0, 16 * stage:16 * stage + 8], op0=ALU.add, op1=ALU.mult)
            for g, (who, stage) in enumerate(((1, 0), (0, 0), (0, 1), (0, 2))):
                i = dve.scalar_tensor_tensor(out=gain2[:, 5 + g, :], in0=mod[:, (3 * stage + 2) * KD:(3 * stage + 3) * KD, who],
                                             scalar=1.0 if stage == 1 else 0.5, in1=xcol[:, 0, 16 * stage + 8:16 * stage + 16],
                                             op0=ALU.mult, op1=ALU.mult)
            for h in range(2):
                q = 64 * h
                i = dve.tensor_copy(dsk[q:q + 64, :], skip_all[q:q + 64, :].rearrange("p (q h) -> p h q", h=2)[:, h])
            i.then_inc(t_gn.sem, 1)
            dve.wait_ge(t_gn.sem, 1)

        gain = lambda g: (lambda k: gain2[:, g, k:k + 1])
        shift = lambda who, stage: (lambda k: mod[:, 3 * stage * KD + k, who:who + 1])

        def chunk_reads(js):
            counts, reads = {p_ea: 0, p_ed: 0}, []
            for j in js:
                s_ = p_ed if 4 <= j < 11 else p_ea
                counts[s_] += 1
                reads.append((s_, counts[s_]))
            return reads, counts[p_ea], counts[p_ed]

        CTX_JS, X_JS = (6, 7, 8, 9, 10, 11), tuple(range(12))
        _, CTX_NA, CTX_ND = chunk_reads(CTX_JS)
        _, X_NA, X_ND = chunk_reads(X_JS)

        def proj_load(sp, n0, js):
            for idx, j in enumerate(js):
                load_cols(sp, n0.at(idx), a["w_in_2"][0], 256 * j if j < 11 else MIX2_COLS - P, 256 if j < 11 else P)

        def proj_width(js, idx):
            return KD * P if idx < len(js) and js[idx] == 11 else CHUNK

        def proj_pe(pe, n0, js, base_a, base_d, pre):
            reads = chunk_reads(js)[0]
            for idx, j in enumerate(js):
                if idx >= RING:
                    sem_, cnt = reads[idx - RING]
                    pe.wait_ge(sem_, cnt + (base_a if sem_ is p_ea else base_d))
                n = n0.at(idx)
                cols_pe(pe, n, lin[:, n.slot, :], 2 if j < 11 else 1,
                        (lambda k: pe.wait_ge(e_h.sem, e_h.after(pre, k + 1))) if idx == 0 else None,
                        256 if j < 11 else P)

        def proj_act(act, n0, js, base_d, cv_, first, dt_):
            conv_js = [j for j in js if 4 <= j < 11]

            def silu(q):
                act.wait_ge(p_ed, base_d + q + 1)
                blk = 2 * (conv_js[q] - 4) - first
                nc.scalar.activation(cv_[:, blk:blk + 2, :], cv_[:, blk:blk + 2, :], ACT.Silu).then_inc(p_si, 1)
            q = 0
            for idx, j in enumerate(js):
                split_high(act, n0.at(idx + 2), proj_width(js, idx + 2))
                act.wait_ge(s_used, n0.count(idx + 1))
                ps = lin[:, n0.at(idx).slot, :].rearrange("p (b t) -> p b t", b=2)
                if 4 <= j < 11:
                    for b in range(2):
                        blk = 2 * (j - 4) + b
                        i = nc.scalar.activation(cv_[:, blk - first, :], ps[:, b, :], ACT.Identity,
                                                 bias=xcol[:, 1, V_CB + blk:V_CB + blk + 1],
                                                 scale=xcol[:, 1, CONV_BLOCKS + blk:CONV_BLOCKS + blk + 1])
                    i.then_inc(p_c0, 1)
                    if q:
                        silu(q - 1)
                    q += 1
                elif j == 11:
                    nc.scalar.activation(dt_[:], ps[:, 0, :], ACT.Copy).then_inc(p_ea, 1)
                elif j == 0:
                    nc.scalar.activation(uf[:], ps, ACT.Copy).then_inc(p_ea, 1)
                else:
                    nc.scalar.activation(zs[:, 2 * j - 2:2 * j, :], ps, ACT.Silu).then_inc(p_ea, 1)
            silu(q - 1)

        def proj_dve(dve, st, n0, js, base_d, cv_, first):
            q = 0
            for idx, j in enumerate(js):
                split_low(dve, n0.at(idx + 2), proj_width(js, idx + 2))
                if not 4 <= j < 11:
                    continue
                q += 1
                dve.wait_ge(p_c0, base_d + q)
                ps = lin[:, n0.at(idx).slot, :].rearrange("p (b t) -> p b t", b=2)
                for tap in (0, 2):
                    for b in range(2):
                        blk = 2 * (j - 4) + b
                        w = xcol[:, 1, tap * CONV_BLOCKS + blk:tap * CONV_BLOCKS + blk + 1]
                        o, i_ = (slice(1, T), slice(0, T - 1)) if tap == 0 else (slice(0, T - 1), slice(1, T))
                        i = dve.scalar_tensor_tensor(out=cv_[:, blk - first, o], in0=ps[:, b, i_], scalar=w,
                                                     in1=cv_[:, blk - first, o], op0=ALU.mult, op1=ALU.add)
                    if tap == 0:
                        st(i)
                i.then_inc(p_ed, 1)

        def proj_pool(pool, n0, js):
            for idx in range(len(js)):
                split_low(pool, n0.at(idx + 2), proj_width(js, idx + 2))

        X_, M_, E_, Z_, Q_, DT_, DA_, CS_ = range(8)

        def steps_pe(pe, c, dt_, copied):
            pe.wait_ge(p_ea, copied)
            for t in range(2):
                i = pe.transpose(misc[:, t * P:(t + 1) * P], dt_[:, t * P:(t + 1) * P], K["ident"])
            i.then_inc(d_tr.sem, 1)
            pe.wait_ge(d_dt.sem, d_dt.after(c))
            for t in range(2):
                for d in range(2):
                    own = (("col_lt", "col_gt"), ("col_ge", "col_le"))[c][d]
                    earlier = (c == 1) == (d == 0)
                    other = 1 - t if (t == 1) == earlier else None
                    dst = misc[:, T + 24 * t + 12 * d:T + 24 * t + 12 * d + 12]
                    i = mm(dst, K[own], small[:, DA_, t, 12 * d:12 * d + 12], start=True, stop=other is None)
                    if other is not None:
                        i = mm(dst, K["ones"], small[:, DA_, other, 12 * d:12 * d + 12], start=False, stop=True)
            i.then_inc(d_cs.sem, 1)

        def steps_act(act, c):
            if c == 0:
                nc.scalar.activation(drow[:, 2, :], drow[:, 1, :], ACT.Exp).then_inc(d_a.sem, 1)
            act.wait_ge(d_x.sem, d_x.after(c))
            nc.scalar.activation(small[:, E_, :, :], small[:, E_, :, :], ACT.Exp, scale=-1.0).then_inc(d_e.sem, 1)

        def steps_dve(dve, st, c):
            v = lambda j: small[:, j, :, :]
            dve.wait_ge(d_tr.sem, d_tr.after(c))
            ps = misc[:, 0:2 * P].rearrange("p (t c) -> p t c", t=2)[:, :, 104:128]
            st(dve.tensor_tensor(v(X_), ps, drow[:, 0:1, :].broadcast_to([P, 2, 24]), ALU.add))
            dve.tensor_scalar(v(M_), v(X_), 0.0, None, ALU.max)
            st(dve.tensor_scalar(v(Z_), v(X_), -1.0, None, ALU.mult))
            dve.tensor_tensor(v(E_), v(X_), v(Z_), ALU.max).then_inc(d_x.sem, 1)
            dve.wait_ge(d_e.sem, d_e.after(c))
            st(dve.tensor_scalar(v(Z_), v(E_), 2.0, None, ALU.add))
            st(dve.reciprocal(v(Q_), v(Z_)))
            st(dve.tensor_tensor(v(Z_), v(Q_), v(E_), ALU.mult))
            st(dve.tensor_tensor(v(Q_), v(Z_), v(Z_), ALU.mult))
            st(dve.tensor_scalar(v(E_), v(Q_), 1.0 / 17, None, ALU.mult))
            for k in range(7, 0, -1):
                st(dve.scalar_tensor_tensor(out=v(E_), in0=v(E_), scalar=1.0 / (2 * k + 1), in1=v(Q_), op0=ALU.add, op1=ALU.mult))
            st(dve.scalar_tensor_tensor(out=v(E_), in0=v(E_), scalar=1.0, in1=v(Z_), op0=ALU.add, op1=ALU.mult))
            st(dve.scalar_tensor_tensor(out=v(DT_), in0=v(E_), scalar=2.0, in1=v(M_), op0=ALU.mult, op1=ALU.add))
            dve.wait_ge(d_a.sem, 1)
            dve.scalar_tensor_tensor(out=v(DA_), in0=v(DT_), scalar=-1.0, in1=drow[:, 2:3, :].broadcast_to([P, 2, 24]),
                                     op0=ALU.mult, op1=ALU.mult).then_inc(d_dt.sem, 1)
            dve.wait_ge(d_cs.sem, d_cs.after(c))
            dve.tensor_copy(v(CS_), misc[:, T:T + 48].rearrange("p (t c) -> p t c", t=2)).then_inc(d_cc.sem, 1)
            dve.wait_ge(d_cc.sem, d_cc.after(c))

        def x_turned(q0, q1):
            src = acc[:, 2 + q0 // 4] if q0 < 8 else lin[:, 0]
            return src[:, (q0 % 4) * P:(q0 % 4 + q1 - q0) * P]

        def ctx_state_pe(pe):
            pe.wait_ge(p_si, CTX_ND)
            for t in range(2):
                for b in range(4):
                    i = pe.transpose(acc[:, t, b * P:(b + 1) * P], ctx_cv[:, 6 + b, t * P:(t + 1) * P], K["ident"])
            i.then_inc(c_bt.sem, 1)
            for t in range(2):
                for b in range(6):
                    q = 6 * t + b
                    i = pe.transpose(x_turned(q, q + 1), ctx_cv[:, b, t * P:(t + 1) * P], K["ident"])
            i.then_inc(c_xt.sem, 1)
            pe.wait_ge(c_bc.sem, 1)
            pe.wait_ge(c_xw.sem, 1)
            for g in range(GROUPS):
                for d in range(2):
                    for t in range(2):
                        i = mm(acc[:, g, GW * d:GW * d + GW], btok[:, t, g * P:(g + 1) * P], xw[:, t, d, g * GW:(g + 1) * GW],
                               start=(t == 0), stop=(t == 1))
            i.then_inc(c_h.sem, 1)

        def ctx_state_act(act):
            act.wait_ge(d_cc.sem, 1)
            nc.scalar.activation(small[:, CS_, :, :], small[:, CS_, :, :], ACT.Exp).then_inc(c_w.sem, 1)
            act.wait_ge(c_bt.sem, 1)
            nc.scalar.activation(btok[:], acc[:, 0:2, :], ACT.Copy).then_inc(c_bc.sem, 1)
            act.wait_ge(c_h.sem, 1)
            nc.scalar.activation(h0, acc[:, :, 0:2 * GW].rearrange("p g (d c) -> p g d c", d=2), ACT.Copy).then_inc(c_hc.sem, 1)

        def ctx_state_dve(dve, st):
            dve.wait_ge(c_w.sem, 1)
            st(dve.tensor_tensor(small[:, Q_, :, :], small[:, CS_, :, :], small[:, DT_, :, :], ALU.mult))
            dve.wait_ge(c_xt.sem, 1)
            for t in range(2):
                for d in range(2):
                    w = small[:, Q_, t, 12 * d:12 * d + 12].unsqueeze(2)
                    q0 = 6 * t
                    while q0 < 6 * t + 6:
                        q1 = min(6 * t + 6, (q0 // 4 + 1) * 4)
                        ha, hb = 2 * (q0 - 6 * t), 2 * (q1 - 6 * t)
                        i = dve.tensor_tensor(xw[:, t, d, ha * 64:hb * 64].rearrange("p (h c) -> p h c", c=64),
                                              x_turned(q0, q1).rearrange("p (h c) -> p h c", c=64),
                                              w[:, ha:hb, :].broadcast_to([P, hb - ha, 64]), ALU.mult)
                        q0 = q1
            i.then_inc(c_xw.sem, 1)

        def fourier_pe(pe):
            pe.wait_ge(p_ea, CTX_NA + 1)
            for t in range(2):
                for b in range(2):
                    i = mm(acc[:, t, b * T:(b + 1) * T], uf[:, b, t * P:(t + 1) * P], K2["dft_head"])
            i.then_inc(f_p.sem, 1)
            pe.wait_ge(f_pc.sem, 1)
            for b in range(2):
                for t in range(2):
                    for part, name in enumerate(("dft_cos", "dft_sin")):
                        i = mm(acc[:, 2, b * T:(b + 1) * T], pcs[:, t, b, part * P:(part + 1) * P],
                               K2[name].rearrange("p (t l) -> p t l", t=2)[:, t, :],
                               start=(t == 0 and part == 0), stop=(t == 1 and part == 1))
            i.then_inc(f_f.sem, 1)
            pe.wait_ge(f_fc.sem, 1)
            for b in range(2):
                i = mm(acc[:, 3, b * T:(b + 1) * T], fw[:, b, :], uf[:, b, :])
            i.then_inc(f_y.sem, 1)

        def fourier_act(act):
            act.wait_ge(f_p.sem, 1)
            nc.scalar.activation(pcs, acc[:, 0:2, :].rearrange("p t (b c) -> p t b c", b=2), ACT.Copy).then_inc(f_pc.sem, 1)
            act.wait_ge(f_f.sem, 1)
            nc.scalar.activation(uf[:], acc[:, 2, :].rearrange("p (b t) -> p b t", b=2), ACT.Copy).then_inc(f_fc.sem, 1)
            act.wait_ge(f_y.sem, 1)
            nc.scalar.activation(work[:, 0:2, :], acc[:, 3, :].rearrange("p (b t) -> p b t", b=2), ACT.Copy).then_inc(f_yc.sem, 1)

        def head_rows(h):
            return slice(64 * (h % 2), 64 * (h % 2) + 64)

        def mixer2_pe(pe, n0):
            fourier_pe(pe)
            steps_pe(pe, 1, dtT, CTX_NA + X_NA)
            pe.wait_ge(d_cc.sem, d_cc.after(1))
            for d, own in enumerate(("col_ge", "col_le")):
                for l in range(2):
                    dst = misc[0:12, (2 * d + l) * P:(2 * d + l + 1) * P]
                    other = 1 - l if (l == 1) == (d == 0) else None
                    i = mm(dst, small[:, DA_, l, 12 * d:12 * d + 12], K[own], start=True, stop=other is None)
                    if other is not None:
                        i = mm(dst, small[:, DA_, other, 12 * d:12 * d + 12], K["ones"], start=False, stop=True)
            i.then_inc(x_csr.sem, 1)
            pe.wait_ge(p_si, CTX_ND + X_ND)
            pe.wait_ge(f_yc.sem, 1)
            for g in range(GROUPS):
                for b in range(2):
                    i = mm(acc[:, g, b * T:(b + 1) * T], cv[:, 10 + g, b * P:(b + 1) * P], cv[:, g, :])
            i.then_inc(x_cb.sem, 1)
            for t in range(2):
                for b in range(6):
                    q = 6 * t + b
                    i = pe.transpose(lin[:, q // 4, (q % 4) * P:(q % 4 + 1) * P], cv[:, 4 + b, t * P:(t + 1) * P], K["ident"])
            i.then_inc(x_xt.sem, 1)
            pe.wait_ge(x_csc.sem, 1)
            pe.wait_ge(x_cbc.sem, 1)
            pe.wait_ge(x_xc.sem, 1)
            csr_row = csr[:].rearrange("p d t -> p (d t)")

            def spread(h):
                if h >= 2:
                    pe.wait_ge(x_d.sem, h - 1)
                mm(acc[:, h % 2, :], K2["pick_head"].rearrange("p (h c) -> p h c", h=12)[0:12, h, :], csr_row).then_inc(x_cs.sem, 1)
            spread(0)
            spread(1)
            for h in range(SSD_HEADS):
                p = h // 2
                if h % 2 == 0:
                    if p:
                        pe.wait_ge(x_t.sem, p)
                    if p >= RING:
                        pe.wait_ge(x_yp.sem, p - 2)
                    mm(acc[:, 2, :], K2["pick_pair"].rearrange("p (h c) -> p h c", h=6)[0:12, p, :], csr_row).then_inc(x_ps.sem, 1)
                    for hh in (h, h + 1):
                        for d in range(2):
                            i = mm(acc[head_rows(hh), 3, d * T:(d + 1) * T], h0[:, hh // 3, d, 64 * (hh % 3):64 * (hh % 3) + 64],
                                   cv[:, hh // 3, :])
                    i.then_inc(x_yo.sem, 1)
                pe.wait_ge(x_mm.sem, h + 1)
                for t in range(2):
                    i = mm(lin[head_rows(h), p % RING, 0:T], xtok[:, t, 64 * h:64 * h + 64], mt[:, h % 2, t, :], start=(t == 0), stop=(t == 1))
                i.then_inc(x_y.sem, 1)
                if h + 2 < SSD_HEADS:
                    spread(h + 2)
            for p in range(6):
                pe.wait_ge(x_sq.sem, p + 1)
                i = mm(misc[0:4, 0:T], K2["member"].rearrange("p (b g) -> p b g", g=4)[:, p, :], zs[:, p, :], start=(p == 0), stop=(p == 5))
            i.then_inc(x_gs.sem, 1)
            pe.wait_ge(x_gi.sem, 1)
            for p in range(6):
                i = mm(acc[:, p // 2, (p % 2) * T:(p % 2) * T + T], K2["spread"].rearrange("p (b c) -> p b c", b=6)[0:4, p, :], grs[:])
            i.then_inc(x_sp.sem, 1)
            pe.wait_ge(x_cat.sem, 6)
            for p in range(OUT_CHUNKS):
                pe.wait_ge(x_cl.sem, p + 1)
                rows_pe(pe, n0.at(p), lambda h: hhi[:, 2 * p + h, :], lambda h: hlo[:, 2 * p + h, :], None, p == 0,
                        p == OUT_CHUNKS - 1, lambda h: None)

        def mixer2_act(act, n0):
            fourier_act(act)
            split_high(act, n0.at(2))
            steps_act(act, 1)
            act.wait_ge(x_csr.sem, 1)
            nc.scalar.activation(csr[:], misc[0:12, :].rearrange("p (d t) -> p d t", d=2), ACT.Copy).then_inc(x_csc.sem, 1)
            act.wait_ge(x_cb.sem, 1)
            nc.scalar.activation(cb[:], acc[:].rearrange("p g (i t) -> p g i t", i=2), ACT.Copy).then_inc(x_cbc.sem, 1)
            for h in range(SSD_HEADS):
                if h % 2 == 0:
                    act.wait_ge(x_ps.sem, h // 2 + 1)
                    if h:
                        act.wait_ge(x_t.sem, h // 2)
                    nc.scalar.activation(ep[:], acc[:, 2, :].rearrange("p (d t) -> p d t", d=2), ACT.Exp).then_inc(x_ep.sem, 1)
                act.wait_ge(x_d.sem, h + 1)
                nc.scalar.activation(ex[:, h % 2, :], ex[:, h % 2, :], ACT.Exp).then_inc(x_e.sem, 1)
            for p in range(6):
                act.wait_ge(x_yp.sem, p + 1)
                nc.scalar.activation(zs[:, p, :], work[:, 2 + p, :], ACT.Square).then_inc(x_sq.sem, 1)
            act.wait_ge(x_gs.sem, 1)
            nc.scalar.activation(grt[:], misc[0:4, 0:T], ACT.Sqrt, bias=K["eps6"][0:4, :], scale=1.0 / GW).then_inc(x_gr.sem, 1)
            for p in range(OUT_CHUNKS):
                if p:
                    act.wait_ge(x_cat.sem, 2 * p)
                else:
                    act.wait_ge(f_yc.sem, 1)
                nc.scalar.activation(hhi[:, 2 * p:2 * p + 2, :], work[:, 2 * p:2 * p + 2, :], ACT.Copy).then_inc(x_ch.sem, 1)
            for j in (3, 4, 5):
                split_high(act, n0.at(j))

        def mixer2_dve(dve, st, n0):
            split_low(dve, n0.at(2))
            steps_dve(dve, st, 1)
            dve.wait_ge(x_xt.sem, 1)
            dve.tensor_copy(xtok[:].rearrange("p t c -> p (t c)"), lin[:].rearrange("p b c -> p (b c)")).then_inc(x_xc.sem, 1)
            bars = K2["bars"]

            def differences(h):
                dve.wait_ge(x_cs.sem, h + 1)
                if h >= 2:
                    dve.wait_ge(x_m.sem, h - 1)
                cs = acc[:, h % 2, :].rearrange("p (d t) -> p d t", d=2)
                e = ex[:, h % 2, :]
                for dst, t, d, l0, l1, b0 in ((e[:, 0:T], 0, 0, 0, T, 0), (e[:, T:T + P], 0, 1, 0, P, 2 * P),
                                              (e[:, T + P:2 * T], 1, 0, P, T, 0), (e[:, 2 * T:3 * T], 1, 1, 0, T, P)):
                    i = dve.scalar_tensor_tensor(out=dst, in0=cs[:, d, l0:l1], scalar=small[:, CS_, t, 12 * d + h:12 * d + h + 1],
                                                 in1=bars[:, b0:b0 + l1 - l0], op0=ALU.subtract, op1=ALU.min)
                i.then_inc(x_d.sem, 1)

            differences(0)
            for h in range(SSD_HEADS):
                p = h // 2
                if h + 1 < SSD_HEADS:
                    differences(h + 1)
                if h % 2 == 0:
                    dve.wait_ge(x_yo.sem, p + 1)
                    dve.wait_ge(x_ep.sem, p + 1)
                    if p:
                        dve.wait_ge(x_yp.sem, p)
                    dve.tensor_tensor(yo[:], acc[:, 3, :].rearrange("p (d t) -> p d t", d=2), ep[:], ALU.mult).then_inc(x_t.sem, 1)
                dve.wait_ge(x_e.sem, h + 1)
                if h >= 2:
                    dve.wait_ge(x_y.sem, h - 1)
                e = ex[:, h % 2, :]
                m = mt[:, h % 2]
                dt = lambda t, d: small[:, DT_, t, 12 * d + h:12 * d + h + 1]
                dve.tensor_scalar(m[:, 0, :], e[:, 0:T], dt(0, 0), None, ALU.mult)
                st(dve.tensor_scalar(m[:, 1, :], e[:, 2 * T:3 * T], dt(1, 1), None, ALU.mult))
                dve.scalar_tensor_tensor(out=m[:, 0, 0:P], in0=e[:, T:T + P], scalar=dt(0, 1), in1=m[:, 0, 0:P], op0=ALU.mult, op1=ALU.add)
                dve.scalar_tensor_tensor(out=m[:, 1, P:T], in0=e[:, T + P:2 * T], scalar=dt(1, 0), in1=m[:, 1, P:T],
                                         op0=ALU.mult, op1=ALU.add).then_inc(x_m.sem, 1)
                if h % 2 == 1:
                    dve.wait_ge(x_y.sem, h + 1)
                    dve.wait_ge(x_t.sem, p + 1)
                    w = work[:, 2 + p, :]
                    st(dve.scalar_tensor_tensor(out=w, in0=cv[:, 4 + p, :], scalar=dsk[:, p:p + 1], in1=lin[:, p % RING, 0:T],
                                                op0=ALU.mult, op1=ALU.add))
                    st(dve.tensor_tensor(w, w, yo[:, 0, :], ALU.add))
                    st(dve.tensor_tensor(w, w, yo[:, 1, :], ALU.add))
                    dve.tensor_tensor(w, w, zs[:, p, :], ALU.mult).then_inc(x_yp.sem, 1)
            dve.wait_ge(x_gr.sem, 1)
            dve.reciprocal(grs[:], grt[:]).then_inc(x_gi.sem, 1)
            dve.wait_ge(x_sp.sem, 1)
            for p in range(6):
                dve.scalar_tensor_tensor(out=work[:, 2 + p, :], in0=work[:, 2 + p, :], scalar=xcol[:, 0, V_SSDN + p:V_SSDN + p + 1],
                                         in1=acc[:, p // 2, (p % 2) * T:(p % 2) * T + T], op0=ALU.mult, op1=ALU.mult).then_inc(x_cat.sem, 1)
            for p in range(OUT_CHUNKS):
                dve.wait_ge(x_ch.sem, p + 1)
                dve.tensor_tensor(hlo[:, 2 * p:2 * p + 2, :], work[:, 2 * p:2 * p + 2, :],
                                  hhi[:, 2 * p:2 * p + 2, :].bitcast(F32), ALU.subtract).then_inc(x_cl.sem, 1)
            for j in (3, 4, 5):
                split_low(dve, n0.at(j))

        def mixer2_pool(pool, n0):
            split_low(pool, n0.at(2))
            for h in range(SSD_HEADS):
                pool.wait_ge(x_m.sem, h + 1)
                pool.tensor_tensor(mt[:, h % 2], mt[:, h % 2], cb[:, h // 3], ALU.mult).then_inc(x_mm.sem, 1)
            for j in (3, 4, 5):
                split_low(pool, n0.at(j))

        AFTER1 = LAYERS * LAYER_CHUNKS
        FFN_CHUNKS = UP_CHUNKS + DOWN_CHUNKS
        N_CTX = Place(AFTER1)
        N_CTXP = Place(AFTER1 + FFN_CHUNKS)
        N_FFN1 = Place(AFTER1 + FFN_CHUNKS + CTX_PROJ_CHUNKS)
        N_PROJ = N_FFN1.at(FFN_CHUNKS)
        N_OUT2 = N_PROJ.at(MIX2_CHUNKS)
        N_FFN2 = N_OUT2.at(OUT_CHUNKS)
        END = N_FFN2.count(FFN_CHUNKS)

        @block.sync
        def _(sp):
            sp.dma_start(tab[:], a["tables"]).then_inc(s_tab, 16)
            sp.dma_start(tab1[:], a["tables_1"]).then_inc(s_tab, 16)
            sp.dma_start(outt, a["x"].rearrange("o (t p) d -> p (o t) d", p=P)).then_inc(s_x, 16)
            sp.dma_start(crow[0:8, :], a["c_2"].rearrange("o (k p) -> (o k) p", p=P)).then_inc(s_crow, 16)
            sp.dma_start(crow[8:16, :], a["c_ctx_2"].rearrange("(k p) -> k p", p=P)).then_inc(s_crow, 16)
            sp.wait_ge(s_zero, 2)
            load_mixer_params(sp, 0)
            load_ffn_params(sp, 0)
            for L in range(LAYERS):
                n0 = base(L)
                w = one(a["w_in"], L)
                for j, (c0, width) in enumerate(((0, 256), (256, 256), (512, 256), (768, 256), (1024, 140),
                                                 (SGU_COL, 256), (SGU_COL + 256, 256), (POOL_COL, 256))):
                    load_cols(sp, n0.at(j), w, c0, width)
                for p in range(OUT_CHUNKS):
                    if p == 3:
                        for t in range(L * ADA_LAYER, (L + 1) * ADA_LAYER):
                            ada_load(sp, t)
                    load_rows(sp, n0.at(MIX1_CHUNKS + p), one(a["w_out"], L), 2 * P * OUT1_ORDER[p])
                if L + 1 == LAYERS:
                    sp.wait_ge(e_ad.sem, ADA_BLOCKS)
                    for t in range(2):
                        sp.dma_start(ada[t][:].rearrange("p k c -> p (k c)"), a["ctx_2"][0, t * P:(t + 1) * P, :]).then_inc(s_ctx, 16)
                w = one(a["ffn_up"], L)
                load_ffn(sp, n0.at(MIX1_CHUNKS + OUT_CHUNKS), w[:, 0:FF], w[:, FF:2 * FF], one(a["ffn_down"], L))
                sp.wait_ge(s_used, n0.count(MIX1_CHUNKS + OUT_CHUNKS))
                sp.wait_ge(m_cal.sem, m_cal.after(L))
                sp.wait_ge(m_vw.sem, m_vw.after(L))
                if L + 1 < LAYERS:
                    load_mixer_params(sp, L + 1)
                    load_ffn_params(sp, L + 1)
                else:
                    sp.wait_ge(s_zero, 3)
                    load_second_params(sp)
            ffn = lambda n, i: load_ffn(sp, n, a[f"ffn{i}_w_gate_2"][0], a[f"ffn{i}_w_up_2"][0], a[f"ffn{i}_w_down_2"][0])
            ffn(N_CTX, 1)
            proj_load(sp, N_CTXP, CTX_JS)
            ffn(N_FFN1, 1)
            proj_load(sp, N_PROJ, X_JS)
            for p in range(OUT_CHUNKS):
                load_rows(sp, N_OUT2.at(p), a["w_out_2"][0], 2 * P * p)
            ffn(N_FFN2, 2)
            sp.wait_ge(s_outr, 1)
            sp.dma_start(out.rearrange("o (t p) d -> p (o t) d", p=P), outt).then_inc(s_out, 16)
            sp.wait_ge(s_out, 16)

        @block.tensor
        def _(pe):
            st = Steps(pe, s_st["pe"])
            pe.wait_ge(s_tab, 32)
            pe.wait_ge(s_crow, 32)
            pe.transpose(misc[:, 0:16], crow[:], K["ident"][0:16, 0:16]).then_inc(e_ct, 1)
            pe.wait_ge(s_x, 16)
            turn_in_pe(pe, lambda t: outt[:, t, :])
            pe.wait_ge(e_cs, 1)
            for L in range(LAYERS):
                n0 = base(L)
                mixer1_pe(pe, st, L, n0)
                pe.wait_ge(e_am.sem, e_am.after(L))
                post_pe(pe, 2 * L)
                pre_pe(pe, 2 * L + 1)
                ffn_pe(pe, L, n0.at(MIX1_CHUNKS + OUT_CHUNKS))
                post_pe(pe, 2 * L + 1)
            second_start_pe(pe)
            pe.wait_ge(s_ctx, 32)
            pe.wait_ge(e_x.sem, e_x.after(3))
            turn_in_pe(pe, lambda t: ada[t][:].rearrange("p k c -> p (k c)"))
            pe.wait_ge(t_gn.sem, 1)
            pre_pe(pe, 4)
            ffn_pe(pe, 2, N_CTX)
            post_pe(pe, 4)
            pre_pe(pe, 5)
            proj_pe(pe, N_CTXP, CTX_JS, 0, 0, 5)
            steps_pe(pe, 0, ctx_dt, CTX_NA)
            ctx_state_pe(pe)
            pre_pe(pe, 6)
            pe.wait_ge(c_hc.sem, 1)
            ffn_pe(pe, 3, N_FFN1)
            post_pe(pe, 5)
            pre_pe(pe, 7)
            proj_pe(pe, N_PROJ, X_JS, CTX_NA, CTX_ND, 7)
            mixer2_pe(pe, N_OUT2)
            post_pe(pe, 6)
            pre_pe(pe, 8)
            ffn_pe(pe, 4, N_FFN2)
            post_pe(pe, 7)
            pe.wait_ge(e_x.sem, e_x.after(7))
            for k in range(KD):
                for t in range(2):
                    i = pe.transpose(acc[:, 2 * t + k // 4, (k % 4) * P:(k % 4 + 1) * P], xT[:, k, t * P:(t + 1) * P], K["ident"])
            i.then_inc(s_fin, 1)

        @block.scalar
        def _(act):
            st = Steps(act, s_st["act"])
            act.wait_ge(s_tab, 32)
            act.wait_ge(e_ct, 1)
            nc.scalar.activation(csil[:].rearrange("p v k -> p (v k)"), misc[:, 0:16], ACT.Silu).then_inc(e_cs, 1)
            split_high(act, Place(0))
            split_high(act, Place(1))
            for L in range(LAYERS):
                n0 = base(L)
                act.wait_ge(e_vt.sem, e_vt.after(L))
                if L:
                    act.wait_ge(e_pt.sem, e_pt.after(2 * L - 1))
                nc.scalar.activation(vcol[:], misc[:, 0:R_ROWS], ACT.Copy)
                nc.scalar.activation(pecol[:], misc[:, 128:160], ACT.Copy)
                nc.scalar.activation(fcol[:], misc[:, 256:256 + 176].rearrange("p (j r) -> p j r", j=2), ACT.Copy).then_inc(e_vc.sem, 1)
                pre_act(act, 2 * L, xT, after_post(2 * L - 1) if L else
                        (lambda eng, k: eng.wait_ge(e_xc.sem, k // 2 + 1)))
                mixer1_act(act, st, L, n0)
                post_act(act, 2 * L, n0.count(MIX1_CHUNKS + OUT_CHUNKS))
                pre_act(act, 2 * L + 1, xT, after_post(2 * L))
                n1 = n0.at(MIX1_CHUNKS + OUT_CHUNKS)
                ffn1_act(act, L, n1)
                down_split(act, n1, split_high, 2)
                post_act(act, 2 * L + 1, n0.count(LAYER_CHUNKS))
            act.wait_ge(t_gn.sem, 1)
            pre_act(act, 4, cT, lambda eng, k: eng.wait_ge(e_xc.sem, 4 + k // 2 + 1), shift(1, 0))
            ffn2_act(act, 2, N_CTX)
            down_split(act, N_CTX, split_high, 2)
            post_act(act, 4, N_CTXP.count())
            pre_act(act, 5, cT, after_post(4), shift(1, 1))
            proj_act(act, N_CTXP, CTX_JS, 0, ctx_cv, 4, ctx_dt)
            steps_act(act, 0)
            ctx_state_act(act)
            pre_act(act, 6, xT, lambda eng, k: None, shift(0, 0))
            ffn2_act(act, 3, N_FFN1)
            down_split(act, N_FFN1, split_high, 2)
            post_act(act, 5, N_PROJ.count())
            pre_act(act, 7, xT, after_post(5), shift(0, 1))
            proj_act(act, N_PROJ, X_JS, CTX_ND, cv, 0, dtT)
            mixer2_act(act, N_OUT2)
            post_act(act, 6, N_FFN2.count())
            pre_act(act, 8, xT, after_post(6), shift(0, 2))
            ffn2_act(act, 4, N_FFN2)
            down_split(act, N_FFN2, split_high, 0)
            post_act(act, 7, END)
            act.wait_ge(s_fin, 1)
            for t in range(2):
                i = nc.scalar.activation(outt[:, t, :].rearrange("p (b c) -> p b c", b=2), acc[:, 2 * t:2 * t + 2, :], ACT.Copy)
            i.then_inc(s_outr, 1)

        @block.vector
        def _(dve):
            st = Steps(dve, s_st["dve"])
            dve = nc.vector
            split_low(dve, Place(0))
            split_low(dve, Place(1))
            turn_in_dve(dve, 0, xT)
            col = lambda r: (lambda k: vcol[:, r + k:r + k + 1])
            for L in range(LAYERS):
                n0 = base(L)
                dve.wait_ge(e_vc.sem, e_vc.after(L))
                pre_dve(dve, st, 2 * L, xT, col(R_MIX_PRE))
                mixer1_dve(dve, st, L, n0)
                dve.wait_ge(e_ad.sem, e_ad.after(L))
                dve.tensor_copy(mod[:, L * ADA_LAYER:(L + 1) * ADA_LAYER, :],
                                misc[:, T:T + 2 * ADA_LAYER].rearrange("p (b v) -> p b v", v=2)).then_inc(e_am.sem, 1)
                post_dve(dve, st, 2 * L, col(R_MIX_POST))
                pre_dve(dve, st, 2 * L + 1, xT, col(R_FFN_PRE))
                n1 = n0.at(MIX1_CHUNKS + OUT_CHUNKS)
                ffn1_dve(dve, st, L, n1)
                down_split(dve, n1, split_low, 2)
                post_dve(dve, st, 2 * L + 1, col(R_FFN_POST))
            second_start_dve(dve, st)
            turn_in_dve(dve, 1, cT)
            pre_dve(dve, st, 4, cT, gain(0), shift(1, 0))
            ffn2_dve(dve, 2, N_CTX)
            down_split(dve, N_CTX, split_low, 2)
            post_dve(dve, st, 4, gain(5))
            pre_dve(dve, st, 5, cT, gain(1), shift(1, 1))
            proj_dve(dve, st, N_CTXP, CTX_JS, 0, ctx_cv, 4)
            steps_dve(dve, st, 0)
            ctx_state_dve(dve, st)
            pre_dve(dve, st, 6, xT, gain(2), shift(0, 0))
            ffn2_dve(dve, 3, N_FFN1)
            down_split(dve, N_FFN1, split_low, 2)
            post_dve(dve, st, 5, gain(6))
            pre_dve(dve, st, 7, xT, gain(3), shift(0, 1))
            proj_dve(dve, st, N_PROJ, X_JS, CTX_ND, cv, 0)
            mixer2_dve(dve, st, N_OUT2)
            post_dve(dve, st, 6, gain(7))
            pre_dve(dve, st, 8, xT, gain(4), shift(0, 2))
            ffn2_dve(dve, 4, N_FFN2)
            down_split(dve, N_FFN2, split_low, 0)
            post_dve(dve, st, 7, gain(8))

        @block.gpsimd
        def _(pool):
            st = Steps(pool, s_st["pool"])
            pool = nc.gpsimd
            pool.memset(pw[:], 0.0).then_inc(s_zero, 1)
            pool.memset(glu[:], 0.0)
            pool.memset(psum2[:], 0.0)
            pool.memset(zpad[:], 0.0).then_inc(s_zero, 1)
            split_low(pool, Place(0))
            split_low(pool, Place(1))
            for L in range(LAYERS):
                n0 = base(L)
                mixer1_pool(pool, st, L, n0)
                post_pool(pool, 2 * L, xT)
                n1 = n0.at(MIX1_CHUNKS + OUT_CHUNKS)
                if L + 1 == LAYERS:
                    pool.memset(fw[:], 0.0).then_inc(s_zero, 1)
                ffn1_pool(pool, L, n1)
                down_split(pool, n1, split_low, 2)
                post_pool(pool, 2 * L + 1, xT)
            ffn2_pool(pool, 2, N_CTX)
            down_split(pool, N_CTX, split_low, 2)
            post_pool(pool, 4, cT)
            proj_pool(pool, N_CTXP, CTX_JS)
            ffn2_pool(pool, 3, N_FFN1)
            down_split(pool, N_FFN1, split_low, 2)
            post_pool(pool, 5, xT)
            proj_pool(pool, N_PROJ, X_JS)
            mixer2_pool(pool, N_OUT2)
            post_pool(pool, 6, xT)
            ffn2_pool(pool, 4, N_FFN2)
            down_split(pool, N_FFN2, split_low, 0)
            post_pool(pool, 7, xT)


_INS = (
    "x", "norm_mix_pre", "norm_mix_post", "norm_ffn_pre", "norm_ffn_post", "w_in", "w_out", "conv_dw_w", "conv_dw_b",
    "conv_ln_g", "conv_ln_b", "nsa_pe_k", "nsa_pe_v", "nsa_ck_w1", "nsa_ck_w2", "nsa_cv_w1", "nsa_cv_w2", "sgu_ln_g",
    "sgu_ln_b", "sgu_w", "sgu_b", "pool_w", "pool_scale", "ffn_up", "ffn_conv_w", "ffn_conv_b", "ffn_down",
    "c_2", "ctx_2", "c_ctx_2", "ada_w_2", "ada_b_2", "ffn1_norm_pre_2", "ffn1_norm_post_2", "ffn1_w_gate_2",
    "ffn1_w_up_2", "ffn1_w_down_2", "mix_norm_pre_2", "mix_norm_post_2", "w_in_2", "fourier_w_2", "conv_w_2",
    "conv_b_2", "dt_bias_2", "a_log_2", "d_skip_2", "ssd_norm_2", "w_out_2", "ffn2_norm_pre_2", "ffn2_norm_post_2",
    "ffn2_w_gate_2", "ffn2_w_up_2", "ffn2_w_down_2",
)


def kernel(**inputs):
    import concourse.bacc as bacc
    from concourse.bass_utils import run_bass_kernel_spmd

    nc = bacc.Bacc("TRN2", target_bir_lowering=False, num_devices=1)
    (at, table), (at1, table1), (at2, table2) = tables()
    arrays, args = {}, []
    for name in _INS + ("tables", "tables_1", "tables_2"):
        x = {"tables": table, "tables_1": table1, "tables_2": table2}.get(name)
        if x is None:
            x = np.ascontiguousarray(inputs[name])
        arrays["in_" + name] = x
        args.append(nc.dram_tensor("in_" + name, x.shape, mybir.dt.from_np(x.dtype), kind="ExternalInput").ap())
    out = nc.dram_tensor("out_dram", (1, T, D), F32, kind="ExternalOutput").ap()
    build(nc, _INS + ("tables", "tables_1", "tables_2"), args, out, at, at1, at2)
    result = run_bass_kernel_spmd(nc, [arrays], core_ids=[0])
    return result.results[0]["out_dram"]
```

```python
from contextlib import ExitStack

import numpy as np

import concourse.bass as bass
from concourse import mybir
from concourse.alu_op_type import AluOpType as ALU

ACT = mybir.ActivationFunctionType
F32 = mybir.dt.float32
F32R = mybir.dt.float32r
AX_X = mybir.AxisListType.X

P = 128
T = 256
D = 1024
KD = D // P
FF = 2816
FB = FF // P
LAYERS = 2
RING = 3
CHUNK = 2048
DVE_PART = 1280
PAD = 30
N_CMP = 15
HEADS1 = 4
SGU_COL, POOL_COL = 1164, 1676
MIX1_CHUNKS = 8
OUT_CHUNKS = 4
UP_CHUNKS = FB
DOWN_CHUNKS = FB // 2
LAYER_CHUNKS = MIX1_CHUNKS + OUT_CHUNKS + UP_CHUNKS + DOWN_CHUNKS
OUT1_ORDER = (3, 2, 1, 0)

ADA_BLOCKS = 72
ADA_LAYER = ADA_BLOCKS // LAYERS
SSD_HEADS, GROUPS, GW = 12, 4, 192
CONV_BLOCKS = 14
MIX2_CHUNKS = 12
CTX_PROJ_CHUNKS = 6
MIX2_COLS = 2840

V_SSDN, V_ADAB, V_ROWS = 48, 54, 126
V_CW, V_CB, V_ROWS2 = 0, 42, 56

R_MIX_PRE, R_MIX_POST, R_FFN_PRE, R_FFN_POST = 0, 8, 16, 24
R_DW, R_DWB, R_CLG, R_CLB, R_PSC, R_SGB, R_ROWS = 32, 94, 96, 98, 100, 102, 106


def tables():
    i = np.arange(P)
    blk = lambda m: np.kron(np.eye(2), m)
    cols = {}
    cols["ident"] = np.eye(P)
    cols["ones"] = np.ones((P, P))
    row, col = i[:, None], i[None, :]
    cols["col_ge"] = col >= row
    cols["col_le"] = col <= row
    cols["col_lt"] = col < row
    cols["col_gt"] = col > row
    cols["bar_ge"] = np.where(col >= row, 0.0, -1e30)
    cols["bar_le"] = np.where(col <= row, 0.0, -1e30)
    shared, cols = cols, {}
    half = 32
    r = np.zeros((64, 64))
    r[np.arange(half) + half, np.arange(half)] = -1.0
    r[np.arange(half), np.arange(half) + half] = 1.0
    cols["rope_turn"] = blk(r)
    twice = np.zeros((P, P))
    twice[:64] = np.concatenate([np.eye(64), np.eye(64)], axis=1)
    cols["twice"] = twice
    turned = np.zeros((P, P))
    turned[:64] = np.concatenate([r, r], axis=1)
    cols["twice_turn"] = turned
    inv = (np.float32(10000.0) ** (-np.arange(half, dtype=np.float32) * np.float32(2.0) / np.float32(64)))
    ang = (np.arange(T, dtype=np.float32)[:, None] * inv[None, :].astype(np.float32)).astype(np.float32)
    cols["cos"] = np.tile(np.cos(ang).T, (4, 1))
    cols["sin"] = np.tile(np.sin(ang).T, (4, 1))
    ends = np.arange(16) * 16 + 31
    seen = np.stack([ends[None, :] <= (b * P + i)[:, None] for b in range(2)], axis=1)
    cols["cmp_bar"] = np.where(seen, 0.0, -1e30).reshape(P, 32)
    cols["cmp_seen"] = seen.reshape(P, 32)
    w = np.array([[2, 4], [8, 16]])
    n = np.zeros((P, 2, T))
    for b in range(2):
        for h in range(2):
            n[64 * h:64 * h + 64, b] = 1.0 / np.minimum(np.arange(T) + 1, w[b, h])
    cols["inv_count"] = n.reshape(P, 2 * T)
    shared["eps6"] = np.full((P, 1), 1e-6)
    shared["eps5"] = np.full((P, 1), 1e-5)
    cols2 = {}
    cols2["bars"] = np.concatenate([np.where(col >= row, 0.0, -1e30), np.zeros((P, P)), np.where(col <= row, 0.0, -1e30)], axis=1)
    d = np.arange(64)
    angle = 2 * np.pi * ((d[:, None] * d[None, :]) % 64) / 64
    cols2["dft_head"] = np.concatenate([blk(np.cos(angle)) / 128, blk(-np.sin(angle)) / 128], axis=1)
    t = np.arange(T)
    angle = (2 * np.pi * ((t[:, None] * t[None, :]) % T) / T).reshape(2, P, T).transpose(1, 0, 2)
    cols2["dft_cos"] = np.cos(angle)
    cols2["dft_sin"] = np.sin(angle)
    pick = np.zeros((P, 12, P))
    pair = np.zeros((P, 6, P))
    for h in range(12):
        pick[h, h] = 1.0
        pair[h, h // 2, 64 * (h % 2):64 * (h % 2) + 64] = 1.0
    cols2["pick_head"] = pick
    cols2["pick_pair"] = pair
    feature = np.arange(6 * P) // 192
    member = (feature[:, None] == np.arange(4)[None, :]).reshape(6, P, 4)
    cols2["member"] = member.transpose(1, 0, 2)
    spread = np.zeros((P, 6, P))
    spread[0:4] = member.transpose(2, 0, 1)
    cols2["spread"] = spread
    def packed(cols):
        at, parts, n = {}, [], 0
        for name, a in cols.items():
            a = np.asarray(a, np.float32).reshape(P, -1)
            at[name] = (n, a.shape[1])
            parts.append(a)
            n += a.shape[1]
        return at, np.ascontiguousarray(np.concatenate(parts, axis=1))

    return packed(shared), packed(cols), packed(cols2)


class Event:

    def __init__(self, sem, per=1):
        self.sem, self.per = sem, per

    def after(self, call, steps=None):
        return call * self.per + (self.per if steps is None else steps)


class Place:

    def __init__(self, fixed, turns=0):
        self.fixed, self.turns = fixed, turns

    def at(self, steps, turns=0):
        return Place(self.fixed + steps, self.turns + turns)

    @property
    def slot(self):
        return self.fixed % RING

    @property
    def reused(self):
        return self.fixed >= RING or not isinstance(self.turns, int) or self.turns > 0

    def count(self, steps=0):
        return self.turns * RING + (self.fixed + steps)

    def landed(self):
        return self.turns * 32 + 32 * (self.fixed // RING + 1)


class Steps:

    def __init__(self, eng, sem):
        self.eng, self.sem, self.base, self.n = eng, sem, 0, 0

    def __call__(self, ins):
        self.n += 1
        ins.then_inc(self.sem, 1)
        self.eng.wait_ge(self.sem, self.base + self.n)

    def enter(self, i, first, per):
        self.saved = (self.base, self.n, first, per)
        self.base, self.n = self.base + self.n + (i - first) * per, 0

    def leave(self, last):
        base, n, first, per = self.saved
        assert self.n == per, (self.n, per)
        self.base, self.n = base, n + (last - first) * per


def build(nc, names, ins, out, at, at1, at2):
    a = dict(zip(names, ins))
    ctx = ExitStack()
    with ctx:
        def sb(name, shape, dt=F32):
            return ctx.enter_context(nc.sbuf_tensor(name, shape, dt))

        def sem(name):
            return ctx.enter_context(nc.semaphore(name))

        def event(name, per=1):
            return Event(sem(name), per)

        tab = sb("tab", [P, a["tables"].shape[1]])
        K = {k: tab[:, o:o + w] for k, (o, w) in at.items()}
        raw = [sb(f"raw{i}", [P, CHUNK]) for i in range(RING)]
        whi = [sb(f"whi{i}", [P, CHUNK], F32R) for i in range(RING)]
        wlo = [sb(f"wlo{i}", [P, CHUNK], F32R) for i in range(RING)]
        xT = sb("xT", [P, KD, T])
        hhi = sb("hhi", [P, KD, T], F32R)
        hlo = sb("hlo", [P, KD, T], F32R)
        work = sb("work", [P, KD, T])
        root = sb("root", [P, T])
        rstd = sb("rstd", [P, T])
        crow = sb("crow", [16, P])
        vcol = sb("vcol", [P, R_ROWS])
        fcol = sb("fcol", [P, 2, 88])
        csil = sb("csil", [P, 2, KD])
        mod = sb("mod", [P, ADA_BLOCKS, 2])
        before = nc.sbuf_bytes_remaining
        with ExitStack() as one_ctx:
            def one_(name, shape, dt=F32):
                return one_ctx.enter_context(nc.sbuf_tensor(name, shape, dt))

            vrow = one_("vrow", [R_ROWS, P])
            perow = one_("perow", [32, P])
            pecol = one_("pecol", [P, 32])
            frow = one_("frow", [88, 2, P])
            sgln = one_("sgln", [P, 2, T])
            wsp = one_("wsp", [P, 4, P])
            bsp = one_("bsp", [P, 2, P])
            cw1 = one_("cw1", [P, 32, 64])
            cw2 = one_("cw2", [P, 192])
            pw = one_("pw", [P, 2, P])
            glu = one_("glu", [P, 2, PAD + T])
            zpad = one_("zpad", [P, 2, 16 + T])
            psum2 = one_("psum2", [P, 4, 16 + T])
            gates = one_("gates", [P, 2, 12])
            hid = one_("hid", [P, 16])
            kc = one_("kc", [P, 16])
            vc = one_("vc", [N_CMP, 64])
            mx = one_("mx", [P, 8])
            sm = one_("sm", [P, 8])
            smc = one_("smc", [P, 8])
            gs = one_("gs", [P, 8])
            bns = one_("bns", [P, 2, 6])
            mv = one_("mv", [P, 2, 2])
            srt = one_("srt", [P, 4])
            tab1 = one_("tab1", [P, a["tables_1"].shape[1]])
            K.update({k: tab1[:, o:o + w] for k, (o, w) in at1.items()})
            size_one = before - nc.sbuf_bytes_remaining
        tab2 = sb("tab2", [P, a["tables_2"].shape[1]])
        K2 = {k: tab2[:, o:o + w] for k, (o, w) in at2.items()}
        cT = sb("cT", [P, KD, T])
        h0 = cT[:].rearrange("p k t -> p (k t)")[:, 0:GROUPS * 2 * GW].rearrange("p (g d c) -> p g d c", g=GROUPS, d=2)
        xrow = sb("xrow", [P, 2, P])
        xcol = sb("xcol", [P, 2, P])
        gain2 = sb("gain2", [P, 9, KD])
        drow = sb("drow", [P, 3, 24])
        small = sb("small", [P, 8, 2, 24])
        skip_all = sb("skip_all", [P, SSD_HEADS])
        dsk = sb("dsk", [P, 6])
        fw = sb("fw", [P, 2, P])
        short = size_one - (before - nc.sbuf_bytes_remaining)
        if short > 0:
            sb("rest_of_region", [P, short // 4 + 8])
        with ExitStack() as turn_ctx:
            def tmp(name, shape, dt=F32):
                return turn_ctx.enter_context(nc.sbuf_tensor(name, shape, dt))

            wspT = tmp("wspT", [P, 4, P])
            aT = tmp("aT", [P, 2, T])
            sig = tmp("sig", [P, 2, T])
            qT = tmp("qT", [P, 2, T])
            qrot = tmp("qrot", [P, 2, T])
            krot = tmp("krot", [P, 2, T])
            rt = tmp("rt", [P, 2, T])
            kvT = tmp("kvT", [P, 4, T])
            uT = tmp("uT", [P, 2, T])
            vT = tmp("vT", [P, 2, T])
            pooled = tmp("pooled", [P, 2, T])
            vtok = tmp("vtok", [P, 4, 64])
            cbuf = tmp("cbuf", [P, 32, N_CMP])
            sc = tmp("sc", [P, 4, T])
            prob = tmp("prob", [P, 4, T])
            scc = tmp("scc", [P, 8, 16])
            probc = tmp("probc", [P, 8, 16])
            pT = tmp("pT", [P, 6, 4, P])
            outt = pT[:].rearrange("p b h k -> p (b h k)")[:, 0:2 * D].rearrange("p (t d) -> p t d", t=2)
            pcT = tmp("pcT", [16, 8, P])
            vn = tmp("vn", [P, 2, T])
            croot = tmp("croot", [P, T])
            crstd = tmp("crstd", [P, T])
            convy = aT
        with ExitStack() as turn_ctx:
            def tmp(name, shape, dt=F32):
                return turn_ctx.enter_context(nc.sbuf_tensor(name, shape, dt))

            ctx_cv = tmp("ctx_cv", [P, 10, T])
            ctx_dt = tmp("ctx_dt", [P, T])
            btok = tmp("btok", [P, 2, 4 * P])
            xw = tmp("xw", [P, 2, 2, 6 * P])
        with ExitStack() as turn_ctx:
            def tmp(name, shape, dt=F32):
                return turn_ctx.enter_context(nc.sbuf_tensor(name, shape, dt))

            uf = tmp("uf", [P, 2, T])
            zs = tmp("zs", [P, 6, T])
            cv = tmp("cv", [P, CONV_BLOCKS, T])
            dtT = tmp("dtT", [P, T])
            xtok = tmp("xtok", [P, 2, 6 * P])
            cb = tmp("cb", [P, GROUPS, 2, T])
            csr = tmp("csr", [SSD_HEADS, 2, T])
            ex = tmp("ex", [P, 2, 3 * T])
            pcs = ex[:].rearrange("p a b -> p (a b)")[:, 0:4 * T].rearrange("p (t b c) -> p t b c", t=2, b=2)
            mt = tmp("mt", [P, 2, 2, T])
            ep = tmp("ep", [P, 2, T])
            yo = tmp("yo", [P, 2, T])
            grt = tmp("grt", [4, T])
            grs = tmp("grs", [4, T])
        ahi = sb("ahi", [P, FB, T], F32R)
        alo = sb("alo", [P, FB, T], F32R)
        taps = sb("taps", [P, RING, 2, T])
        gel = taps[:, :, 0, :]
        prod = gel
        ada = [sb(f"ada{i}", [P, KD, P]) for i in range(RING)]

        lin = ctx.enter_context(nc.psum_tensor("lin", [P, RING, 512], F32))
        acc = ctx.enter_context(nc.psum_tensor("acc", [P, 4, 512], F32))
        misc = ctx.enter_context(nc.psum_tensor("misc", [P, 512], F32))

        s_raw = [sem(f"raw_landed{i}") for i in range(RING)]
        s_hi = sem("high_parts_ready")
        s_lo = sem("low_parts_ready_vector")
        s_lop = sem("low_parts_ready_gpsimd")
        s_used = sem("chunk_used")
        s_tab = sem("tables_landed")
        s_tab1 = sem("block_one_tables_landed")
        s_x = sem("x_landed")
        s_par = sem("mixer_vectors_landed")
        s_parw = sem("mixer_weights_landed")
        s_fpar = sem("ffn_vectors_landed")
        s_zero = sem("zeros_written")
        s_st = {e: sem(f"{e}_own_steps") for e in ("pe", "act", "dve", "pool")}
        s_fin = sem("output_turned")
        s_outr = sem("output_ready")
        s_out = sem("output_landed")

        e_xt = event("input_turned", 4)
        e_xc = event("input_copied", 4)
        e_vt = event("vectors_turned", 1)
        e_vc = event("vectors_copied", 1)
        e_sq = event("squares_ready", KD)
        e_ss = event("sum_of_squares_ready", 1)
        e_rt = event("root_ready", 1)
        e_bk = event("bank_of_wide_sums_complete", 3)
        e_nv = event("normed_ready", KD)
        e_nh = event("norm_high_ready", KD)
        e_h = event("h_ready", KD)
        e_psq = event("post_squares_ready", 4)
        e_pt = event("post_scaled_ready", KD // 2)
        e_xe = event("residual_even_blocks_updated", KD // 2)
        e_xo = event("residual_odd_blocks_updated", KD // 2)
        e_c0 = event("first_tap_ready", FB)
        e_cv = event("taps_ready", FB)
        e_gl = event("gelu_ready", FB)
        e_pr = event("product_ready", FB)
        e_ah = event("act_high_ready", FB)
        e_al = event("act_ready", FB)
        e_sg = event("gate_silu_ready", FB)
        s_crow = sem("conditions_landed")
        e_ct = sem("conditions_turned")
        e_cs = sem("conditions_ready")
        s_ada = [sem(f"modulation_landed{i}") for i in range(RING)]
        e_ad = event("modulation_block_used", ADA_LAYER)
        e_am = event("modulation_copied", 1)
        s_p2 = sem("second_parameters_landed")
        s_ctx = sem("ctx_landed")
        p_ea = sem("projection_read_scalar")
        p_ed = sem("projection_read_vector")
        p_c0 = sem("middle_tap_ready")
        p_si = sem("convolved_ready")
        (t_vt, t_vc, t_gn, d_tr, d_x, d_e, d_a, d_dt, d_cs, d_cc, c_w, c_xt, c_bt, c_bc, c_xw, c_h, c_hc, f_p, f_pc, f_f,
         f_fc, f_y, f_yc, x_cb, x_cbc, x_xt, x_xc, x_csr, x_csc, x_csl, x_cs, x_d, x_e, x_m, x_mm, x_y, x_yo, x_ps, x_ep, x_t, x_yp,
         x_sq, x_gs, x_gr, x_gi, x_sp, x_cat, x_ch, x_cl) = (event(name) for name in (
             "second_vectors_turned", "second_vectors_copied", "gains_ready", "steps_turned", "steps_biased",
             "steps_exponential", "decay_rates_ready", "steps_ready", "decays_summed", "decays_copied",
             "state_weights_ready", "x_turned", "b_turned", "b_copied", "weighted_x_ready", "states_ready", "states_copied",
             "fourier_heads", "fourier_heads_copied", "fourier_tokens", "fourier_tokens_copied", "fourier_out",
             "fourier_out_copied", "bc_ready", "bc_copied", "x_rows_turned", "x_rows_copied", "decays_by_head",
             "decays_by_head_copied", "decays_low_parts_ready", "decays_spread", "decay_differences_ready", "decay_factors_ready",
             "matrix_factors_ready", "mixing_matrix_ready", "head_output_ready", "state_output_ready",
             "pair_decays_spread", "pair_decays_ready", "state_terms_ready", "pair_gated", "pair_squares_ready",
             "group_sums_ready", "group_roots_ready", "group_factors_ready", "group_factors_spread", "pair_normed",
             "second_branch_high", "second_branch_ready"))
        m_ev = event("projection_copied", MIX1_CHUNKS)
        m_rope = event("turned_keys_queries_ready", 1)
        m_tr = event("values_gates_turned", 1)
        m_qk = event("rotary_ready", 1)
        m_vt = event("values_gates_copied", 1)
        m_cb = event("compression_input_ready", 1)
        m_hid = event("compression_hidden", 1)
        m_hg = event("compression_gelu", 1)
        m_kc = event("compressed_ready", 1)
        m_kcc = event("compressed_copied", 1)
        m_glu = event("glu_ready", 1)
        m_sc = event("scores_ready", 4)
        m_mx = event("maxima_ready", 4)
        m_ex = event("exponentials_ready", 4)
        m_pb = event("probabilities_ready", 4)
        m_pt = event("probabilities_turned", 8)
        m_pc = event("probabilities_copied", 8)
        m_o = event("attention_out", 1)
        m_vx = event("gate_values_turned", 2)
        m_bn = event("gate_variance_ready", 1)
        m_br = event("gate_root_ready", 1)
        m_vn = event("gate_values_centred", 1)
        m_vw = event("gate_values_ready", 1)
        m_ws = event("spatial_weights_ready", 1)
        m_f = event("spatial_out", 1)
        m_pl = event("pooled_ready", 1)
        m_pm = event("pool_out", 1)
        m_cy = event("conv_ready", 1)
        m_cs = event("conv_sum_ready", 2)
        m_cc = event("conv_centred", 1)
        m_cq = event("conv_squares", 1)
        m_cr = event("conv_root", 1)
        m_cn = event("conv_normed", 1)
        m_csg = event("gating_output_ready", 1)
        m_cns = event("attention_output_ready", 1)
        m_cah = event("branch_high_ready", 4)
        m_cal = event("branch_ready", 4)

        block = ctx.enter_context(nc.Block())

        def mm(out_, lhsT, rhs, start=True, stop=True, **kw):
            return nc.tensor.matmul(out_, lhsT, rhs, start=start, stop=stop, **kw)

        def mm3(out_, w, xh, xl, first, last):
            wh, wl = w
            mm(out_, wh, xh, start=first, stop=False, skip_group_check=True)
            mm(out_, wh, xl, start=False, stop=False, skip_group_check=True)
            return mm(out_, wl, xh, start=False, stop=last, skip_group_check=True)

        def ring(place):
            return whi[place.slot], wlo[place.slot]

        def load(sp, n, pieces):
            if n.reused:
                sp.wait_ge(s_lo, n.count(1 - RING))
                sp.wait_ge(s_lop, n.count(1 - RING))
            assert len(pieces) == 2
            for dst, src in pieces:
                sp.dma_start(dst, src).then_inc(s_raw[n.slot], 16)

        def split_high(act, n, width=CHUNK):
            act.wait_ge(s_raw[n.slot], n.landed())
            if n.reused:
                act.wait_ge(s_used, n.count(1 - RING))
            nc.scalar.activation(whi[n.slot][:, 0:width], raw[n.slot][:, 0:width], ACT.Copy).then_inc(s_hi, 1)

        def split_low(eng, n, width=CHUNK):
            eng.wait_ge(s_hi, n.count(1))
            part = DVE_PART * width // CHUNK
            lo, hi, done = (0, part, s_lo) if eng is dve_ else (part, width, s_lop)
            eng.tensor_tensor(wlo[n.slot][:, lo:hi], raw[n.slot][:, lo:hi],
                              whi[n.slot][:, lo:hi].bitcast(F32), ALU.subtract).then_inc(done, 1)

        dve_ = nc.vector

        def by_threes(eng, n_steps, body, steps=None, per=0):
            full = n_steps // RING
            for j in range(RING):
                body(j, 0)
            with eng.Fori(1, full) as turn:
                if steps:
                    steps.enter(turn, 1, per)
                for j in range(RING):
                    body(j, turn)
                if steps:
                    steps.leave(full)
            for j in range(n_steps - RING * full):
                body(j, full)

        def base(layer):
            return Place(0, layer * (LAYER_CHUNKS // RING))

        def load_cols(sp, n, w, c0, width):
            dst = raw[n.slot][:, 0:KD * width].rearrange("p (k c) -> p k c", k=KD)
            src = w.rearrange("(k p) c -> p k c", p=P)
            h = KD // 2
            load(sp, n, [(dst[:, 0:h], src[:, 0:h, c0:c0 + width]), (dst[:, h:KD], src[:, h:KD, c0:c0 + width])])

        def load_rows(sp, n, w, r0):
            load(sp, n, [(raw[n.slot][:, D * j:D * j + D], w[bass.ds(r0 + j * P, P), :]) for j in range(2)])

        def load_ffn(sp, n0, w_gate, w_up, w_down, more=lambda down, j, turn: None):
            def up(j, turn):
                n = n0.at(j, turn)
                dst = raw[n.slot][:].rearrange("p (s k c) -> p s k c", s=2, k=KD)
                load(sp, n, [(dst[:, s], w.rearrange("(k p) c -> p k c", p=P)[:, :, bass.ds(turn * (RING * P) + j * P, P)])
                             for s, w in enumerate((w_gate, w_up))])
                more(False, j, turn)
            by_threes(sp, UP_CHUNKS, up)

            def down(j, turn):
                load_rows(sp, n0.at(UP_CHUNKS + j, turn), w_down, turn * (2 * RING * P) + 2 * j * P)
                more(True, j, turn)
            by_threes(sp, DOWN_CHUNKS, down)

        def one(ap, layer):
            return ap[bass.ds(layer, 1)].squeeze(0)

        def load_mixer_vectors(eng, layer):
            rows = lambda n: one(a[n], layer).rearrange("(r p) -> r p", p=P)
            for r0, name, k in ((R_MIX_PRE, "norm_mix_pre", 8), (R_MIX_POST, "norm_mix_post", 8),
                                (R_FFN_PRE, "norm_ffn_pre", 8), (R_FFN_POST, "norm_ffn_post", 8),
                                (R_DWB, "conv_dw_b", 2), (R_CLG, "conv_ln_g", 2), (R_CLB, "conv_ln_b", 2),
                                (R_PSC, "pool_scale", 2)):
                eng.dma_start(vrow[r0:r0 + k, :], rows(name)).then_inc(s_par, 16)
            eng.dma_start(vrow[R_DW:R_DW + 62, :], one(a["conv_dw_w"], layer).rearrange("k (b p) -> (k b) p", p=P)).then_inc(s_par, 16)
            eng.dma_start(vrow[R_SGB:R_SGB + 4, :], one(a["sgu_b"], layer)).then_inc(s_par, 16)
            eng.dma_start(perow[:, 0:64], one(a["nsa_pe_k"], layer)).then_inc(s_par, 16)
            eng.dma_start(perow[:, 64:128], one(a["nsa_pe_v"], layer)).then_inc(s_par, 16)

        def load_gate_weights(eng, layer):
            for j, name in enumerate(("sgu_ln_g", "sgu_ln_b")):
                eng.dma_start(sgln[:, j, :], a[name][bass.ds(layer, 1), :].broadcast_to([P, T])).then_inc(s_parw, 16)
            eng.dma_start(wsp[:], one(a["sgu_w"], layer).rearrange("g t s -> t g s")).then_inc(s_parw, 16)
            for g in range(4):
                eng.dma_start(bsp[64 * (g % 2):64 * (g % 2) + 64, g // 2, :],
                             one(a["sgu_b"], layer)[g:g + 1, :].broadcast_to([64, P])).then_inc(s_parw, 16)

        def load_mixer_weights(eng, layer):
            for h, name in enumerate(("nsa_ck_w1", "nsa_cv_w1")):
                eng.dma_start(cw1[64 * h:64 * h + 64, :, :],
                             one(a[name], layer).rearrange("(l d) e -> d l e", d=64)).then_inc(s_parw, 16)
            eng.dma_start(cw2[0:64, 0:64], one(a["nsa_ck_w2"], layer)).then_inc(s_parw, 16)
            eng.dma_start(cw2[0:64, 64:128], one(a["nsa_ck_w2"], layer)).then_inc(s_parw, 16)
            eng.dma_start(cw2[64:128, 128:192], one(a["nsa_cv_w2"], layer)).then_inc(s_parw, 16)
            for g in range(4):
                h = 64 * (g % 2)
                eng.dma_start(pw[h:h + 64, g // 2, h:h + 64],
                             a["pool_w"][bass.ds(layer, 1), g].squeeze(0)).then_inc(s_parw, 16)
        N_PAR, N_PARW = 12 * 16, 16 * 16

        def load_ffn_params(eng, layer):
            rows = one(a["ffn_conv_w"], layer).rearrange("k (b p) -> k b p", p=P)
            eng.dma_start(frow[0:44, 0, :], rows[0]).then_inc(s_fpar, 16)
            eng.dma_start(frow[44:88, 0, :], rows[1]).then_inc(s_fpar, 16)
            eng.dma_start(frow[0:44, 1, :], rows[2]).then_inc(s_fpar, 16)
            eng.dma_start(frow[44:88, 1, :], one(a["ffn_conv_b"], layer).rearrange("(b p) -> b p", p=P)).then_inc(s_fpar, 16)
        N_FPAR = 4 * 16

        PRE = lambda c: 2 * c if c <= 5 else 2 * c - 1
        POST = lambda c: 2 * c + 1 if c <= 4 else 2 * c + 2

        def sum_step(k):
            return mm(misc[:, 0:T], K["ones"], work[:, k, :], start=(k == 0), stop=(k == KD - 1), skip_group_check=True)

        def root_act(act, c):
            act.wait_ge(e_ss.sem, e_ss.after(c))
            nc.scalar.activation(root[:], misc[:, 0:T], ACT.Sqrt, bias=K["eps6"], scale=1.0 / D).then_inc(e_rt.sem, 1)

        def rstd_dve(dve, st, c):
            dve.wait_ge(e_rt.sem, e_rt.after(c))
            st(dve.reciprocal(rstd[:], root[:]))

        def pre_pe(pe, c):
            for k in range(KD):
                pe.wait_ge(e_sq.sem, e_sq.after(c, k + 1))
                i = sum_step(k)
            i.then_inc(e_ss.sem, 1)

        def pre_act(act, c, x, x_ready, shift=None, between=None):
            for k in range(KD):
                x_ready(act, k)
                nc.scalar.activation(work[:, k, :], x[:, k, :], ACT.Square).then_inc(e_sq.sem, 1)
            if between:
                between()
            root_act(act, PRE(c))
            for k in range(KD):
                act.wait_ge(e_nv.sem, e_nv.after(c, k + 1))
                if shift:
                    i = nc.scalar.activation(hhi[:, k, :], work[:, k, :], ACT.Identity, bias=shift(k))
                else:
                    i = nc.scalar.activation(hhi[:, k, :], work[:, k, :], ACT.Copy)
                i.then_inc(e_nh.sem, 1)

        def pre_dve(dve, st, c, x, gain, shift=None):
            rstd_dve(dve, st, PRE(c))
            for k in range(KD + 1):
                if k < KD:
                    dve.scalar_tensor_tensor(out=work[:, k, :], in0=x[:, k, :], scalar=gain(k), in1=rstd[:],
                                             op0=ALU.mult, op1=ALU.mult).then_inc(e_nv.sem, 1)
                if k == 0:
                    continue
                dve.wait_ge(e_nh.sem, e_nh.after(c, k))
                if shift:
                    i = dve.scalar_tensor_tensor(out=hlo[:, k - 1, :], in0=work[:, k - 1, :], scalar=shift(k - 1),
                                                 in1=hhi[:, k - 1, :].bitcast(F32), op0=ALU.add, op1=ALU.subtract)
                else:
                    i = dve.tensor_tensor(hlo[:, k - 1, :], work[:, k - 1, :], hhi[:, k - 1, :].bitcast(F32), ALU.subtract)
                i.then_inc(e_h.sem, 1)

        def post_sums(pe, c, b):
            pe.wait_ge(e_psq.sem, e_psq.after(c, b + 1))
            for k in (2 * b, 2 * b + 1):
                i = sum_step(k)
            if b == 3:
                i.then_inc(e_ss.sem, 1)

        def post_act(act, c, used):
            for b in range(4):
                if b < 3:
                    act.wait_ge(e_bk.sem, e_bk.after(c, b + 1))
                else:
                    act.wait_ge(s_used, used)
                nc.scalar.activation(work[:, 2 * b:2 * b + 2, :], acc[:, b, :].rearrange("p (k t) -> p k t", k=2),
                                     ACT.Square).then_inc(e_psq.sem, 1)
            root_act(act, POST(c))

        def post_dve(dve, st, c, gain, x):
            rstd_dve(dve, st, POST(c))

            def add(k):
                dve.tensor_tensor(x[:, k, :], x[:, k, :], work[:, k, :], ALU.add).then_inc(e_xo.sem, 1)
            for k in range(KD):
                i = dve.scalar_tensor_tensor(out=work[:, k, :], in0=acc[:, k // 2, (k % 2) * T:(k % 2) * T + T],
                                             scalar=gain(k), in1=rstd[:], op0=ALU.mult, op1=ALU.mult)
                if k % 2:
                    st(i)
                    add(k)
                else:
                    i.then_inc(e_pt.sem, 1)

        def post_pool(pool, c, x):
            for k in range(0, KD, 2):
                pool.wait_ge(e_pt.sem, e_pt.after(c, k // 2 + 1))
                pool.tensor_tensor(x[:, k, :], x[:, k, :], work[:, k, :], ALU.add).then_inc(e_xe.sem, 1)

        def x_updated(eng, c, k=KD - 1):
            eng.wait_ge(e_xe.sem, e_xe.after(c, k // 2 + 1))
            if k > 0:
                eng.wait_ge(e_xo.sem, e_xo.after(c, (k + 1) // 2))

        def after_post(c):
            return lambda eng, k: x_updated(eng, c, k)

        def cols_pe(pe, n, out_, blocks, first_k=None, width=256, offs=(0, P)):
            w = [t[:, 0:KD * width].rearrange("p (k c) -> p k c", k=KD) for t in ring(n)]
            pe.wait_ge(s_lo, n.count(1))
            pe.wait_ge(s_lop, n.count(1))
            for b in range(blocks):
                for k in range(KD):
                    if first_k and b == 0:
                        first_k(k)
                    i = mm3(out_[:, b * T:(b + 1) * T], [t[:, k, offs[b]:offs[b] + P] for t in w], hhi[:, k, :],
                            hlo[:, k, :], k == 0, k == KD - 1)
            i.then_inc(s_used, 1)
            return i

        def rows_pe(pe, n, xh, xl, first, post, half_ready):
            last = post is not None
            w = [t[:].rearrange("p (j m) -> p j m", j=2) for t in ring(n)]
            pe.wait_ge(s_lo, n.count(1))
            pe.wait_ge(s_lop, n.count(1))
            for j in range(2):
                half_ready(j)
                for m in range(KD):
                    i = mm3(acc[:, m // 2, (m % 2) * T:(m % 2) * T + T], [t[:, j, m * P:(m + 1) * P] for t in w],
                            xh(j), xl(j), first and j == 0 and m % 2 == 0, last and j == 1)
                    if last and j == 1 and m % 2:
                        i.then_inc(e_bk.sem if m < KD - 1 else s_used, 1)
                        if m > 1:
                            post_sums(pe, post, m // 2 - 1)
            if last:
                post_sums(pe, post, 3)
            else:
                i.then_inc(s_used, 1)

        def ffn_pe(pe, f, n0, post, more=lambda down, j, turn: None, before_sums=lambda: None):
            def up(j, turn):
                n = n0.at(j, turn)
                static = isinstance(turn, int) and turn == 0
                if not static:
                    pe.wait_ge(e_cv.sem, f * FB + turn * RING + (j + 1 - RING))
                w = [t[:].rearrange("p (s k c) -> p s k c", s=2, k=KD) for t in ring(n)]
                pe.wait_ge(s_lo, n.count(1))
                pe.wait_ge(s_lop, n.count(1))
                for s in range(2):
                    for k in range(KD):
                        if static and j == 0 and s == 0:
                            pe.wait_ge(e_h.sem, e_h.after(PRE_OF(f), k + 1))
                        i = mm3(lin[:, n.slot, s * T:(s + 1) * T], [t[:, s, k, :] for t in w], hhi[:, k, :],
                                hlo[:, k, :], k == 0, k == KD - 1)
                i.then_inc(s_used, 1)
                more(False, j, turn)
            by_threes(pe, UP_CHUNKS, up)

            def down(j, turn):
                n = n0.at(UP_CHUNKS + j, turn)
                first = isinstance(turn, int) and turn == 0 and j == 0
                last = isinstance(turn, int) and 3 * turn + j == DOWN_CHUNKS - 1
                blk = turn * (2 * RING) + 2 * j
                more(True, j, turn)
                if last:
                    before_sums()
                rows_pe(pe, n, lambda h: ahi[:, bass.ds(blk + h, 1), :].squeeze(1),
                            lambda h: alo[:, bass.ds(blk + h, 1), :].squeeze(1), first, post if last else None,
                            lambda h: pe.wait_ge(e_al.sem, f * FB + (blk + h) + 1))
            by_threes(pe, DOWN_CHUNKS, down)

        def ffn1_act(act, f, n0):
            def gelu(i, slot):
                act.wait_ge(e_cv.sem, f * FB + i + 1)
                nc.scalar.activation(gel[:, slot, :], taps[:, slot, 0, :], ACT.Gelu_apprx_tanh).then_inc(e_gl.sem, 1)

            def high(i, slot):
                act.wait_ge(e_pr.sem, f * FB + i + 1)
                nc.scalar.activation(ahi[:, bass.ds(i, 1), :].squeeze(1), prod[:, slot, :], ACT.Copy).then_inc(e_ah.sem, 1)

            def step(j, turn):
                i = turn * RING + j
                static = isinstance(turn, int)
                if not (static and turn == 0 and j < 2):
                    high(i - 2, (j - 2) % RING)
                if not (static and turn == 0 and j < 1):
                    gelu(i - 1, (j - 1) % RING)
                split_high(act, n0.at(j + 2, turn))
                act.wait_ge(s_used, n0.count(j + 1) + turn * RING)
                if not (static and turn == 0):
                    act.wait_ge(e_al.sem, f * FB + i - 2)
                slot = n0.at(j).slot
                for s in range(2):
                    b = i + s * FB
                    nc.scalar.activation(taps[:, j, s, :], lin[:, slot, s * T:(s + 1) * T], ACT.Identity,
                                         bias=fcol[:, 1, bass.ds(b + 44, 1)], scale=fcol[:, 1, bass.ds(b, 1)])\
                        .then_inc(e_c0.sem, 1) if s else \
                        nc.scalar.activation(taps[:, j, s, :], lin[:, slot, s * T:(s + 1) * T], ACT.Identity,
                                             bias=fcol[:, 1, bass.ds(b + 44, 1)], scale=fcol[:, 1, bass.ds(b, 1)])
            by_threes(act, UP_CHUNKS, step)
            high(FB - 2, (FB - 2) % RING)
            gelu(FB - 1, (FB - 1) % RING)
            high(FB - 1, (FB - 1) % RING)

        def ffn1_dve(dve, st, f, n0):
            def step(j, turn):
                i = turn * RING + j
                split_low(dve, n0.at(j + 2, turn))
                dve.wait_ge(e_c0.sem, f * FB + i + 1)
                slot = n0.at(j).slot
                for tap in (1, 0):
                    d = 2 - tap
                    for s in range(2):
                        ins = dve.scalar_tensor_tensor(
                            out=taps[:, j, s, d:T], in0=lin[:, slot, s * T:(s + 1) * T - d],
                            scalar=fcol[:, 0, bass.ds(i + (s * FB + 44 * tap), 1)], in1=taps[:, j, s, d:T],
                            op0=ALU.mult, op1=ALU.add)
                    if tap:
                        st(ins)
                    else:
                        ins.then_inc(e_cv.sem, 1)
            by_threes(dve, UP_CHUNKS, step, st, RING)

        def ffn1_pool(pool, f, n0):
            def product(i, slot):
                pool.wait_ge(e_gl.sem, f * FB + i + 1)
                pool.tensor_tensor(prod[:, slot, :], gel[:, slot, :], taps[:, slot, 1, :], ALU.mult).then_inc(e_pr.sem, 1)

            def low(i, slot):
                pool.wait_ge(e_ah.sem, f * FB + i + 1)
                pool.tensor_tensor(alo[:, bass.ds(i, 1), :].squeeze(1), prod[:, slot, :],
                                   ahi[:, bass.ds(i, 1), :].squeeze(1).bitcast(F32), ALU.subtract).then_inc(e_al.sem, 1)

            def step(j, turn):
                i = turn * RING + j
                split_low(pool, n0.at(j + 2, turn))
                if not (isinstance(turn, int) and turn == 0 and j < 2):
                    low(i - 2, (j - 2) % RING)
                if not (isinstance(turn, int) and turn == 0 and j < 1):
                    product(i - 1, (j - 1) % RING)
            by_threes(pool, UP_CHUNKS, step)
            low(FB - 2, (FB - 2) % RING)
            product(FB - 1, (FB - 1) % RING)
            low(FB - 1, (FB - 1) % RING)

        def ffn2_act(act, f, n0):
            def high(i, slot):
                act.wait_ge(e_cv.sem, f * FB + i + 1)
                nc.scalar.activation(ahi[:, bass.ds(i, 1), :].squeeze(1), prod[:, slot, :], ACT.Copy).then_inc(e_ah.sem, 1)

            def step(j, turn):
                i = turn * RING + j
                split_high(act, n0.at(j + 2, turn))
                if not (isinstance(turn, int) and turn == 0 and j == 0):
                    high(i - 1, (j - 1) % RING)
                act.wait_ge(s_used, n0.count(j + 1) + turn * RING)
                if not (isinstance(turn, int) and turn == 0):
                    act.wait_ge(e_al.sem, f * FB + i - 2)
                nc.scalar.activation(gel[:, j, :], lin[:, n0.at(j).slot, 0:T], ACT.Silu).then_inc(e_sg.sem, 1)
            by_threes(act, UP_CHUNKS, step)
            high(FB - 1, (FB - 1) % RING)

        def ffn2_dve(dve, f, n0):
            def step(j, turn):
                split_low(dve, n0.at(j + 2, turn))
                dve.wait_ge(e_sg.sem, (f - LAYERS) * FB + turn * RING + (j + 1))
                dve.tensor_tensor(prod[:, j, :], gel[:, j, :], lin[:, n0.at(j).slot, T:2 * T], ALU.mult).then_inc(e_cv.sem, 1)
            by_threes(dve, UP_CHUNKS, step)

        def ffn2_pool(pool, f, n0):
            def low(i, slot):
                pool.wait_ge(e_ah.sem, f * FB + i + 1)
                pool.tensor_tensor(alo[:, bass.ds(i, 1), :].squeeze(1), prod[:, slot, :],
                                   ahi[:, bass.ds(i, 1), :].squeeze(1).bitcast(F32), ALU.subtract).then_inc(e_al.sem, 1)

            def step(j, turn):
                i = turn * RING + j
                split_low(pool, n0.at(j + 2, turn))
                if not (isinstance(turn, int) and turn == 0 and j == 0):
                    low(i - 1, (j - 1) % RING)
            by_threes(pool, UP_CHUNKS, step)
            low(FB - 1, (FB - 1) % RING)

        def down_split(eng, n0, split, after=2, first_steps=None):
            def step(j, turn):
                static = isinstance(turn, int)
                if not (static and RING * turn + j + 2 >= DOWN_CHUNKS + after):
                    split(eng, n0.at(UP_CHUNKS + j + 2, turn))
                if first_steps and static and turn == 0:
                    first_steps(j)
            by_threes(eng, DOWN_CHUNKS, step)

        PRE_OF = lambda f: 2 * f + 1 if f < LAYERS else 2 * f

        turn_bank = lambda c, q: lin[:, q + 1, :] if c and q < 2 else acc[:, q, :]

        def turn_in_pe(pe, c, x):
            for q in range(4):
                if c and q == 2:
                    x_updated(pe, 2 * LAYERS - 1)
                for k in (2 * q, 2 * q + 1):
                    for t in range(2):
                        o = (k % 2) * T + t * P
                        i = pe.transpose(turn_bank(c, q)[:, o:o + P], x(t)[:, k * P:(k + 1) * P], K["ident"])
                i.then_inc(e_xt.sem, 1)

        def turn_in_dve(dve, c, xt):
            for q in range(4):
                dve.wait_ge(e_xt.sem, e_xt.after(c, q + 1))
                dve.tensor_copy(xt[:, 2 * q:2 * q + 2, :], turn_bank(c, q).rearrange("p (k t) -> p k t", k=2)).then_inc(e_xc.sem, 1)

        def cat_pe(pe, L, n, pos, first, last):
            pair = OUT1_ORDER[pos]
            pe.wait_ge(m_cal.sem, m_cal.after(L, pos + 1))
            rows_pe(pe, n, lambda h: hhi[:, 2 * pair + h, :], lambda h: hlo[:, 2 * pair + h, :], first, 2 * L if last else None,
                    lambda h: None)

        def heads(h):
            return slice(64 * (h % 2), 64 * (h % 2) + 64), h // 2

        ROUNDS = ((0, 0, "acc", 0), (1, 0, "acc", 1), (0, 1, "acc", 2), (1, 1, "acc", 2))

        def round_scores(r):
            branch, tb, where, b = ROUNDS[r]
            keys = (tb + 1) * P
            t = acc if where == "acc" else lin
            if tb == 0:
                return t[:, b, :].rearrange("p (h k) -> p h k", h=4)
            return t[:, b:b + 2, :].rearrange("p b (h k) -> p (b h) k", h=2)

        def mixer1_pe(pe, st, L, n0):
            if not L:
                pe.wait_ge(s_tab1, 16)
            pe.wait_ge(s_par, L * N_PAR + N_PAR)
            pe.wait_ge(s_fpar, L * N_FPAR + N_FPAR)
            pe.transpose(lin[:, 0, 0:R_ROWS], vrow[:], K["ident"][0:R_ROWS, 0:R_ROWS])
            pe.transpose(lin[:, 0, 128:160], perow[:], K["ident"][0:32, 0:32])
            for j in range(2):
                i = pe.transpose(lin[:, 0, 256 + 88 * j:256 + 88 * j + 88], frow[:, j, :], K["ident"][0:88, 0:88])
            i.then_inc(e_vt.sem, 1)
            pre_pe(pe, 2 * L)
            pe.wait_ge(e_vc.sem, e_vc.after(L))

            def project(j):
                if j >= RING:
                    pe.wait_ge(m_ev.sem, m_ev.after(L, j + 1 - RING))
                n = n0.at(j)
                width, offs = (140, (0, 12)) if j == 2 else (256, (0, P))
                cols_pe(pe, n, lin[:, n.slot, :], 2,
                        (lambda k: pe.wait_ge(e_h.sem, e_h.after(2 * L, k + 1))) if j == 0 else None, width, offs)

            def scores(r):
                branch, tb, _, _ = ROUNDS[r]
                s = round_scores(r)
                for h in (0, 2, 1, 3):
                    ps, hp = heads(h)
                    i = mm(s[:, h, :], qrot[ps, hp, tb * P:(tb + 1) * P], krot[ps, branch, 0:(tb + 1) * P])
                    if h == 2:
                        st(i)
                i.then_inc(m_sc.sem, 1)

            blk = 0

            def turn(r):
                nonlocal blk
                branch, tb, _, _ = ROUNDS[r]
                pe.wait_ge(m_pb.sem, m_pb.after(L, r + 1))
                for kb in range(tb + 1):
                    if blk >= 2:
                        pe.wait_ge(m_pc.sem, m_pc.after(L, blk - 1))
                    for h in range(HEADS1):
                        i = pe.transpose(acc[:, blk % 2, h * P:(h + 1) * P], prob[:, h, kb * P:(kb + 1) * P], K["ident"])
                    i.then_inc(m_pt.sem, 1)
                    blk += 1

            for j in range(4):
                project(j)
            pe.wait_ge(m_ev.sem, m_ev.after(L, 3))
            for j in range(2):
                mm(acc[:, 0, j * T:(j + 1) * T], K["rope_turn"], qT[:, j, :])
            for b in range(2):
                mm(acc[:, 1, b * T:(b + 1) * T], K["twice"][0:64, :], kvT[0:64, 1 + b, :])
                i = mm(acc[:, 2, b * T:(b + 1) * T], K["twice_turn"][0:64, :], kvT[0:64, 1 + b, :])
            i.then_inc(m_rope.sem, 1)
            for b in range(3):
                for t in range(2):
                    o = (2 * b + t) * P
                    dst = acc[:, 3, o:o + P] if b < 2 else misc[:, t * P:(t + 1) * P]
                    i = pe.transpose(dst, kvT[:, 1 + b, t * P:(t + 1) * P], K["ident"])
            i.then_inc(m_tr.sem, 1)
            project(4)
            pe.wait_ge(m_cb.sem, m_cb.after(L))
            pe.wait_ge(s_parw, L * N_PARW + N_PARW)
            pe.wait_ge(m_vt.sem, m_vt.after(L))
            for h in range(2):
                for l in range(32):
                    q = slice(64 * h, 64 * h + 64)
                    i = mm(misc[q, 256:256 + N_CMP], cw1[q, l, :], cbuf[q, l, :], start=(l == 0), stop=(l == 31))
            i.then_inc(m_hid.sem, 1)
            pe.wait_ge(m_qk.sem, m_qk.after(L))
            scores(0)
            scores(1)
            project(5)
            pe.wait_ge(m_hg.sem, m_hg.after(L))
            st(mm(misc[:, 272:272 + N_CMP], cw2[0:64, 0:P], hid[0:64, 0:N_CMP]))
            mm(misc[0:N_CMP, 288:352], hid[64:128, 0:N_CMP], cw2[64:128, 128:192]).then_inc(m_kc.sem, 1)
            scores(2)
            pe.wait_ge(m_kcc.sem, m_kcc.after(L))
            for odd in range(2):
                for t in range(2):
                    for h in (odd, 2 + odd):
                        ps, hp = heads(h)
                        o = (t * 4 + h) * 16
                        i = mm(misc[:, o:o + N_CMP], qT[ps, hp, t * P:(t + 1) * P], kc[ps, 0:N_CMP])
                if not odd:
                    st(i)
            i.then_inc(m_cmp.sem, 1)
            turn(0)
            project(6)
            turn(1)
            pe.wait_ge(m_mx.sem, m_mx.after(L, 3))
            scores(3)
            turn(2)
            project(7)
            pe.wait_ge(m_ev.sem, m_ev.after(L, 7))
            for t in range(2):
                for b in range(2):
                    i = pe.transpose(lin[:, 2, t * T + b * P:t * T + (b + 1) * P], vT[:, b, t * P:(t + 1) * P], K["ident"])
            i.then_inc(m_vx.sem, 1)
            for g in range(4):
                i = pe.transpose(lin[:, 0, g * P:(g + 1) * P], wsp[:, g, :], K["ident"])
            i.then_inc(m_vx.sem, 1)
            turn(3)
            pe.wait_ge(m_pcr.sem, m_pcr.after(L))
            for t in range(2):
                pe.wait_ge(m_pc.sem, m_pc.after(L, 5 + t))
                for h in range(HEADS1):
                    i = pe.transpose(acc[0:N_CMP, t, h * P:(h + 1) * P], probc[:, t * 4 + h, 0:N_CMP], K["ident"])
                i.then_inc(m_pt.sem, 1)
            pe.wait_ge(m_pc.sem, m_pc.after(L, 8))
            for t in range(2):
                for h in range(HEADS1):
                    ps, hp = heads(h)
                    dst = acc[ps, 2, hp * T + t * P:hp * T + (t + 1) * P]
                    mm(dst, vc[:], pcT[0:N_CMP, t * 4 + h, :], start=True, stop=False)
                    for branch in range(2):
                        for kb in range(t + 1):
                            b = BLK[(branch, kb, t)]
                            i = mm(dst, vtok[:, 2 * branch + kb, :], pT[:, b, h, :], start=False,
                                   stop=(branch == 1 and kb == t))
            i.then_inc(m_o.sem, 1)
            pe.wait_ge(m_ws.sem, m_ws.after(L))
            pe.wait_ge(m_vw.sem, m_vw.after(L))
            for g in range(4):
                for t in range(2):
                    i = mm(acc[64 * (g % 2):64 * (g % 2) + 64, 3, (g // 2) * T + t * P:(g // 2) * T + (t + 1) * P],
                           vn[:, t, 64 * g:64 * g + 64], wspT[:, g, :])
            i.then_inc(m_f.sem, 1)
            pe.wait_ge(m_pl.sem, m_pl.after(L))
            for b in range(2):
                i = mm(lin[:, 0, b * T:(b + 1) * T], pw[:, b, :], pooled[:, b, :])
            i.then_inc(m_pm.sem, 1)
            pe.wait_ge(m_cy.sem, m_cy.after(L))
            for b in range(2):
                i = mm(misc[:, 0:T], K["ones"], convy[:, b, :], start=(b == 0), stop=(b == 1))
            i.then_inc(m_cs.sem, 1)
            pe.wait_ge(m_csg.sem, m_csg.after(L))
            pe.wait_ge(m_cns.sem, m_cns.after(L))
            for p in range(OUT_CHUNKS):
                cat_pe(pe, L, n0.at(MIX1_CHUNKS + p), p, p == 0, p == OUT_CHUNKS - 1)
                if p == 0:
                    pe.wait_ge(m_cq.sem, m_cq.after(L))
                    for b in range(2):
                        i = mm(misc[:, T:2 * T], K["ones"], sig[:, b, :], start=(b == 0), stop=(b == 1))
                    i.then_inc(m_cs.sem, 1)

        BLK = {(0, 0, 0): 0, (1, 0, 0): 1, (0, 0, 1): 2, (0, 1, 1): 3, (1, 0, 1): 4, (1, 1, 1): 5}
        m_cmp = event("compressed_scores", 1)
        m_cmx = event("compressed_maxima", 1)
        m_cex = event("compressed_exponentials", 1)
        m_pcr = event("compressed_probabilities", 1)

        def mixer1_act(act, st, L, n0):
            def split(j):
                split_high(act, n0.at(j + 2), 1120 if j + 2 == 2 else CHUNK)

            def take(j):
                act.wait_ge(s_used, n0.count(j + 1))
                src = lin[:, n0.at(j).slot, :].rearrange("p (b t) -> p b t", b=2)
                dst, fn = ((qT[:], ACT.Copy), (kvT[:, 0:2, :], ACT.Copy), (kvT[:, 2:4, :], ACT.Copy), (aT[:], ACT.Copy),
                           (sig[:], ACT.Sigmoid), (uT[:], ACT.Gelu_apprx_tanh), (vT[:], ACT.Gelu_apprx_tanh),
                           (zpad[:, :, 16:16 + T], ACT.Copy))[j]
                nc.scalar.activation(dst, src, fn).then_inc(m_ev.sem, 1)

            blk = 0

            def copies(count):
                nonlocal blk
                for _ in range(count):
                    act.wait_ge(m_pt.sem, m_pt.after(L, blk + 1))
                    nc.scalar.activation(pT[:, blk, :, :], acc[:, blk % 2, :].rearrange("p (h k) -> p h k", h=4),
                                         ACT.Copy).then_inc(m_pc.sem, 1)
                    blk += 1

            def exponentials(r):
                keys = (ROUNDS[r][1] + 1) * P
                act.wait_ge(m_mx.sem, m_mx.after(L, r + 1))
                if r:
                    act.wait_ge(m_pb.sem, m_pb.after(L, r))
                    act.wait_ge(m_pt.sem, m_pt.after(L, (0, 1, 2, 4)[r]))
                for h in range(HEADS1):
                    i = nc.scalar.activation(prob[:, h, 0:keys], sc[:, h, 0:keys], ACT.Exp, bias=mx[:, h:h + 1],
                                             accum_out=sm[:, h:h + 1])
                i.then_inc(m_ex.sem, 1)

            for j in range(4):
                split(j)
                take(j)
            act.wait_ge(m_tr.sem, m_tr.after(L))
            nc.scalar.activation(vtok[:], acc[:, 3, :].rearrange("p (b c) -> p b c", b=4)[:, :, 64:128], ACT.Copy)
            nc.scalar.activation(gates[:], misc[:, 0:2 * P].rearrange("p (t c) -> p t c", t=2)[:, :, 116:128],
                                 ACT.Sigmoid).then_inc(m_vt.sem, 1)
            split(4)
            take(4)
            act.wait_ge(m_hid.sem, m_hid.after(L))
            nc.scalar.activation(hid[:, 0:N_CMP], misc[:, 256:256 + N_CMP], ACT.Gelu_apprx_tanh).then_inc(m_hg.sem, 1)
            split(5)
            exponentials(0)
            take(5)
            act.wait_ge(m_kc.sem, m_kc.after(L))
            nc.scalar.activation(kc[:, 0:N_CMP], misc[:, 272:272 + N_CMP], ACT.Copy)
            nc.scalar.activation(vc[:], misc[0:N_CMP, 288:352], ACT.Copy).then_inc(m_kcc.sem, 1)
            copies(1)
            exponentials(1)
            split(6)
            take(6)
            copies(1)
            exponentials(2)
            act.wait_ge(m_cmx.sem, m_cmx.after(L))
            nc.scalar.activation(probc[:, :, 0:N_CMP], scc[:, :, 0:N_CMP], ACT.Exp).then_inc(m_cex.sem, 1)
            copies(2)
            split(7)
            exponentials(3)
            take(7)
            split_high(act, n0.at(MIX1_CHUNKS + 2))
            copies(2)
            act.wait_ge(m_bn.sem, m_bn.after(L))
            nc.scalar.activation(srt[:, 0:2], mv[:, :, 1], ACT.Sqrt, bias=K["eps5"]).then_inc(m_br.sem, 1)
            for t in range(2):
                act.wait_ge(m_pt.sem, m_pt.after(L, 7 + t))
                nc.scalar.activation(pcT[0:N_CMP, 4 * t:4 * t + 4, :], acc[0:N_CMP, t, :].rearrange("p (h k) -> p h k", h=4),
                                     ACT.Copy).then_inc(m_pc.sem, 1)
            act.wait_ge(m_pm.sem, m_pm.after(L))
            for b in range(2):
                i = nc.scalar.activation(work[:, 6 + b, :], lin[:, 0, b * T:(b + 1) * T], ACT.Copy,
                                         scale=vcol[:, R_PSC + b:R_PSC + b + 1])
            i.then_inc(m_cpool.sem, 1)
            for pos in range(3):
                done = (m_cpool, m_csg, m_cns)[pos]
                act.wait_ge(done.sem, done.after(L))
                p = OUT1_ORDER[pos]
                nc.scalar.activation(hhi[:, 2 * p:2 * p + 2, :], work[:, 2 * p:2 * p + 2, :], ACT.Copy).then_inc(m_cah.sem, 1)
            act.wait_ge(m_cc.sem, m_cc.after(L))
            nc.scalar.activation(sig[:], convy[:], ACT.Square).then_inc(m_cq.sem, 1)
            split_high(act, n0.at(MIX1_CHUNKS + 3))
            act.wait_ge(m_cs.sem, m_cs.after(L, 2))
            nc.scalar.activation(croot[:], misc[:, T:2 * T], ACT.Sqrt, bias=K["eps5"], scale=1.0 / T).then_inc(m_cr.sem, 1)
            act.wait_ge(m_cn.sem, m_cn.after(L))
            for b in range(2):
                i = nc.scalar.activation(work[:, b, :], convy[:, b, :], ACT.Silu, bias=vcol[:, R_CLB + b:R_CLB + b + 1],
                                         scale=vcol[:, R_CLG + b:R_CLG + b + 1])
            st(i)
            nc.scalar.activation(hhi[:, 0:2, :], work[:, 0:2, :], ACT.Copy).then_inc(m_cah.sem, 1)
            for j in (4, 5):
                split_high(act, n0.at(MIX1_CHUNKS + j))

        m_cpool = event("pool_scaled", 1)

        def mixer1_dve(dve, st, L, n0):
            def low(j):
                split_low(dve, n0.at(j), 1120 if j == 2 else CHUNK)
            low(2)
            low(3)
            dve.wait_ge(m_ev.sem, m_ev.after(L, 2))
            src = kvT[:, 0, :].rearrange("p (n l) -> p l n", l=16)
            for half in range(2):
                i = dve.tensor_tensor(cbuf[:, 16 * half:16 * half + 16, :], src[:, :, half:half + N_CMP],
                                      pecol[:, 16 * half:16 * half + 16].unsqueeze(2).broadcast_to([P, 16, N_CMP]), ALU.add)
            i.then_inc(m_cb.sem, 1)
            low(4)
            low(5)
            dve.wait_ge(m_rope.sem, m_rope.after(L))
            cos = K["cos"].unsqueeze(1).broadcast_to([P, 2, T])
            sin = K["sin"].unsqueeze(1).broadcast_to([P, 2, T])
            bank = lambda b: acc[:, b, :].rearrange("p (j t) -> p j t", j=2)
            dve.scalar_tensor_tensor(out=qrot[:], in0=qT[:], scalar=0.125, in1=cos, op0=ALU.mult, op1=ALU.mult)
            st(dve.scalar_tensor_tensor(out=rt[:], in0=bank(0), scalar=0.125, in1=sin, op0=ALU.mult, op1=ALU.mult))
            dve.tensor_tensor(krot[:], bank(1), cos, ALU.mult)
            st(dve.tensor_tensor(qrot[:], qrot[:], rt[:], ALU.add))
            st(dve.tensor_tensor(rt[:], bank(2), sin, ALU.mult))
            dve.tensor_tensor(krot[:], krot[:], rt[:], ALU.add).then_inc(m_qk.sem, 1)
            low(6)
            dve.wait_ge(m_ev.sem, m_ev.after(L, 5))
            dve.tensor_tensor(glu[:, :, PAD:PAD + T], aT[:], sig[:], ALU.mult).then_inc(m_glu.sem, 1)
            dve.wait_ge(m_glu.sem, m_glu.after(L))
            def conv(t0, t1):
                for k in range(t0, t1):
                    for b in range(2):
                        w = vcol[:, R_DW + 2 * k + b:R_DW + 2 * k + b + 1]
                        if k == 0:
                            i = dve.tensor_scalar(convy[:, b, :], glu[:, b, 0:T], w, vcol[:, R_DWB + b:R_DWB + b + 1],
                                                  ALU.mult, ALU.add)
                        else:
                            i = dve.scalar_tensor_tensor(out=convy[:, b, :], in0=glu[:, b, k:k + T], scalar=w,
                                                         in1=convy[:, b, :], op0=ALU.mult, op1=ALU.add)
                    st(i)

            def low_branch(pos):
                p = OUT1_ORDER[pos]
                dve.wait_ge(m_cah.sem, m_cah.after(L, pos + 1))
                dve.tensor_tensor(hlo[:, 2 * p:2 * p + 2, :], work[:, 2 * p:2 * p + 2, :],
                                  hhi[:, 2 * p:2 * p + 2, :].bitcast(F32), ALU.subtract).then_inc(m_cal.sem, 1)

            def highest(r):
                branch, tb, _, _ = ROUNDS[r]
                keys = (tb + 1) * P
                dve.wait_ge(m_sc.sem, m_sc.after(L, r + 1))
                if r:
                    dve.wait_ge(m_pb.sem, m_pb.after(L, r))
                s = round_scores(r)
                bar = K["bar_le"].unsqueeze(1).broadcast_to([P, 4, P])
                if tb:
                    dve.tensor_copy(sc[:, :, 0:P], s[:, :, 0:P])
                st(dve.tensor_tensor(sc[:, :, tb * P:keys], s[:, :, tb * P:keys], bar, ALU.add))
                st(dve.tensor_reduce(mx[:, 4:8], sc[:, :, 0:keys], AX_X, ALU.max))
                dve.tensor_scalar(mx[:, 0:4], mx[:, 4:8], -1.0, None, ALU.mult).then_inc(m_mx.sem, 1)

            def probabilities(r):
                branch, tb, _, _ = ROUNDS[r]
                keys = (tb + 1) * P
                dve.wait_ge(m_ex.sem, m_ex.after(L, r + 1))
                st(dve.reciprocal(gs[:, 0:4], sm[:, 0:4]))
                g = gates[:, tb, :].rearrange("p (h b) -> p h b", b=3)[:, :, 1 + branch]
                st(dve.tensor_tensor(gs[:, 4:8], gs[:, 0:4], g, ALU.mult))
                dve.tensor_tensor(prob[:, :, 0:keys], prob[:, :, 0:keys],
                                  gs[:, 4:8].unsqueeze(2).broadcast_to([P, 4, keys]), ALU.mult).then_inc(m_pb.sem, 1)

            conv(0, 7)
            low(7)
            highest(0)
            conv(7, 12)
            probabilities(0)
            highest(1)
            conv(12, 15)
            probabilities(1)
            dve.wait_ge(m_cmp.sem, m_cmp.after(L))
            c8 = misc[:, 0:P].rearrange("p (r k) -> p r k", r=8)[:, :, 0:N_CMP]
            bar = K["cmp_bar"].rearrange("p (t k) -> p t k", t=2)[:, :, 0:N_CMP]
            for t in range(2):
                i = dve.scalar_tensor_tensor(out=scc[:, 4 * t:4 * t + 4, 0:N_CMP], in0=c8[:, 4 * t:4 * t + 4, :], scalar=0.125,
                                             in1=bar[:, t:t + 1, :].broadcast_to([P, 4, N_CMP]), op0=ALU.mult, op1=ALU.add)
            st(i)
            st(dve.tensor_reduce(mx[:], scc[:, :, 0:N_CMP], AX_X, ALU.max))
            dve.tensor_tensor(scc[:, :, 0:N_CMP], scc[:, :, 0:N_CMP], mx[:].unsqueeze(2).broadcast_to([P, 8, N_CMP]),
                              ALU.subtract).then_inc(m_cmx.sem, 1)
            low(8)
            highest(2)
            conv(15, 18)
            probabilities(2)
            highest(3)
            dve.wait_ge(m_cex.sem, m_cex.after(L))
            st(dve.tensor_reduce(smc[:], probc[:, :, 0:N_CMP], AX_X, ALU.add))
            st(dve.reciprocal(gs[:], smc[:]))
            g = gates[:].rearrange("p t (h b) -> p (t h) b", b=3)[:, :, 0]
            st(dve.tensor_tensor(gs[:], gs[:], g, ALU.mult))
            st(dve.tensor_tensor(probc[:, :, 0:N_CMP], probc[:, :, 0:N_CMP],
                                 gs[:].unsqueeze(2).broadcast_to([P, 8, N_CMP]), ALU.mult))
            seen = K["cmp_seen"].rearrange("p (t k) -> p t k", t=2)[:, :, 0:N_CMP]
            for t in range(2):
                i = dve.tensor_tensor(probc[:, 4 * t:4 * t + 4, 0:N_CMP], probc[:, 4 * t:4 * t + 4, 0:N_CMP],
                                      seen[:, t:t + 1, :].broadcast_to([P, 4, N_CMP]), ALU.mult)
            i.then_inc(m_pcr.sem, 1)
            low(9)
            conv(18, 22)
            probabilities(3)
            low(10)
            dve.wait_ge(m_vx.sem, m_vx.after(L, 1))
            for t in range(2):
                i = dve.bn_stats(bns[:, t, :], lin[:, 2, t * T:(t + 1) * T])
            st(i)
            for t in range(2):
                i = dve.bn_aggr(mv[:, t, :], bns[:, t, :])
            i.then_inc(m_bn.sem, 1)
            dve.wait_ge(m_vx.sem, m_vx.after(L, 2))
            dve.tensor_tensor(wspT[:], lin[:, 0, :].rearrange("p (g t) -> p g t", g=4),
                              K["col_ge"].unsqueeze(1).broadcast_to([P, 4, P]), ALU.mult).then_inc(m_ws.sem, 1)
            conv(22, 25)
            dve.wait_ge(m_br.sem, m_br.after(L))
            st(dve.reciprocal(srt[:, 2:4], srt[:, 0:2]))
            for t in range(2):
                i = dve.tensor_scalar(vn[:, t, :], lin[:, 2, t * T:(t + 1) * T], mv[:, t, 0:1], srt[:, 2 + t:3 + t],
                                      ALU.subtract, ALU.mult)
            i.then_inc(m_vn.sem, 1)
            conv(25, 31)
            dve.sem_inc(m_cy.sem, 1)
            dve.wait_ge(m_f.sem, m_f.after(L))
            f = acc[:, 3, :].rearrange("p (b t s) -> p b t s", b=2, t=2)
            for b in range(2):
                i = dve.tensor_tensor(work[:, 4 + b, :].rearrange("p (t s) -> p t s", t=2), f[:, b],
                                      bsp[:, b:b + 1, :].broadcast_to([P, 2, P]), ALU.add)
            st(i)
            dve.tensor_tensor(work[:, 4:6, :], work[:, 4:6, :], uT[:], ALU.mult).then_inc(m_csg.sem, 1)
            dve.wait_ge(m_o.sem, m_o.after(L))
            dve.tensor_copy(work[:, 2:4, :], acc[:, 2, :].rearrange("p (b t) -> p b t", b=2)).then_inc(m_cns.sem, 1)
            for pos in range(3):
                low_branch(pos)
            dve.wait_ge(m_cs.sem, m_cs.after(L, 1))
            dve.scalar_tensor_tensor(out=convy[:], in0=misc[:, 0:T].unsqueeze(1).broadcast_to([P, 2, T]), scalar=-1.0 / T,
                                     in1=convy[:], op0=ALU.mult, op1=ALU.add).then_inc(m_cc.sem, 1)
            low(11)
            dve.wait_ge(m_cr.sem, m_cr.after(L))
            st(dve.reciprocal(crstd[:], croot[:]))
            dve.tensor_tensor(convy[:], convy[:], crstd[:].unsqueeze(1).broadcast_to([P, 2, T]), ALU.mult).then_inc(m_cn.sem, 1)
            low_branch(3)
            low(12)
            low(13)

        def mixer1_pool(pool, st, L, n0):
            for j in range(2, MIX1_CHUNKS + 3):
                split_low(pool, n0.at(j), 1120 if j == 2 else CHUNK)
                if j == MIX1_CHUNKS + 2:
                    break
            pool.wait_ge(m_ev.sem, m_ev.after(L, 8))
            W = 16 + T
            for b in range(2):
                src = zpad[:, b, :]
                for s in range(2 * b + 2):
                    d = 1 << s
                    st(pool.tensor_tensor(psum2[:, s, d:W], src[:, d:W], src[:, 0:W - d], ALU.add))
                    src = psum2[:, s, :]
                for h in range(2):
                    q = slice(64 * h, 64 * h + 64)
                    i = pool.tensor_tensor(pooled[q, b, :], psum2[q, 2 * b + h, 16:W],
                                           K["inv_count"][q, b * T:(b + 1) * T], ALU.mult)
                st(i)
                i = pool.tensor_tensor(pooled[:, b, :], pooled[:, b, :], zpad[:, b, 16:W], ALU.subtract)
            i.then_inc(m_pl.sem, 1)
            pool.wait_ge(m_vn.sem, m_vn.after(L))
            pool.wait_ge(s_parw, L * N_PARW + N_PARW)
            st(pool.tensor_tensor(vn[:], vn[:], sgln[:, 0:1, :].broadcast_to([P, 2, T]), ALU.mult))
            pool.tensor_tensor(vn[:], vn[:], sgln[:, 1:2, :].broadcast_to([P, 2, T]), ALU.add).then_inc(m_vw.sem, 1)
            for j in range(3, 6):
                split_low(pool, n0.at(MIX1_CHUNKS + j))

        def ada_blocks(down, j, turn):
            first = isinstance(turn, int) and turn == 0
            if not down:
                return [(turn * RING + j, j)]
            if first:
                return [(UP_CHUNKS + 2 * j + h, (UP_CHUNKS + 2 * j + h) % RING) for h in range(2)]
            return [(turn * RING + (UP_CHUNKS + RING + j), (UP_CHUNKS + j) % RING)]

        def ada_load(sp, L, down, j, turn):
            for t, slot in ada_blocks(down, j, turn):
                if L or down or not (isinstance(turn, int) and turn == 0):
                    sp.wait_ge(e_ad.sem, L * ADA_LAYER + t + (1 - RING))
                sp.dma_start(ada[slot][:], a["ada_w_2"][0].rearrange("(k p) c -> p k c", p=P)
                             [:, :, bass.ds(t * P + L * ADA_LAYER * P, P)]).then_inc(s_ada[slot], 16)

        def ada_pe(pe, L, down, j, turn):
            for t, slot in ada_blocks(down, j, turn):
                rounds = turn + (UP_CHUNKS + RING + j) // RING if down and not (isinstance(turn, int) and turn == 0) \
                    else (t // RING if isinstance(turn, int) else turn)
                pe.wait_ge(s_ada[slot], (rounds + (L * ADA_LAYER // RING + 1)) * 16)
                for k in range(KD):
                    i = mm(misc[:, bass.ds(2 * t + T, 2)], ada[slot][:, k, :], csil[:, :, k], start=(k == 0), stop=(k == KD - 1))
                i.then_inc(e_ad.sem, 1)

        N_P2 = 18 * 16

        def load_second_params(eng, part):
            rows = lambda name: a[name].rearrange("o (r p) -> (o r) p", p=P)
            go = lambda dst, src: eng.dma_start(dst, src).then_inc(s_p2, 16)
            if part == 0:
                for j, name in enumerate(("ffn1_norm_pre_2", "ffn1_norm_post_2", "mix_norm_pre_2", "mix_norm_post_2",
                                          "ffn2_norm_pre_2", "ffn2_norm_post_2")):
                    go(xrow[8 * j:8 * j + 8, 0, :], rows(name))
            elif part == 1:
                go(tab2[:], a["tables_2"])
                go(xrow[V_SSDN:V_SSDN + 6, 0, :], rows("ssd_norm_2"))
                go(xrow[V_ADAB:V_ADAB + ADA_BLOCKS, 0, :], rows("ada_b_2"))
                go(xrow[V_CW:V_CW + 3 * CONV_BLOCKS, 1, :], a["conv_w_2"][0].rearrange("k (b p) -> (k b) p", p=P))
                go(xrow[V_CB:V_CB + CONV_BLOCKS, 1, :], rows("conv_b_2"))
                go(skip_all[:], a["d_skip_2"].broadcast_to([P, SSD_HEADS]))
            else:
                go(drow[:, 0, :], a["dt_bias_2"].rearrange("o d h -> o (d h)").broadcast_to([P, 24]))
                go(drow[:, 1, :], a["a_log_2"].rearrange("o d h -> o (d h)").broadcast_to([P, 24]))
                for h in range(4):
                    q = 64 * (h % 2)
                    go(fw[q:q + 64, h // 2, q:q + 64], a["fourier_w_2"][0, h])

        def second_start_pe(pe):
            pe.wait_ge(s_p2, N_P2)
            pe.transpose(lin[:, 0, 0:V_ROWS], xrow[0:V_ROWS, 0, :], K["ident"][0:V_ROWS, 0:V_ROWS])
            pe.transpose(lin[:, 0, P:P + V_ROWS2], xrow[0:V_ROWS2, 1, :], K["ident"][0:V_ROWS2, 0:V_ROWS2]).then_inc(t_vt.sem, 1)

        def second_start_dve(dve, st):
            dve.wait_ge(t_vt.sem, 1)
            dve.tensor_copy(xcol[:, 0, 0:V_ROWS], lin[:, 0, 0:V_ROWS])
            dve.tensor_copy(xcol[:, 1, 0:V_ROWS2], lin[:, 0, P:P + V_ROWS2]).then_inc(t_vc.sem, 1)
            dve.wait_ge(t_vc.sem, 1)
            st(dve.tensor_tensor(mod[:], mod[:], xcol[:, 0, V_ADAB:V_ADAB + ADA_BLOCKS].unsqueeze(2).broadcast_to([P, ADA_BLOCKS, 2]), ALU.add))
            for g, (who, stage) in enumerate(((1, 0), (1, 1), (0, 0), (0, 1), (0, 2))):
                dve.scalar_tensor_tensor(out=gain2[:, g, :], in0=mod[:, (3 * stage + 1) * KD:(3 * stage + 2) * KD, who], scalar=1.0,
                                         in1=xcol[:, 0, 16 * stage:16 * stage + 8], op0=ALU.add, op1=ALU.mult)
            for g, (who, stage) in enumerate(((1, 0), (0, 0), (0, 1), (0, 2))):
                i = dve.scalar_tensor_tensor(out=gain2[:, 5 + g, :], in0=mod[:, (3 * stage + 2) * KD:(3 * stage + 3) * KD, who],
                                             scalar=1.0 if stage == 1 else 0.5, in1=xcol[:, 0, 16 * stage + 8:16 * stage + 16],
                                             op0=ALU.mult, op1=ALU.mult)
            for h in range(2):
                q = 64 * h
                i = dve.tensor_copy(dsk[q:q + 64, :], skip_all[q:q + 64, :].rearrange("p (q h) -> p h q", h=2)[:, h])
            i.then_inc(t_gn.sem, 1)
            dve.wait_ge(t_gn.sem, 1)

        gain = lambda g: (lambda k: gain2[:, g, k:k + 1])
        shift = lambda who, stage: (lambda k: mod[:, 3 * stage * KD + k, who:who + 1])

        def chunk_reads(js):
            counts, reads = {p_ea: 0, p_ed: 0}, []
            for j in js:
                s_ = p_ed if 4 <= j < 11 else p_ea
                counts[s_] += 1
                reads.append((s_, counts[s_]))
            return reads, counts[p_ea], counts[p_ed]

        CTX_JS, X_JS = (6, 7, 8, 9, 10, 11), tuple(range(12))
        _, CTX_NA, CTX_ND = chunk_reads(CTX_JS)
        _, X_NA, X_ND = chunk_reads(X_JS)

        def proj_load(sp, n0, js):
            for idx, j in enumerate(js):
                load_cols(sp, n0.at(idx), a["w_in_2"][0], 256 * j if j < 11 else MIX2_COLS - P, 256 if j < 11 else P)

        def proj_width(js, idx):
            return KD * P if idx < len(js) and js[idx] == 11 else CHUNK

        def proj_pe(pe, n0, js, base_a, base_d, pre):
            reads = chunk_reads(js)[0]
            for idx, j in enumerate(js):
                if idx >= RING:
                    sem_, cnt = reads[idx - RING]
                    pe.wait_ge(sem_, cnt + (base_a if sem_ is p_ea else base_d))
                n = n0.at(idx)
                cols_pe(pe, n, lin[:, n.slot, :], 2 if j < 11 else 1,
                        (lambda k: pe.wait_ge(e_h.sem, e_h.after(pre, k + 1))) if idx == 0 else None,
                        256 if j < 11 else P)

        def proj_act(act, n0, js, base_d, cv_, first, dt_):
            conv_js = [j for j in js if 4 <= j < 11]

            def silu(q):
                act.wait_ge(p_ed, base_d + q + 1)
                blk = 2 * (conv_js[q] - 4) - first
                nc.scalar.activation(cv_[:, blk:blk + 2, :], cv_[:, blk:blk + 2, :], ACT.Silu).then_inc(p_si, 1)
            q = 0
            for idx, j in enumerate(js):
                split_high(act, n0.at(idx + 2), proj_width(js, idx + 2))
                act.wait_ge(s_used, n0.count(idx + 1))
                ps = lin[:, n0.at(idx).slot, :].rearrange("p (b t) -> p b t", b=2)
                if 4 <= j < 11:
                    for b in range(2):
                        blk = 2 * (j - 4) + b
                        i = nc.scalar.activation(cv_[:, blk - first, :], ps[:, b, :], ACT.Identity,
                                                 bias=xcol[:, 1, V_CB + blk:V_CB + blk + 1],
                                                 scale=xcol[:, 1, CONV_BLOCKS + blk:CONV_BLOCKS + blk + 1])
                    i.then_inc(p_c0, 1)
                    if q:
                        silu(q - 1)
                    q += 1
                elif j == 11:
                    nc.scalar.activation(dt_[:], ps[:, 0, :], ACT.Copy).then_inc(p_ea, 1)
                elif j == 0:
                    nc.scalar.activation(uf[:], ps, ACT.Copy).then_inc(p_ea, 1)
                else:
                    nc.scalar.activation(zs[:, 2 * j - 2:2 * j, :], ps, ACT.Silu).then_inc(p_ea, 1)
            silu(q - 1)

        def proj_dve(dve, st, n0, js, base_d, cv_, first):
            q = 0
            for idx, j in enumerate(js):
                split_low(dve, n0.at(idx + 2), proj_width(js, idx + 2))
                if not 4 <= j < 11:
                    continue
                q += 1
                dve.wait_ge(p_c0, base_d + q)
                ps = lin[:, n0.at(idx).slot, :].rearrange("p (b t) -> p b t", b=2)
                for tap in (0, 2):
                    for b in range(2):
                        blk = 2 * (j - 4) + b
                        w = xcol[:, 1, tap * CONV_BLOCKS + blk:tap * CONV_BLOCKS + blk + 1]
                        o, i_ = (slice(1, T), slice(0, T - 1)) if tap == 0 else (slice(0, T - 1), slice(1, T))
                        i = dve.scalar_tensor_tensor(out=cv_[:, blk - first, o], in0=ps[:, b, i_], scalar=w,
                                                     in1=cv_[:, blk - first, o], op0=ALU.mult, op1=ALU.add)
                    if tap == 0:
                        st(i)
                i.then_inc(p_ed, 1)

        def proj_pool(pool, n0, js):
            for idx in range(len(js)):
                split_low(pool, n0.at(idx + 2), proj_width(js, idx + 2))

        X_, M_, E_, Z_, Q_, DT_, DA_, CS_ = range(8)

        def steps_turned_pe(pe, c, dt_, copied):
            pe.wait_ge(p_ea, copied)
            for t in range(2):
                i = pe.transpose(misc[:, t * P:(t + 1) * P], dt_[:, t * P:(t + 1) * P], K["ident"])
            i.then_inc(d_tr.sem, 1)

        def steps_pe(pe, c):
            pe.wait_ge(d_dt.sem, d_dt.after(c))
            for t in range(2):
                for d in range(2):
                    own = (("col_lt", "col_gt"), ("col_ge", "col_le"))[c][d]
                    earlier = (c == 1) == (d == 0)
                    other = 1 - t if (t == 1) == earlier else None
                    dst = misc[:, T + 24 * t + 12 * d:T + 24 * t + 12 * d + 12]
                    i = mm(dst, K[own], small[:, DA_, t, 12 * d:12 * d + 12], start=True, stop=other is None)
                    if other is not None:
                        i = mm(dst, K["ones"], small[:, DA_, other, 12 * d:12 * d + 12], start=False, stop=True)
            i.then_inc(d_cs.sem, 1)

        def steps_act(act, c):
            if c == 0:
                nc.scalar.activation(drow[:, 2, :], drow[:, 1, :], ACT.Exp).then_inc(d_a.sem, 1)
            act.wait_ge(d_x.sem, d_x.after(c))
            nc.scalar.activation(small[:, E_, :, :], small[:, E_, :, :], ACT.Exp, scale=-1.0).then_inc(d_e.sem, 1)

        def steps_dve(dve, st, c, between=lambda: None):
            v = lambda j: small[:, j, :, :]
            dve.wait_ge(d_tr.sem, d_tr.after(c))
            ps = misc[:, 0:2 * P].rearrange("p (t c) -> p t c", t=2)[:, :, 104:128]
            st(dve.tensor_tensor(v(X_), ps, drow[:, 0:1, :].broadcast_to([P, 2, 24]), ALU.add))
            dve.tensor_scalar(v(M_), v(X_), 0.0, None, ALU.max)
            st(dve.tensor_scalar(v(Z_), v(X_), -1.0, None, ALU.mult))
            dve.tensor_tensor(v(E_), v(X_), v(Z_), ALU.max).then_inc(d_x.sem, 1)
            dve.wait_ge(d_e.sem, d_e.after(c))
            st(dve.tensor_scalar(v(Z_), v(E_), 2.0, None, ALU.add))
            st(dve.reciprocal(v(Q_), v(Z_)))
            st(dve.tensor_tensor(v(Z_), v(Q_), v(E_), ALU.mult))
            st(dve.tensor_tensor(v(Q_), v(Z_), v(Z_), ALU.mult))
            st(dve.tensor_scalar(v(E_), v(Q_), 1.0 / 17, None, ALU.mult))
            for k in range(7, 0, -1):
                st(dve.scalar_tensor_tensor(out=v(E_), in0=v(E_), scalar=1.0 / (2 * k + 1), in1=v(Q_), op0=ALU.add, op1=ALU.mult))
            st(dve.scalar_tensor_tensor(out=v(E_), in0=v(E_), scalar=1.0, in1=v(Z_), op0=ALU.add, op1=ALU.mult))
            st(dve.scalar_tensor_tensor(out=v(DT_), in0=v(E_), scalar=2.0, in1=v(M_), op0=ALU.mult, op1=ALU.add))
            dve.wait_ge(d_a.sem, 1)
            dve.scalar_tensor_tensor(out=v(DA_), in0=v(DT_), scalar=-1.0, in1=drow[:, 2:3, :].broadcast_to([P, 2, 24]),
                                     op0=ALU.mult, op1=ALU.mult).then_inc(d_dt.sem, 1)
            between()
            dve.wait_ge(d_cs.sem, d_cs.after(c))
            dve.tensor_copy(v(CS_), misc[:, T:T + 48].rearrange("p (t c) -> p t c", t=2)).then_inc(d_cc.sem, 1)
            dve.wait_ge(d_cc.sem, d_cc.after(c))

        def x_turned(q0, q1):
            src = acc[:, 2 + q0 // 4] if q0 < 8 else lin[:, 0]
            return src[:, (q0 % 4) * P:(q0 % 4 + q1 - q0) * P]

        def ctx_turned_pe(pe):
            pe.wait_ge(p_si, CTX_ND)
            for t in range(2):
                for b in range(4):
                    i = pe.transpose(acc[:, t, b * P:(b + 1) * P], ctx_cv[:, 6 + b, t * P:(t + 1) * P], K["ident"])
            i.then_inc(c_bt.sem, 1)
            for t in range(2):
                for b in range(6):
                    q = 6 * t + b
                    i = pe.transpose(x_turned(q, q + 1), ctx_cv[:, b, t * P:(t + 1) * P], K["ident"])
            i.then_inc(c_xt.sem, 1)

        def ctx_state_pe(pe):
            pe.wait_ge(c_bc.sem, 1)
            pe.wait_ge(c_xw.sem, 1)
            for g in range(GROUPS):
                for d in range(2):
                    for t in range(2):
                        i = mm(acc[:, g, GW * d:GW * d + GW], btok[:, t, g * P:(g + 1) * P], xw[:, t, d, g * GW:(g + 1) * GW],
                               start=(t == 0), stop=(t == 1))
            i.then_inc(c_h.sem, 1)

        def ctx_parts_act(act):
            act.wait_ge(d_cc.sem, 1)
            nc.scalar.activation(small[:, CS_, :, :], small[:, CS_, :, :], ACT.Exp).then_inc(c_w.sem, 1)
            act.wait_ge(c_bt.sem, 1)
            nc.scalar.activation(btok[:], acc[:, 0:2, :], ACT.Copy).then_inc(c_bc.sem, 1)

        def ctx_state_act(act):
            act.wait_ge(c_h.sem, 1)
            nc.scalar.activation(h0, acc[:, :, 0:2 * GW].rearrange("p g (d c) -> p g d c", d=2), ACT.Copy).then_inc(c_hc.sem, 1)

        def ctx_state_dve(dve, st):
            dve.wait_ge(c_w.sem, 1)
            st(dve.tensor_tensor(small[:, Q_, :, :], small[:, CS_, :, :], small[:, DT_, :, :], ALU.mult))
            dve.wait_ge(c_xt.sem, 1)
            for t in range(2):
                for d in range(2):
                    w = small[:, Q_, t, 12 * d:12 * d + 12].unsqueeze(2)
                    q0 = 6 * t
                    while q0 < 6 * t + 6:
                        q1 = min(6 * t + 6, (q0 // 4 + 1) * 4)
                        ha, hb = 2 * (q0 - 6 * t), 2 * (q1 - 6 * t)
                        i = dve.tensor_tensor(xw[:, t, d, ha * 64:hb * 64].rearrange("p (h c) -> p h c", c=64),
                                              x_turned(q0, q1).rearrange("p (h c) -> p h c", c=64),
                                              w[:, ha:hb, :].broadcast_to([P, hb - ha, 64]), ALU.mult)
                        q0 = q1
            i.then_inc(c_xw.sem, 1)

        def fourier_pe(pe):
            pe.wait_ge(p_ea, CTX_NA + 1)
            for t in range(2):
                for b in range(2):
                    i = mm(acc[:, t, b * T:(b + 1) * T], uf[:, b, t * P:(t + 1) * P], K2["dft_head"])
            i.then_inc(f_p.sem, 1)
            pe.wait_ge(f_pc.sem, 1)
            for b in range(2):
                for t in range(2):
                    for part, name in enumerate(("dft_cos", "dft_sin")):
                        i = mm(acc[:, 2, b * T:(b + 1) * T], pcs[:, t, b, part * P:(part + 1) * P],
                               K2[name].rearrange("p (t l) -> p t l", t=2)[:, t, :],
                               start=(t == 0 and part == 0), stop=(t == 1 and part == 1))
            i.then_inc(f_f.sem, 1)
            pe.wait_ge(f_fc.sem, 1)
            for b in range(2):
                i = mm(acc[:, 3, b * T:(b + 1) * T], fw[:, b, :], uf[:, b, :])
            i.then_inc(f_y.sem, 1)

        def fourier_act(act):
            act.wait_ge(f_p.sem, 1)
            nc.scalar.activation(pcs, acc[:, 0:2, :].rearrange("p t (b c) -> p t b c", b=2), ACT.Copy).then_inc(f_pc.sem, 1)
            act.wait_ge(f_f.sem, 1)
            nc.scalar.activation(uf[:], acc[:, 2, :].rearrange("p (b t) -> p b t", b=2), ACT.Copy).then_inc(f_fc.sem, 1)
            act.wait_ge(f_y.sem, 1)
            nc.scalar.activation(work[:, 0:2, :], acc[:, 3, :].rearrange("p (b t) -> p b t", b=2), ACT.Copy).then_inc(f_yc.sem, 1)

        def head_rows(h):
            return slice(64 * (h % 2), 64 * (h % 2) + 64)

        free_hi = hhi[:].rearrange("p k t -> p (k t)")[0:SSD_HEADS]
        free_lo = hlo[:].rearrange("p k t -> p (k t)")[0:SSD_HEADS]
        pick_head = free_hi[:, 0:SSD_HEADS * P]
        pick_pair = free_lo[:, 0:6 * P]
        csr_hi = free_lo[:, 6 * P:6 * P + 2 * T]
        csr_lo = free_lo[:, 6 * P + 2 * T:6 * P + 4 * T]

        def mixer2_pe(pe, n0):
            steps_turned_pe(pe, 1, dtT, CTX_NA + X_NA)
            fourier_pe(pe)
            pe.wait_ge(p_si, CTX_ND + X_ND)
            pe.wait_ge(f_yc.sem, 1)
            for g in range(GROUPS):
                for b in range(2):
                    i = mm(acc[:, g, b * T:(b + 1) * T], cv[:, 10 + g, b * P:(b + 1) * P], cv[:, g, :])
            i.then_inc(x_cb.sem, 1)
            for t in range(2):
                for b in range(6):
                    q = 6 * t + b
                    i = pe.transpose(lin[:, q // 4, (q % 4) * P:(q % 4 + 1) * P], cv[:, 4 + b, t * P:(t + 1) * P], K["ident"])
            i.then_inc(x_xt.sem, 1)
            steps_pe(pe, 1)
            pe.wait_ge(d_cc.sem, d_cc.after(1))
            for d, own in enumerate(("col_ge", "col_le")):
                for l in range(2):
                    dst = misc[0:12, (2 * d + l) * P:(2 * d + l + 1) * P]
                    other = 1 - l if (l == 1) == (d == 0) else None
                    i = mm(dst, small[:, DA_, l, 12 * d:12 * d + 12], K[own], start=True, stop=other is None)
                    if other is not None:
                        i = mm(dst, small[:, DA_, other, 12 * d:12 * d + 12], K["ones"], start=False, stop=True)
            i.then_inc(x_csr.sem, 1)
            pe.wait_ge(x_csl.sem, 1)
            pe.wait_ge(x_cbc.sem, 1)
            pe.wait_ge(x_xc.sem, 1)

            def spread_rows(dst, pick):
                mm(dst, pick, csr_hi, start=True, stop=False)
                return mm(dst, pick, csr_lo, start=False, stop=True)

            def spread(h):
                if h >= 2:
                    pe.wait_ge(x_d.sem, h - 1)
                spread_rows(acc[:, h % 2, :], pick_head[:, h * P:(h + 1) * P]).then_inc(x_cs.sem, 1)
            spread(0)
            spread(1)
            for h in range(SSD_HEADS):
                p = h // 2
                if h + 2 < SSD_HEADS:
                    spread(h + 2)
                if h % 2 == 0:
                    if p:
                        pe.wait_ge(x_t.sem, p)
                    if p >= RING:
                        pe.wait_ge(x_yp.sem, p - 2)
                    spread_rows(acc[:, 2, :], pick_pair[:, p * P:(p + 1) * P]).then_inc(x_ps.sem, 1)
                    for hh in (h, h + 1):
                        for d in range(2):
                            i = mm(acc[head_rows(hh), 3, d * T:(d + 1) * T], h0[:, hh // 3, d, 64 * (hh % 3):64 * (hh % 3) + 64],
                                   cv[:, hh // 3, :])
                    i.then_inc(x_yo.sem, 1)
                pe.wait_ge(x_mm.sem, h + 1)
                for t in range(2):
                    i = mm(lin[head_rows(h), p % RING, 0:T], xtok[:, t, 64 * h:64 * h + 64], mt[:, h % 2, t, :], start=(t == 0), stop=(t == 1))
                i.then_inc(x_y.sem, 1)
            for p in range(6):
                pe.wait_ge(x_sq.sem, p + 1)
                i = mm(misc[0:4, 0:T], K2["member"].rearrange("p (b g) -> p b g", g=4)[:, p, :], zs[:, p, :], start=(p == 0), stop=(p == 5))
            i.then_inc(x_gs.sem, 1)
            pe.wait_ge(x_gi.sem, 1)
            for p in range(6):
                i = mm(acc[:, p // 2, (p % 2) * T:(p % 2) * T + T], K2["spread"].rearrange("p (b c) -> p b c", b=6)[0:4, p, :], grs[:])
            i.then_inc(x_sp.sem, 1)
            pe.wait_ge(x_cat.sem, 6)
            for p in range(OUT_CHUNKS):
                pe.wait_ge(x_cl.sem, p + 1)
                rows_pe(pe, n0.at(p), lambda h: hhi[:, 2 * p + h, :], lambda h: hlo[:, 2 * p + h, :], p == 0,
                        6 if p == OUT_CHUNKS - 1 else None, lambda h: None)

        def mixer2_act(act, n0):
            steps_act(act, 1)
            nc.scalar.activation(pick_head, K2["pick_head"][0:SSD_HEADS, :], ACT.Copy)
            nc.scalar.activation(pick_pair, K2["pick_pair"][0:SSD_HEADS, :], ACT.Copy)
            fourier_act(act)
            split_high(act, n0.at(2))
            act.wait_ge(x_cb.sem, 1)
            nc.scalar.activation(cb[:], acc[:].rearrange("p g (i t) -> p g i t", i=2), ACT.Copy).then_inc(x_cbc.sem, 1)
            act.wait_ge(x_csr.sem, 1)
            nc.scalar.activation(csr[:], misc[0:12, :].rearrange("p (d t) -> p d t", d=2), ACT.Copy)
            nc.scalar.activation(csr_hi, misc[0:12, :], ACT.Copy).then_inc(x_csc.sem, 1)
            for h in range(SSD_HEADS):
                act.wait_ge(x_d.sem, h + 1)
                nc.scalar.activation(ex[:, h % 2, :], ex[:, h % 2, :], ACT.Exp).then_inc(x_e.sem, 1)
                if h % 2 == 0:
                    act.wait_ge(x_ps.sem, h // 2 + 1)
                    if h:
                        act.wait_ge(x_t.sem, h // 2)
                    nc.scalar.activation(ep[:], acc[:, 2, :].rearrange("p (d t) -> p d t", d=2), ACT.Exp).then_inc(x_ep.sem, 1)
            for p in range(6):
                act.wait_ge(x_yp.sem, p + 1)
                nc.scalar.activation(zs[:, p, :], work[:, 2 + p, :], ACT.Square).then_inc(x_sq.sem, 1)
            act.wait_ge(x_gs.sem, 1)
            nc.scalar.activation(grt[:], misc[0:4, 0:T], ACT.Sqrt, bias=K["eps6"][0:4, :], scale=1.0 / GW).then_inc(x_gr.sem, 1)
            for p in range(OUT_CHUNKS):
                if p:
                    act.wait_ge(x_cat.sem, 2 * p)
                else:
                    act.wait_ge(f_yc.sem, 1)
                nc.scalar.activation(hhi[:, 2 * p:2 * p + 2, :], work[:, 2 * p:2 * p + 2, :], ACT.Copy).then_inc(x_ch.sem, 1)
            for j in (3, 4, 5):
                split_high(act, n0.at(j))

        def mixer2_dve(dve, st, n0):
            steps_dve(dve, st, 1, lambda: split_low(dve, n0.at(2)))
            dve.wait_ge(x_xt.sem, 1)
            dve.tensor_copy(xtok[:].rearrange("p t c -> p (t c)"), lin[:].rearrange("p b c -> p (b c)")).then_inc(x_xc.sem, 1)
            dve.wait_ge(x_csc.sem, 1)
            dve.tensor_tensor(csr_lo, csr[:].rearrange("p d t -> p (d t)"), csr_hi.bitcast(F32), ALU.subtract).then_inc(x_csl.sem, 1)
            bars = K2["bars"]

            def differences(h):
                dve.wait_ge(x_cs.sem, h + 1)
                if h >= 2:
                    dve.wait_ge(x_m.sem, h - 1)
                cs = acc[:, h % 2, :].rearrange("p (d t) -> p d t", d=2)
                e = ex[:, h % 2, :]
                for dst, t, d, l0, l1, b0 in ((e[:, 0:T], 0, 0, 0, T, 0), (e[:, T:T + P], 0, 1, 0, P, 2 * P),
                                              (e[:, T + P:2 * T], 1, 0, P, T, 0), (e[:, 2 * T:3 * T], 1, 1, 0, T, P)):
                    i = dve.scalar_tensor_tensor(out=dst, in0=cs[:, d, l0:l1], scalar=small[:, CS_, t, 12 * d + h:12 * d + h + 1],
                                                 in1=bars[:, b0:b0 + l1 - l0], op0=ALU.subtract, op1=ALU.min)
                i.then_inc(x_d.sem, 1)

            def pair_output(p):
                dve.wait_ge(x_y.sem, 2 * p + 2)
                w = work[:, 2 + p, :]
                st(dve.scalar_tensor_tensor(out=w, in0=cv[:, 4 + p, :], scalar=dsk[:, p:p + 1], in1=lin[:, p % RING, 0:T],
                                            op0=ALU.mult, op1=ALU.add))
                st(dve.tensor_tensor(w, w, yo[:, 0, :], ALU.add))
                st(dve.tensor_tensor(w, w, yo[:, 1, :], ALU.add))
                dve.tensor_tensor(w, w, zs[:, p, :], ALU.mult).then_inc(x_yp.sem, 1)

            differences(0)
            for h in range(SSD_HEADS):
                p = h // 2
                if h + 1 < SSD_HEADS:
                    differences(h + 1)
                dve.wait_ge(x_e.sem, h + 1)
                if h >= 2:
                    dve.wait_ge(x_y.sem, h - 1)
                e = ex[:, h % 2, :]
                m = mt[:, h % 2]
                dt = lambda t, d: small[:, DT_, t, 12 * d + h:12 * d + h + 1]
                dve.tensor_scalar(m[:, 0, :], e[:, 0:T], dt(0, 0), None, ALU.mult)
                st(dve.tensor_scalar(m[:, 1, :], e[:, 2 * T:3 * T], dt(1, 1), None, ALU.mult))
                dve.scalar_tensor_tensor(out=m[:, 0, 0:P], in0=e[:, T:T + P], scalar=dt(0, 1), in1=m[:, 0, 0:P], op0=ALU.mult, op1=ALU.add)
                dve.scalar_tensor_tensor(out=m[:, 1, P:T], in0=e[:, T + P:2 * T], scalar=dt(1, 0), in1=m[:, 1, P:T],
                                         op0=ALU.mult, op1=ALU.add).then_inc(x_m.sem, 1)
                if h % 2 == 0:
                    if p:
                        pair_output(p - 1)
                        dve.wait_ge(x_yp.sem, p)
                    dve.wait_ge(x_yo.sem, p + 1)
                    dve.wait_ge(x_ep.sem, p + 1)
                    dve.tensor_tensor(yo[:], acc[:, 3, :].rearrange("p (d t) -> p d t", d=2), ep[:], ALU.mult).then_inc(x_t.sem, 1)
            dve.wait_ge(x_t.sem, SSD_HEADS // 2)
            pair_output(SSD_HEADS // 2 - 1)
            dve.wait_ge(x_gr.sem, 1)
            dve.reciprocal(grs[:], grt[:]).then_inc(x_gi.sem, 1)
            dve.wait_ge(x_sp.sem, 1)
            for p in range(6):
                dve.scalar_tensor_tensor(out=work[:, 2 + p, :], in0=work[:, 2 + p, :], scalar=xcol[:, 0, V_SSDN + p:V_SSDN + p + 1],
                                         in1=acc[:, p // 2, (p % 2) * T:(p % 2) * T + T], op0=ALU.mult, op1=ALU.mult).then_inc(x_cat.sem, 1)
            for p in range(OUT_CHUNKS):
                dve.wait_ge(x_ch.sem, p + 1)
                dve.tensor_tensor(hlo[:, 2 * p:2 * p + 2, :], work[:, 2 * p:2 * p + 2, :],
                                  hhi[:, 2 * p:2 * p + 2, :].bitcast(F32), ALU.subtract).then_inc(x_cl.sem, 1)
            for j in (3, 4, 5):
                split_low(dve, n0.at(j))

        def mixer2_pool(pool, n0):
            split_low(pool, n0.at(2))
            for h in range(SSD_HEADS):
                pool.wait_ge(x_m.sem, h + 1)
                pool.tensor_tensor(mt[:, h % 2], mt[:, h % 2], cb[:, h // 3], ALU.mult).then_inc(x_mm.sem, 1)
            for j in (3, 4, 5):
                split_low(pool, n0.at(j))

        AFTER1 = LAYERS * LAYER_CHUNKS
        FFN_CHUNKS = UP_CHUNKS + DOWN_CHUNKS
        N_CTX = Place(AFTER1)
        N_CTXP = Place(AFTER1 + FFN_CHUNKS)
        N_FFN1 = Place(AFTER1 + FFN_CHUNKS + CTX_PROJ_CHUNKS)
        N_PROJ = N_FFN1.at(FFN_CHUNKS)
        N_OUT2 = N_PROJ.at(MIX2_CHUNKS)
        N_FFN2 = N_OUT2.at(OUT_CHUNKS)
        out_bank = lambda half, t: (lin[:, 0, :], lin[:, 1, :], lin[:, 2, :], misc[:])[2 * half + t]
        END = N_FFN2.count(FFN_CHUNKS)

        @block.sync
        def _(sp):
            sp.dma_start(tab[:], a["tables"]).then_inc(s_tab, 16)
            sp.dma_start(outt, a["x"].rearrange("o (t p) d -> p (o t) d", p=P)).then_inc(s_x, 16)
            sp.wait_ge(s_fpar, N_FPAR)
            for L in range(LAYERS):
                n0 = base(L)
                w = one(a["w_in"], L)
                for j, (c0, width) in enumerate(((512, 256), (768, 256), (1024, 140), (0, 256), (256, 256),
                                                 (SGU_COL, 256), (SGU_COL + 256, 256), (POOL_COL, 256))):
                    load_cols(sp, n0.at(j), w, c0, width)
                    if not L and j == RING - 1:
                        sp.wait_ge(s_zero, 2)
                        load_gate_weights(sp, 0)
                        load_mixer_weights(sp, 0)
                for p in range(OUT_CHUNKS):
                    load_rows(sp, n0.at(MIX1_CHUNKS + p), one(a["w_out"], L), 2 * P * OUT1_ORDER[p])
                w = one(a["ffn_up"], L)

                def modulation(down, j, turn):
                    if not down and isinstance(turn, int) and turn == 0:
                        if j < 2:
                            return
                        sp.wait_ge(s_used, n0.count(MIX1_CHUNKS + OUT_CHUNKS))
                        sp.wait_ge(m_cal.sem, m_cal.after(L))
                        sp.wait_ge(m_vw.sem, m_vw.after(L))
                        ada_load(sp, L, down, 0, turn)
                        ada_load(sp, L, down, 1, turn)
                    ada_load(sp, L, down, j, turn)
                load_ffn(sp, n0.at(MIX1_CHUNKS + OUT_CHUNKS), w[:, 0:FF], w[:, FF:2 * FF], one(a["ffn_down"], L), modulation)
            ffn = lambda n, i: load_ffn(sp, n, a[f"ffn{i}_w_gate_2"][0], a[f"ffn{i}_w_up_2"][0], a[f"ffn{i}_w_down_2"][0])
            ffn(N_CTX, 1)
            proj_load(sp, N_CTXP, CTX_JS)
            ffn(N_FFN1, 1)
            proj_load(sp, N_PROJ, X_JS)
            for p in range(OUT_CHUNKS):
                load_rows(sp, N_OUT2.at(p), a["w_out_2"][0], 2 * P * p)
            ffn(N_FFN2, 2)
            for half in range(2):
                sp.wait_ge(s_outr, half + 1)
                sp.dma_start(out.rearrange("o (t p) d -> p (o t) d", p=P)[:, :, 512 * half:512 * half + 512],
                             outt[:, :, 512 * half:512 * half + 512]).then_inc(s_out, 16)
            sp.wait_ge(s_out, 32)

        @block.tensor
        def _(pe):
            st = Steps(pe, s_st["pe"])
            pe.wait_ge(s_tab, 16)
            pe.wait_ge(s_crow, 32)
            pe.transpose(misc[:, 0:16], crow[:], K["ident"][0:16, 0:16]).then_inc(e_ct, 1)
            pe.wait_ge(s_x, 16)
            turn_in_pe(pe, 0, lambda t: outt[:, t, :])
            pe.wait_ge(e_cs, 1)
            for L in range(LAYERS):
                n0 = base(L)
                mixer1_pe(pe, st, L, n0)
                pre_pe(pe, 2 * L + 1)
                ffn_pe(pe, L, n0.at(MIX1_CHUNKS + OUT_CHUNKS), 2 * L + 1, lambda down, j, turn: ada_pe(pe, L, down, j, turn),
                       lambda: pe.wait_ge(e_am.sem, e_am.after(L)))
            second_start_pe(pe)
            pe.wait_ge(s_ctx, 32)
            
            turn_in_pe(pe, 1, lambda t: ada[t][:].rearrange("p k c -> p (k c)"))
            pre_pe(pe, 4)
            ffn_pe(pe, 2, N_CTX, 4)
            pre_pe(pe, 5)
            proj_pe(pe, N_CTXP, CTX_JS, 0, 0, 5)
            steps_turned_pe(pe, 0, ctx_dt, CTX_NA)
            ctx_turned_pe(pe)
            steps_pe(pe, 0)
            pe.wait_ge(d_cc.sem, 1)
            pre_pe(pe, 6)
            ctx_state_pe(pe)
            ffn_pe(pe, 3, N_FFN1, 5, lambda down, j, turn:
                   pe.wait_ge(c_hc.sem, 1) if down and j == 0 and isinstance(turn, int) and turn == 0 else None)
            pre_pe(pe, 7)
            proj_pe(pe, N_PROJ, X_JS, CTX_NA, CTX_ND, 7)
            mixer2_pe(pe, N_OUT2)
            pre_pe(pe, 8)
            ffn_pe(pe, 4, N_FFN2, 7)
            for half in range(2):
                for k in range(4 * half, 4 * half + 4):
                    x_updated(pe, 7, k)
                    for t in range(2):
                        i = pe.transpose(out_bank(half, t)[:, (k % 4) * P:(k % 4 + 1) * P], xT[:, k, t * P:(t + 1) * P], K["ident"])
                i.then_inc(s_fin, 1)

        @block.scalar
        def _(act):
            st = Steps(act, s_st["act"])
            queue = nc.scalar
            queue.dma_start(crow[0:8, :], a["c_2"].rearrange("o (k p) -> (o k) p", p=P)).then_inc(s_crow, 16)
            queue.dma_start(crow[8:16, :], a["c_ctx_2"].rearrange("(k p) -> k p", p=P)).then_inc(s_crow, 16)
            load_mixer_vectors(queue, 0)
            load_ffn_params(queue, 0)
            queue.dma_start(tab1[:], a["tables_1"]).then_inc(s_tab1, 16)
            act.wait_ge(s_tab, 16)
            act.wait_ge(e_ct, 1)
            nc.scalar.activation(csil[:].rearrange("p v k -> p (v k)"), misc[:, 0:16], ACT.Silu).then_inc(e_cs, 1)
            for L in range(LAYERS):
                n0 = base(L)

                def vectors():
                    act.wait_ge(e_vt.sem, e_vt.after(L))
                    nc.scalar.activation(vcol[:], lin[:, 0, 0:R_ROWS], ACT.Copy)
                    nc.scalar.activation(pecol[:], lin[:, 0, 128:160], ACT.Copy)
                    nc.scalar.activation(fcol[:], lin[:, 0, 256:256 + 176].rearrange("p (j r) -> p j r", j=2), ACT.Copy)\
                        .then_inc(e_vc.sem, 1)
                    if not L:
                        split_high(act, Place(0))
                pre_act(act, 2 * L, xT, after_post(2 * L - 1) if L else
                        (lambda eng, k: eng.wait_ge(e_xc.sem, k // 2 + 1)), between=vectors)
                if not L:
                    split_high(act, Place(1))
                mixer1_act(act, st, L, n0)
                post_act(act, 2 * L, n0.count(MIX1_CHUNKS + OUT_CHUNKS))
                pre_act(act, 2 * L + 1, xT, after_post(2 * L))
                n1 = n0.at(MIX1_CHUNKS + OUT_CHUNKS)
                ffn1_act(act, L, n1)

                def parameters(j):
                    if j == 0:
                        act.wait_ge(s_used, n0.count(MIX1_CHUNKS + OUT_CHUNKS))
                        act.wait_ge(m_cal.sem, m_cal.after(L))
                        act.wait_ge(m_vw.sem, m_vw.after(L))
                    if L + 1 < LAYERS:
                        if j == 0:
                            load_mixer_vectors(queue, L + 1)
                        elif j == 1:
                            load_ffn_params(queue, L + 1)
                            load_gate_weights(queue, L + 1)
                        else:
                            load_mixer_weights(queue, L + 1)
                    else:
                        if j == 0:
                            act.wait_ge(s_zero, 3)
                        load_second_params(queue, j)
                down_split(act, n1, split_high, 2, parameters)
                if L + 1 == LAYERS:
                    act.wait_ge(e_ad.sem, ADA_BLOCKS)
                    for t in range(2):
                        queue.dma_start(ada[t][:].rearrange("p k c -> p (k c)"), a["ctx_2"][0, t * P:(t + 1) * P, :]).then_inc(s_ctx, 16)
                post_act(act, 2 * L + 1, n0.count(LAYER_CHUNKS))

            def ctx_turned(eng, k):
                x_updated(eng, 2 * LAYERS - 1, k)
                eng.wait_ge(e_xc.sem, 4 + k // 2 + 1)
            pre_act(act, 4, cT, ctx_turned, shift(1, 0), between=lambda: act.wait_ge(t_gn.sem, 1))
            ffn2_act(act, 2, N_CTX)
            down_split(act, N_CTX, split_high, 2)
            post_act(act, 4, N_CTXP.count())
            pre_act(act, 5, cT, after_post(4), shift(1, 1))
            proj_act(act, N_CTXP, CTX_JS, 0, ctx_cv, 4, ctx_dt)
            steps_act(act, 0)
            pre_act(act, 6, xT, lambda eng, k: None, shift(0, 0), between=lambda: ctx_parts_act(act))
            ctx_state_act(act)
            ffn2_act(act, 3, N_FFN1)
            down_split(act, N_FFN1, split_high, 2)
            post_act(act, 5, N_PROJ.count())
            pre_act(act, 7, xT, after_post(5), shift(0, 1))
            proj_act(act, N_PROJ, X_JS, CTX_ND, cv, 0, dtT)
            mixer2_act(act, N_OUT2)
            post_act(act, 6, N_FFN2.count())
            pre_act(act, 8, xT, after_post(6), shift(0, 2))
            ffn2_act(act, 4, N_FFN2)
            down_split(act, N_FFN2, split_high, 0)
            post_act(act, 7, END)
            for half in range(2):
                act.wait_ge(s_fin, half + 1)
                for t in range(2):
                    i = nc.scalar.activation(outt[:, t, 512 * half:512 * half + 512], out_bank(half, t), ACT.Copy)
                i.then_inc(s_outr, 1)

        @block.vector
        def _(dve):
            st = Steps(dve, s_st["dve"])
            dve = nc.vector
            turn_in_dve(dve, 0, xT)
            split_low(dve, Place(0))
            col = lambda r: (lambda k: vcol[:, r + k:r + k + 1])
            for L in range(LAYERS):
                n0 = base(L)
                dve.wait_ge(e_vc.sem, e_vc.after(L))
                pre_dve(dve, st, 2 * L, xT, col(R_MIX_PRE))
                if not L:
                    split_low(dve, Place(1))
                mixer1_dve(dve, st, L, n0)
                post_dve(dve, st, 2 * L, col(R_MIX_POST), xT)
                pre_dve(dve, st, 2 * L + 1, xT, col(R_FFN_PRE))
                n1 = n0.at(MIX1_CHUNKS + OUT_CHUNKS)
                ffn1_dve(dve, st, L, n1)
                down_split(dve, n1, split_low, 1)
                dve.wait_ge(e_ad.sem, e_ad.after(L))
                dve.tensor_copy(mod[:, L * ADA_LAYER:(L + 1) * ADA_LAYER, :],
                                misc[:, T:T + 2 * ADA_LAYER].rearrange("p (b v) -> p b v", v=2)).then_inc(e_am.sem, 1)
                split_low(dve, n1.at(UP_CHUNKS + DOWN_CHUNKS + 1))
                post_dve(dve, st, 2 * L + 1, col(R_FFN_POST), xT)
            turn_in_dve(dve, 1, cT)
            second_start_dve(dve, st)
            pre_dve(dve, st, 4, cT, gain(0), shift(1, 0))
            ffn2_dve(dve, 2, N_CTX)
            down_split(dve, N_CTX, split_low, 2)
            post_dve(dve, st, 4, gain(5), cT)
            pre_dve(dve, st, 5, cT, gain(1), shift(1, 1))
            proj_dve(dve, st, N_CTXP, CTX_JS, 0, ctx_cv, 4)
            steps_dve(dve, st, 0)
            ctx_state_dve(dve, st)
            pre_dve(dve, st, 6, xT, gain(2), shift(0, 0))
            ffn2_dve(dve, 3, N_FFN1)
            down_split(dve, N_FFN1, split_low, 2)
            post_dve(dve, st, 5, gain(6), xT)
            pre_dve(dve, st, 7, xT, gain(3), shift(0, 1))
            proj_dve(dve, st, N_PROJ, X_JS, CTX_ND, cv, 0)
            mixer2_dve(dve, st, N_OUT2)
            post_dve(dve, st, 6, gain(7), xT)
            pre_dve(dve, st, 8, xT, gain(4), shift(0, 2))
            ffn2_dve(dve, 4, N_FFN2)
            down_split(dve, N_FFN2, split_low, 0)
            post_dve(dve, st, 7, gain(8), xT)

        @block.gpsimd
        def _(pool):
            st = Steps(pool, s_st["pool"])
            pool = nc.gpsimd
            pool.memset(pw[:], 0.0).then_inc(s_zero, 1)
            pool.memset(glu[:], 0.0)
            pool.memset(psum2[:], 0.0)
            pool.memset(zpad[:], 0.0).then_inc(s_zero, 1)
            split_low(pool, Place(0))
            split_low(pool, Place(1))
            for L in range(LAYERS):
                n0 = base(L)
                mixer1_pool(pool, st, L, n0)
                post_pool(pool, 2 * L, xT)
                n1 = n0.at(MIX1_CHUNKS + OUT_CHUNKS)
                if L + 1 == LAYERS:
                    pool.memset(fw[:], 0.0).then_inc(s_zero, 1)
                ffn1_pool(pool, L, n1)
                down_split(pool, n1, split_low, 2)
                post_pool(pool, 2 * L + 1, xT)
            ffn2_pool(pool, 2, N_CTX)
            down_split(pool, N_CTX, split_low, 2)
            post_pool(pool, 4, cT)
            proj_pool(pool, N_CTXP, CTX_JS)
            ffn2_pool(pool, 3, N_FFN1)
            down_split(pool, N_FFN1, split_low, 2)
            post_pool(pool, 5, xT)
            proj_pool(pool, N_PROJ, X_JS)
            mixer2_pool(pool, N_OUT2)
            post_pool(pool, 6, xT)
            ffn2_pool(pool, 4, N_FFN2)
            down_split(pool, N_FFN2, split_low, 0)
            post_pool(pool, 7, xT)


_INS = (
    "x", "norm_mix_pre", "norm_mix_post", "norm_ffn_pre", "norm_ffn_post", "w_in", "w_out", "conv_dw_w", "conv_dw_b",
    "conv_ln_g", "conv_ln_b", "nsa_pe_k", "nsa_pe_v", "nsa_ck_w1", "nsa_ck_w2", "nsa_cv_w1", "nsa_cv_w2", "sgu_ln_g",
    "sgu_ln_b", "sgu_w", "sgu_b", "pool_w", "pool_scale", "ffn_up", "ffn_conv_w", "ffn_conv_b", "ffn_down",
    "c_2", "ctx_2", "c_ctx_2", "ada_w_2", "ada_b_2", "ffn1_norm_pre_2", "ffn1_norm_post_2", "ffn1_w_gate_2",
    "ffn1_w_up_2", "ffn1_w_down_2", "mix_norm_pre_2", "mix_norm_post_2", "w_in_2", "fourier_w_2", "conv_w_2",
    "conv_b_2", "dt_bias_2", "a_log_2", "d_skip_2", "ssd_norm_2", "w_out_2", "ffn2_norm_pre_2", "ffn2_norm_post_2",
    "ffn2_w_gate_2", "ffn2_w_up_2", "ffn2_w_down_2",
)


def kernel(**inputs):
    import concourse.bacc as bacc
    from concourse.bass_utils import run_bass_kernel_spmd

    nc = bacc.Bacc("TRN2", target_bir_lowering=False, num_devices=1)
    (at, table), (at1, table1), (at2, table2) = tables()
    arrays, args = {}, []
    for name in _INS + ("tables", "tables_1", "tables_2"):
        x = {"tables": table, "tables_1": table1, "tables_2": table2}.get(name)
        if x is None:
            x = np.ascontiguousarray(inputs[name])
        arrays["in_" + name] = x
        args.append(nc.dram_tensor("in_" + name, x.shape, mybir.dt.from_np(x.dtype), kind="ExternalInput").ap())
    out = nc.dram_tensor("out_dram", (1, T, D), F32, kind="ExternalOutput").ap()
    build(nc, _INS + ("tables", "tables_1", "tables_2"), args, out, at, at1, at2)
    result = run_bass_kernel_spmd(nc, [arrays], core_ids=[0])
    return result.results[0]["out_dram"]
```
